# Optimizing a Trainium2 kernel written in Bass

```python
import math
import jax, jax.numpy as jnp
from jax import lax
import numpy as np

D_MODEL = 2048
BATCH = 1
SEQ = 256
DEPTH = 1

HEAD_DIM = 128
A_Q_HEADS = 8
A_KV_HEADS = 2
A_GROUP = A_Q_HEADS // A_KV_HEADS
WINDOW = 128
A_BLOCK = 128
B_HEADS = 8
GRID_W = 64
WIN_H = 8
WIN_W = 16
Q_COL_BLOCK = 16
K_COL_SPAN = Q_COL_BLOCK + WIN_W
D_FF = 5632
CONV_W = 3
ROPE_THETA = 10000.0
EPS = 1e-6
NEG = -1e30

A_Q_DIM = A_Q_HEADS * HEAD_DIM
A_KV_DIM = A_KV_HEADS * HEAD_DIM
B_DIM = B_HEADS * HEAD_DIM
IN_SPLITS = [A_Q_DIM, A_KV_DIM, A_KV_DIM, B_DIM, B_DIM, B_DIM, D_MODEL, D_MODEL]
IN_COLS = sum(IN_SPLITS)


def rmsnorm(x, g):
    xf = x.astype(jnp.float32)
    y = xf * lax.rsqrt(jnp.mean(xf * xf, axis=-1, keepdims=True) + EPS)
    return (y * g.astype(jnp.float32)).astype(x.dtype)

def rope(x, pos):
    half = x.shape[-1] // 2
    inv_freq = ROPE_THETA ** (-jnp.arange(half, dtype=jnp.float32) * (2.0 / x.shape[-1]))
    ang = pos[:, None] * inv_freq[None, :]
    cos = jnp.cos(ang)[None, :, None, :]
    sin = jnp.sin(ang)[None, :, None, :]
    xf = x.astype(jnp.float32)
    x1, x2 = xf[..., :half], xf[..., half:]
    return jnp.concatenate([x1 * cos - x2 * sin, x2 * cos + x1 * sin], axis=-1).astype(x.dtype)

def window_attention(q, k, v, sink):
    b, s_len, _, d = q.shape
    nb = s_len // A_BLOCK
    qb = q.reshape(b, nb, A_BLOCK, A_KV_HEADS, A_GROUP, d)
    pad = ((0, 0), (A_BLOCK, A_BLOCK), (0, 0), (0, 0))
    kp = jnp.pad(k, pad).reshape(b, nb + 2, A_BLOCK, A_KV_HEADS, d)
    vp = jnp.pad(v, pad).reshape(b, nb + 2, A_BLOCK, A_KV_HEADS, d)
    kb = jnp.concatenate([kp[:, 0:nb], kp[:, 1:nb + 1], kp[:, 2:nb + 2]], axis=2)
    vb = jnp.concatenate([vp[:, 0:nb], vp[:, 1:nb + 1], vp[:, 2:nb + 2]], axis=2)
    s = jnp.einsum('bnqhgd,bnkhd->bnhgqk', qb, kb,
                   preferred_element_type=jnp.float32) * (1.0 / math.sqrt(d))
    qpos = np.arange(nb)[:, None] * A_BLOCK + np.arange(A_BLOCK)[None, :]
    kpos = (np.arange(nb)[:, None] - 1) * A_BLOCK + np.arange(3 * A_BLOCK)[None, :]
    valid = ((np.abs(qpos[:, :, None] - kpos[:, None, :]) <= WINDOW)
             & (kpos >= 0)[:, None, :] & (kpos < s_len)[:, None, :])
    s = jnp.where(jnp.asarray(valid)[None, :, None, None], s, NEG)
    sink_b = sink.astype(jnp.float32).reshape(A_KV_HEADS, A_GROUP)[None, None, :, :, None, None]
    m = jnp.maximum(jnp.max(s, axis=-1, keepdims=True), sink_b)
    p = jnp.exp(s - m)
    p = p / (jnp.sum(p, axis=-1, keepdims=True) + jnp.exp(sink_b - m))
    o = jnp.einsum('bnhgqk,bnkhd->bnqhgd', p.astype(v.dtype), vb)
    return o.reshape(b, s_len, A_Q_HEADS * d)

def neighbourhood_attention(q, k, v, rpb):
    b, s_len, h, d = q.shape
    rows = s_len // GRID_W
    kh = min(WIN_H, rows)
    rb = kh
    nrb = -(-rows // rb)
    rows_p = nrb * rb
    kspan = min(rb + kh, rows)
    ncb = GRID_W // Q_COL_BLOCK
    nq = rb * Q_COL_BLOCK
    nk = kspan * K_COL_SPAN

    qg = jnp.pad(q.reshape(b, rows, GRID_W, h, d), ((0, 0), (0, rows_p - rows), (0, 0), (0, 0), (0, 0)))
    qb = qg.reshape(b, nrb, rb, ncb, Q_COL_BLOCK, h, d).transpose(0, 1, 3, 2, 4, 5, 6)
    qb = qb.reshape(b, nrb, ncb, nq, h, d)

    r0 = np.arange(nrb) * rb
    krows = np.clip(r0 - kh // 2, 0, rows - kspan)[:, None] + np.arange(kspan)[None, :]
    c0 = np.arange(ncb) * Q_COL_BLOCK
    kcols = np.clip(c0 - WIN_W // 2, 0, GRID_W - K_COL_SPAN)[:, None] + np.arange(K_COL_SPAN)[None, :]

    kg = k.reshape(b, rows, GRID_W, h, d)
    vg = v.reshape(b, rows, GRID_W, h, d)
    ridx = krows[:, None, :, None]
    cidx = kcols[None, :, None, :]
    kb = kg[:, ridx, cidx].reshape(b, nrb, ncb, nk, h, d)
    vb = vg[:, ridx, cidx].reshape(b, nrb, ncb, nk, h, d)

    shp_q = (nrb, ncb, rb, Q_COL_BLOCK)
    shp_k = (nrb, ncb, kspan, K_COL_SPAN)
    qr = np.broadcast_to((r0[:, None] + np.arange(rb)[None, :])[:, None, :, None], shp_q).reshape(nrb, ncb, nq)
    qc = np.broadcast_to((c0[:, None] + np.arange(Q_COL_BLOCK)[None, :])[None, :, None, :], shp_q).reshape(nrb, ncb, nq)
    kr = np.broadcast_to(krows[:, None, :, None], shp_k).reshape(nrb, ncb, nk)
    kc = np.broadcast_to(kcols[None, :, None, :], shp_k).reshape(nrb, ncb, nk)
    qr, qc = qr[..., :, None], qc[..., :, None]
    kr, kc = kr[..., None, :], kc[..., None, :]
    rs = np.clip(qr - kh // 2, 0, rows - kh)
    cs = np.clip(qc - WIN_W // 2, 0, GRID_W - WIN_W)
    valid = (kr >= rs) & (kr < rs + kh) & (kc >= cs) & (kc < cs + WIN_W)
    idx_r = np.clip(kr - qr + WIN_H - 1, 0, 2 * WIN_H - 2).astype(np.int32)
    idx_c = np.clip(kc - qc + WIN_W - 1, 0, 2 * WIN_W - 2).astype(np.int32)
    bias = rpb.astype(jnp.float32)[:, idx_r, idx_c].transpose(1, 2, 0, 3, 4)

    s = jnp.einsum('bncqhd,bnckhd->bnchqk', qb, kb,
                   preferred_element_type=jnp.float32) * (1.0 / math.sqrt(d))
    s = jnp.where(jnp.asarray(valid)[None, :, :, None], s + bias[None], NEG)
    p = jax.nn.softmax(s, axis=-1)
    o = jnp.einsum('bnchqk,bnckhd->bncqhd', p.astype(v.dtype), vb)
    o = o.reshape(b, nrb, ncb, rb, Q_COL_BLOCK, h, d).transpose(0, 1, 3, 2, 4, 5, 6)
    o = o.reshape(b, rows_p, GRID_W, h * d)[:, :rows]
    return o.reshape(b, s_len, h * d)

def first_inputs(seed: int = 0) -> dict:
    key = jax.random.key(seed)
    ks = jax.random.split(key, 20)
    f32 = jnp.float32

    def nrm(k, shape, scale):
        return jax.random.normal(k, shape, f32) * scale

    L = DEPTH
    return {
        "x": jax.random.normal(ks[0], (BATCH, SEQ, D_MODEL), f32),
        "norm_mix": 1.0 + nrm(ks[1], (L, D_MODEL), 0.02),
        "w_in": nrm(ks[2], (L, D_MODEL, IN_COLS), D_MODEL ** -0.5),
        "a_q_norm": 1.0 + nrm(ks[3], (L, HEAD_DIM), 0.02),
        "a_k_norm": 1.0 + nrm(ks[4], (L, HEAD_DIM), 0.02),
        "a_sink": nrm(ks[5], (L, A_Q_HEADS), 0.5),
        "b_q_norm": 1.0 + nrm(ks[6], (L, HEAD_DIM), 0.02),
        "b_k_norm": 1.0 + nrm(ks[7], (L, HEAD_DIM), 0.02),
        "b_rpb": nrm(ks[8], (L, B_HEADS, 2 * WIN_H - 1, 2 * WIN_W - 1), 0.1),
        "w_branch_a": nrm(ks[9], (L, A_Q_DIM, D_MODEL), A_Q_DIM ** -0.5),
        "w_branch_b": nrm(ks[10], (L, B_DIM, D_MODEL), B_DIM ** -0.5),
        "w_out": nrm(ks[11], (L, D_MODEL, D_MODEL), D_MODEL ** -0.5),
        "norm_ffn": 1.0 + nrm(ks[12], (L, D_MODEL), 0.02),
        "w_up": nrm(ks[13], (L, D_MODEL, 2 * D_FF), D_MODEL ** -0.5),
        "conv_w": nrm(ks[14], (L, CONV_W, 2 * D_FF), CONV_W ** -0.5),
        "conv_b": nrm(ks[15], (L, 2 * D_FF), 0.01),
        "w_down": nrm(ks[16], (L, D_FF, D_MODEL), D_FF ** -0.5),
    }

def first_block(x, norm_mix, w_in, a_q_norm, a_k_norm, a_sink, b_q_norm, b_k_norm, b_rpb,
              w_branch_a, w_branch_b, w_out, norm_ffn, w_up, conv_w, conv_b, w_down):
    b, s_len, _ = x.shape
    pos = jnp.arange(s_len, dtype=jnp.float32)
    split_points = np.cumsum(IN_SPLITS)[:-1].tolist()
    for l in range(DEPTH):
        h = rmsnorm(x, norm_mix[l])
        proj = h @ w_in[l]
        qa, ka, va, qb, kb, vb, ga, gb = jnp.split(proj, split_points, axis=-1)

        qa = rope(rmsnorm(qa.reshape(b, s_len, A_Q_HEADS, HEAD_DIM), a_q_norm[l]), pos)
        ka = rope(rmsnorm(ka.reshape(b, s_len, A_KV_HEADS, HEAD_DIM), a_k_norm[l]), pos)
        va = va.reshape(b, s_len, A_KV_HEADS, HEAD_DIM)
        out_a = window_attention(qa, ka, va, a_sink[l])

        qb = rmsnorm(qb.reshape(b, s_len, B_HEADS, HEAD_DIM), b_q_norm[l])
        kb = rmsnorm(kb.reshape(b, s_len, B_HEADS, HEAD_DIM), b_k_norm[l])
        vb = vb.reshape(b, s_len, B_HEADS, HEAD_DIM)
        out_b = neighbourhood_attention(qb, kb, vb, b_rpb[l])

        merged = (jax.nn.sigmoid(ga) * (out_a @ w_branch_a[l])
                  + jax.nn.sigmoid(gb) * (out_b @ w_branch_b[l]))
        x = x + merged @ w_out[l]

        h2 = rmsnorm(x, norm_ffn[l])
        u = h2 @ w_up[l]
        up = jnp.pad(u, ((0, 0), (1, 1), (0, 0)))
        cw = conv_w[l]
        u = up[:, :-2] * cw[0] + up[:, 1:-1] * cw[1] + up[:, 2:] * cw[2] + conv_b[l]
        gate, val = jnp.split(u, 2, axis=-1)
        x = x + (jax.nn.silu(gate) * val) @ w_down[l]
    return x


NSA_HEADS = 8
NSA_KV_GROUPS = 2
NSA_HG = NSA_HEADS // NSA_KV_GROUPS
NSA_DK = 128
NSA_WIDTH = NSA_HEADS * NSA_DK
KV_W = NSA_KV_GROUPS * NSA_DK
CMP_BLOCK = 32
CMP_STRIDE = 16
SEL_BLOCK = 64
SEL_TOPN = 16
WINDOW_2 = 512
Q_BLOCK = 128
FORCE = 1e4
NEG_2 = -1e30
RET_HEADS = 4
RET_DK = 256
RET_DV = 256
RET_WIDTH = RET_HEADS * RET_DV
RET_CHUNK = 128
ROPE_BASE = 10000.0
GN_EPS = 1e-6
MIX_WIDTH = NSA_WIDTH + RET_WIDTH
T5_BUCKETS = 32
T5_MAX_DIST = 128
D_FF_2 = 4 * D_MODEL
NORM_EPS = 1e-6
IN_SIZES = [NSA_WIDTH, 6 * KV_W, 3 * NSA_HEADS, RET_HEADS * RET_DK, RET_HEADS * RET_DK, RET_WIDTH, RET_WIDTH]
D_IN = sum(IN_SIZES)
IN_OFFSETS = np.cumsum(IN_SIZES)[:-1].tolist()


def rms_norm(x, g):
    xf = x.astype(jnp.float32)
    y = xf * lax.rsqrt(jnp.mean(xf * xf, axis=-1, keepdims=True) + NORM_EPS)
    return (y * g.astype(jnp.float32)).astype(x.dtype)

def t5_bucket(rel):
    n = jnp.maximum(rel, 0)
    max_exact = T5_BUCKETS // 2
    nf = jnp.maximum(n, 1).astype(jnp.float32)
    large = max_exact + (jnp.log(nf / max_exact) / np.log(T5_MAX_DIST / max_exact)
                         * (T5_BUCKETS - max_exact)).astype(jnp.int32)
    large = jnp.minimum(large, T5_BUCKETS - 1)
    return jnp.where(n < max_exact, n, large)

def rope_2(x, pos):
    d = x.shape[-1]
    inv_freq = ROPE_BASE ** (-jnp.arange(0, d, 2, dtype=jnp.float32) / d)
    ang = pos.astype(jnp.float32)[:, None] * inv_freq[None, :]
    cos = jnp.cos(ang)[None, :, None, :]
    sin = jnp.sin(ang)[None, :, None, :]
    xf = x.astype(jnp.float32)
    x1, x2 = xf[..., : d // 2], xf[..., d // 2:]
    return jnp.concatenate([x1 * cos - x2 * sin, x2 * cos + x1 * sin], axis=-1).astype(x.dtype)

def compress_kv(kv, pe, w1, b1, w2):
    B, S, G, dk = kv.shape
    n_cmp = (S - CMP_BLOCK) // CMP_STRIDE + 1
    idx = jnp.arange(n_cmp)[:, None] * CMP_STRIDE + jnp.arange(CMP_BLOCK)[None, :]
    blocks = kv[:, idx] + pe[None, None, :, None, :]
    flat = blocks.transpose(0, 1, 3, 2, 4).reshape(B, n_cmp, G, CMP_BLOCK * dk)
    hid = jax.nn.gelu(flat @ w1 + b1)
    return hid @ w2

def nsa_attention(q, k_cmp, v_cmp, k_slc, v_slc, k_win, v_win, gates, t5_table):
    B, S, H, dk = q.shape
    G, Hg = NSA_KV_GROUPS, NSA_HG
    n_cmp = k_cmp.shape[1]
    n_sel = S // SEL_BLOCK
    top_n = min(SEL_TOPN, n_sel)
    scale = dk ** -0.5
    cmp_end = jnp.arange(n_cmp) * CMP_STRIDE + CMP_BLOCK - 1
    cs = np.arange(n_cmp) * CMP_STRIDE
    ss = np.arange(n_sel) * SEL_BLOCK
    overlap = (cs[:, None] <= ss[None, :] + SEL_BLOCK - 1) & (cs[:, None] + CMP_BLOCK - 1 >= ss[None, :])
    m_sel = jnp.asarray(overlap, jnp.float32)
    tbl = t5_table.astype(jnp.float32).reshape(T5_BUCKETS, G, Hg)
    ks_blocks = k_slc.reshape(B, n_sel, SEL_BLOCK, G, dk).transpose(0, 3, 1, 2, 4)
    vs_blocks = v_slc.reshape(B, n_sel, SEL_BLOCK, G, dk).transpose(0, 3, 1, 2, 4)
    kw_pad = jnp.pad(k_win, ((0, 0), (WINDOW_2, 0), (0, 0), (0, 0)))
    vw_pad = jnp.pad(v_win, ((0, 0), (WINDOW_2, 0), (0, 0), (0, 0)))
    qg = q.reshape(B, S, G, Hg, dk)
    gg = gates.reshape(B, S, G, Hg, 3)
    b_idx = jnp.arange(B)[:, None, None, None]
    g_idx = jnp.arange(G)[None, :, None, None]
    g_idx5 = jnp.arange(G)[None, :, None, None, None]
    jblk = jnp.arange(n_sel)

    def block(c):
        s0 = c * Q_BLOCK
        qc = lax.dynamic_slice_in_dim(qg, s0, Q_BLOCK, axis=1)
        tq = s0 + jnp.arange(Q_BLOCK)
        rel = tq[:, None] - cmp_end[None, :]
        s = jnp.einsum('bqghd,bngd->bghqn', qc, k_cmp).astype(jnp.float32) * scale
        s = s + tbl[t5_bucket(rel)].transpose(2, 3, 0, 1)[None]
        valid = rel >= 0
        p = jax.nn.softmax(jnp.where(valid, s, NEG_2), axis=-1)
        p = jnp.where(valid, p, 0.0)
        o_cmp = jnp.einsum('bghqn,bngd->bqghd', p.astype(v_cmp.dtype), v_cmp)
        imp = jnp.einsum('bghqn,nj->bgqj', p, m_sel)
        cur = tq // SEL_BLOCK
        blk_valid = jblk[None, :] * SEL_BLOCK <= tq[:, None]
        forced = (jblk[None, :] == 0) | (jblk[None, :] == cur[:, None]) | (jblk[None, :] == cur[:, None] - 1)
        imp = jnp.where(blk_valid, jnp.where(forced, FORCE, imp), -1.0)
        top_val, top_idx = lax.top_k(imp, top_n)
        ksel = ks_blocks[b_idx, g_idx, top_idx]
        vsel = vs_blocks[b_idx, g_idx, top_idx]
        kpos = top_idx[..., None] * SEL_BLOCK + jnp.arange(SEL_BLOCK)
        rel = tq[None, None, :, None, None] - kpos
        s = jnp.einsum('bqghd,bgqnld->bghqnl', qc, ksel).astype(jnp.float32) * scale
        s = s + tbl[t5_bucket(rel), g_idx5].transpose(0, 1, 5, 2, 3, 4)
        valid = ((rel >= 0) & (top_val >= 0)[..., None])[:, :, None]
        s = jnp.where(valid, s, NEG_2).reshape(B, G, Hg, Q_BLOCK, top_n * SEL_BLOCK)
        p = jax.nn.softmax(s, axis=-1).reshape(B, G, Hg, Q_BLOCK, top_n, SEL_BLOCK)
        o_slc = jnp.einsum('bghqnl,bgqnld->bqghd', p.astype(vsel.dtype), vsel)
        kw = lax.dynamic_slice_in_dim(kw_pad, s0, WINDOW_2 + Q_BLOCK, axis=1)
        vw = lax.dynamic_slice_in_dim(vw_pad, s0, WINDOW_2 + Q_BLOCK, axis=1)
        kpos = s0 - WINDOW_2 + jnp.arange(WINDOW_2 + Q_BLOCK)
        rel = tq[:, None] - kpos[None, :]
        valid = (rel >= 0) & (rel < WINDOW_2) & (kpos[None, :] >= 0)
        s = jnp.einsum('bqghd,bkgd->bghqk', qc, kw).astype(jnp.float32) * scale
        s = s + tbl[t5_bucket(rel)].transpose(2, 3, 0, 1)[None]
        p = jax.nn.softmax(jnp.where(valid, s, NEG_2), axis=-1)
        o_win = jnp.einsum('bghqk,bkgd->bqghd', p.astype(vw.dtype), vw)
        gc = lax.dynamic_slice_in_dim(gg, s0, Q_BLOCK, axis=1)
        o = gc[..., 0:1] * o_cmp + gc[..., 1:2] * o_slc + gc[..., 2:3] * o_win
        return o.reshape(B, Q_BLOCK, H * dk)

    out = lax.map(block, jnp.arange(S // Q_BLOCK))
    return out.transpose(1, 0, 2, 3).reshape(B, S, H * dk)

def retention(q, k, v, log_gamma):
    B, S, H, dk = q.shape
    dv = v.shape[-1]
    C = RET_CHUNK
    N = S // C
    k = k * (dk ** -0.5)
    qc = q.reshape(B, N, C, H, dk).transpose(1, 0, 3, 2, 4)
    kc = k.reshape(B, N, C, H, dk).transpose(1, 0, 3, 2, 4)
    vc = v.reshape(B, N, C, H, dv).transpose(1, 0, 3, 2, 4)
    idx = jnp.arange(C, dtype=jnp.float32)
    diff = idx[:, None] - idx[None, :]
    decay = jnp.where(diff[None] >= 0, jnp.exp(jnp.maximum(diff, 0.0)[None] * log_gamma[:, None, None]), 0.0)
    xi = jnp.exp((idx + 1.0)[None, :] * log_gamma[:, None])
    zeta = jnp.exp((C - 1.0 - idx)[None, :] * log_gamma[:, None])
    g_c = jnp.exp(C * log_gamma)
    inner = jnp.einsum('nbhcd,nbhmd->nbhcm', qc, kc).astype(jnp.float32) * decay
    inner = jnp.einsum('nbhcm,nbhme->nbhce', inner, vc.astype(jnp.float32))

    def step(R, xs):
        q_n, k_n, v_n = xs
        cross = jnp.einsum('bhcd,bhde->bhce', q_n.astype(jnp.float32), R) * xi[None, :, :, None]
        R = R * g_c[None, :, None, None] + jnp.einsum(
            'bhcd,bhce->bhde', k_n.astype(jnp.float32) * zeta[None, :, :, None], v_n.astype(jnp.float32))
        return R, cross

    R0 = jnp.zeros((B, H, dk, dv), jnp.float32)
    _, cross = lax.scan(step, R0, (qc, kc, vc))
    o = (inner + cross).transpose(1, 0, 3, 2, 4).reshape(B, S, H, dv)
    mu = jnp.mean(o, axis=-1, keepdims=True)
    var = jnp.mean(jnp.square(o - mu), axis=-1, keepdims=True)
    return (o - mu) * lax.rsqrt(var + GN_EPS)

def second_inputs(seed: int = 0) -> dict:
    key = jax.random.key(seed)
    ks = jax.random.split(key, 20)
    f32 = jnp.float32

    def nrm(k, shape, scale):
        return jax.random.normal(k, shape, f32) * scale

    def gain(k):
        return 1.0 + nrm(k, (DEPTH, D_MODEL), 0.05)

    LDK = CMP_BLOCK * NSA_DK
    return {
        "x": nrm(ks[0], (BATCH, SEQ, D_MODEL), 1.0),
        "norm_mix_pre": gain(ks[1]),
        "w_in": nrm(ks[2], (DEPTH, D_MODEL, D_IN), D_MODEL ** -0.5),
        "cmp_pe_k": nrm(ks[3], (DEPTH, CMP_BLOCK, NSA_DK), 0.1),
        "cmp_w1_k": nrm(ks[4], (DEPTH, LDK, NSA_DK), LDK ** -0.5),
        "cmp_b1_k": nrm(ks[5], (DEPTH, NSA_DK), 0.02),
        "cmp_w2_k": nrm(ks[6], (DEPTH, NSA_DK, NSA_DK), NSA_DK ** -0.5),
        "cmp_pe_v": nrm(ks[7], (DEPTH, CMP_BLOCK, NSA_DK), 0.1),
        "cmp_w1_v": nrm(ks[8], (DEPTH, LDK, NSA_DK), LDK ** -0.5),
        "cmp_b1_v": nrm(ks[9], (DEPTH, NSA_DK), 0.02),
        "cmp_w2_v": nrm(ks[10], (DEPTH, NSA_DK, NSA_DK), NSA_DK ** -0.5),
        "t5_bias": nrm(ks[11], (T5_BUCKETS, NSA_HEADS), 0.2),
        "w_out": nrm(ks[12], (DEPTH, MIX_WIDTH, D_MODEL), MIX_WIDTH ** -0.5),
        "norm_mix_post": gain(ks[13]),
        "norm_mlp_pre": gain(ks[14]),
        "w_up": nrm(ks[15], (DEPTH, D_MODEL, D_FF_2), D_MODEL ** -0.5),
        "w_down": nrm(ks[16], (DEPTH, D_FF_2, D_MODEL), D_FF_2 ** -0.5),
        "norm_mlp_post": gain(ks[17]),
    }

def second_block(x, norm_mix_pre, w_in, cmp_pe_k, cmp_w1_k, cmp_b1_k, cmp_w2_k, cmp_pe_v, cmp_w1_v,
              cmp_b1_v, cmp_w2_v, t5_bias, w_out, norm_mix_post, norm_mlp_pre, w_up, w_down,
              norm_mlp_post):
    B, S, _ = x.shape
    pos = jnp.arange(S)
    log_gamma = jnp.log(1.0 - jnp.exp2(-5.0 - jnp.arange(RET_HEADS, dtype=jnp.float32)))
    for l in range(DEPTH):
        h = rms_norm(x, norm_mix_pre[l])
        proj = h @ w_in[l]
        q_a, kv_a, gate_a, q_r, k_r, v_r, g_r = jnp.split(proj, IN_OFFSETS, axis=-1)
        q_a = q_a.reshape(B, S, NSA_HEADS, NSA_DK)
        kv6 = kv_a.reshape(B, S, 6, NSA_KV_GROUPS, NSA_DK)
        k_cmp = compress_kv(kv6[:, :, 0], cmp_pe_k[l], cmp_w1_k[l], cmp_b1_k[l], cmp_w2_k[l])
        v_cmp = compress_kv(kv6[:, :, 1], cmp_pe_v[l], cmp_w1_v[l], cmp_b1_v[l], cmp_w2_v[l])
        gates = jax.nn.sigmoid(gate_a.reshape(B, S, NSA_HEADS, 3))
        o_a = nsa_attention(q_a, k_cmp, v_cmp, kv6[:, :, 2], kv6[:, :, 3], kv6[:, :, 4], kv6[:, :, 5],
                            gates, t5_bias)
        q_r = rope_2(q_r.reshape(B, S, RET_HEADS, RET_DK), pos)
        k_r = rope_2(k_r.reshape(B, S, RET_HEADS, RET_DK), pos)
        o_r = retention(q_r, k_r, v_r.reshape(B, S, RET_HEADS, RET_DV), log_gamma)
        o_r = (jax.nn.silu(g_r.astype(jnp.float32)) * o_r.reshape(B, S, RET_WIDTH)).astype(x.dtype)
        mix = jnp.concatenate([o_a.astype(x.dtype), o_r], axis=-1) @ w_out[l]
        x = x + rms_norm(mix, norm_mix_post[l])
        h = rms_norm(x, norm_mlp_pre[l])
        u = jnp.square(jax.nn.relu(h @ w_up[l]))
        x = x + rms_norm(u @ w_down[l], norm_mlp_post[l])
    return x


def setup_inputs(seed=0):
    out = dict(first_inputs(seed))
    for name, value in second_inputs(seed + 1).items():
        if name != "x":
            out[name + "_2"] = value
    return out


def reference(
    x, norm_mix, w_in, a_q_norm, a_k_norm, a_sink, b_q_norm, b_k_norm, b_rpb, w_branch_a,
    w_branch_b, w_out, norm_ffn, w_up, conv_w, conv_b, w_down, norm_mix_pre_2, w_in_2,
    cmp_pe_k_2, cmp_w1_k_2, cmp_b1_k_2, cmp_w2_k_2, cmp_pe_v_2, cmp_w1_v_2, cmp_b1_v_2,
    cmp_w2_v_2, t5_bias_2, w_out_2, norm_mix_post_2, norm_mlp_pre_2, w_up_2, w_down_2,
    norm_mlp_post_2,
):
    x = first_block(
        x, norm_mix, w_in, a_q_norm, a_k_norm, a_sink, b_q_norm, b_k_norm, b_rpb, w_branch_a,
        w_branch_b, w_out, norm_ffn, w_up, conv_w, conv_b, w_down,
    )
    return second_block(
        x, norm_mix_pre_2, w_in_2, cmp_pe_k_2, cmp_w1_k_2, cmp_b1_k_2, cmp_w2_k_2, cmp_pe_v_2,
        cmp_w1_v_2, cmp_b1_v_2, cmp_w2_v_2, t5_bias_2, w_out_2, norm_mix_post_2, norm_mlp_pre_2,
        w_up_2, w_down_2, norm_mlp_post_2,
    )


_drawn_inputs = setup_inputs


def setup_inputs(seed=0):
    import zlib

    import numpy as np

    out = dict(_drawn_inputs(seed))
    spreads = {}
    factors = {'norm_mix': 7.425,
     'a_q_norm': 8.0,
     'a_k_norm': 8.0,
     'a_sink': 8.0,
     'b_q_norm': 8.0,
     'b_k_norm': 8.0,
     'b_rpb': 3.307,
     'conv_b': 40.488,
     'cmp_pe_k_2': 64.0,
     'cmp_b1_k_2': 200.0,
     'cmp_b1_v_2': 200.0,
     'norm_ffn': 8.0,
     'norm_mix_pre_2': 4.097,
     'cmp_w1_k_2': 4.323,
     'cmp_w2_k_2': 4.268,
     'cmp_pe_v_2': 38.485,
     't5_bias_2': 7.441,
     'norm_mix_post_2': 51.546,
     'norm_mlp_pre_2': 39.886,
     'norm_mlp_post_2': 53.074}
    for name, (base, spread) in spreads.items():
        noise = np.random.default_rng([zlib.crc32(name.encode()), seed]).standard_normal(out[name].shape)
        drawn = base * np.exp(spread * noise) if base else spread * noise
        out[name] = __import__('jax').numpy.asarray(drawn.astype(out[name].dtype))
    for name, factor in factors.items():
        out[name] = (out[name] * factor).astype(out[name].dtype)
    return out
```

```python
import math

import numpy as np

import concourse.bass as bass
from concourse import mybir

F32 = mybir.dt.float32
F32R = mybir.dt.float32r
ACT = mybir.ActivationFunctionType
ALU = mybir.AluOpType
AX = mybir.AxisListType

P = 128
SEQ = 256
NT = SEQ // P
D = 2048
KC = D // P
DFF1 = 5632
DFF2 = 8192
EPS = 1e-6
NEG = -1e30
HD = 128
SCALE = 1.0 / math.sqrt(HD)
COLS = 512
RAW_SLOTS = 4
SPLIT_SLOTS = 4
AHEAD = 3

IN1_BLOCKS = 9
GATE_BLOCKS = 8
IN2_BLOCKS = 5
RET_BLOCKS = 8
N_GATES = 24
RET_HEADS, RET_D = 4, 256
NCMP, CMP_BLOCK, CMP_STRIDE = 15, 32, 16
UP1_PASSES = [(0, 4), (4, 4), (8, 3)]
UP2_PASSES = 4
T5_BUCKETS = 32

S_IN1 = 0
S_GATE = S_IN1 + 8 * IN1_BLOCKS
S_BRANCH = S_GATE + 8 * GATE_BLOCKS
S_OUT1 = S_BRANCH + 8 * 4
S_FF1 = S_OUT1 + 8 * 4
S_UP1, S_DOWN1 = [], []
_s = S_FF1
for _, _n in UP1_PASSES:
    S_UP1.append(_s)
    _s += 16 * _n
    S_DOWN1.append(_s)
    _s += 8 * _n
S_IN2 = _s
S_RET = S_IN2 + 8 * IN2_BLOCKS
S_OUT2 = S_RET + 8 * RET_BLOCKS
S_UP2, S_DOWN2 = [], []
_s = S_OUT2 + 8 * 4
for _ in range(UP2_PASSES):
    S_UP2.append(_s)
    S_DOWN2.append(_s + 32)
    _s += 64
N_STEPS = _s

R_IN1 = 0
R_GATE = R_IN1 + IN1_BLOCKS
R_BRANCH = R_GATE + GATE_BLOCKS
R_OUT1 = R_BRANCH + 8
R_DOWN1 = [R_OUT1 + 4 + 4 * i for i in range(3)]
R_IN2 = R_DOWN1[-1] + 4
R_RET = R_IN2 + IN2_BLOCKS
R_OUT2 = R_RET + RET_BLOCKS
R_DOWN2 = [R_OUT2 + 4 + 4 * i for i in range(UP2_PASSES)]
C_UP1 = [0, 8, 16]
C_UP2 = [22 + 4 * i for i in range(UP2_PASSES)]

T_MIX1, T_MERGE, T_FFN1, T_MIX2, T_RETO, T_MLP2 = 0, 8, 16, 24, 32, 36

Q_GAIN = {"mix1": 0, "ffn1": 16, "mix2": 32, "mlp2": 48}
Q_BQ, Q_BK = 64, 65
Q_CONVW = 66
Q_CONVB = Q_CONVW + 3 * 88
Q_B1K = Q_CONVB + 88
Q_B1V = Q_B1K + 1
Q_PEK = Q_B1V + 1
Q_PEV = Q_PEK + CMP_BLOCK
Q_COLS = Q_PEV + CMP_BLOCK

FREE = 2

KB = 1024


class Chain:

    def __init__(self, eng, sem):
        self.eng, self.sem, self.n, self.past = eng, sem, 0, 0

    def enter(self, i, links):
        self.past, self.start, self.links = i * links, self.n, links

    def leave(self, passes):
        assert self.n - self.start == self.links, (self.n - self.start, self.links)
        self.n, self.past = self.start + self.links * passes, 0

    def link(self, ins):
        self.n += 1
        ins.then_inc(self.sem, 1)
        self.eng.wait_ge(self.sem, self.past + self.n)


def shape_constants():
    f = np.float32
    q = np.arange(SEQ)
    k = np.arange(SEQ)
    c = {}
    c["ident"] = np.eye(P, dtype=f)

    def tiles(m):
        return np.ascontiguousarray(m.reshape(NT, P, -1).transpose(1, 0, 2))

    band = np.where(np.abs(q[:, None] - k[None, :]) <= 128, 0.0, NEG).astype(f)
    c["band"] = tiles(band)
    qc, kc = q % 64, k % 64
    cs = np.clip(qc - 8, 0, 48)
    near = (kc[None, :] >= cs[:, None]) & (kc[None, :] < cs[:, None] + 16)
    c["near"] = np.ascontiguousarray(tiles(np.where(near, 0.0, NEG).astype(f))[:, ::-1, ::-1])

    def rope(half):
        inv = f(10000.0) ** (-np.arange(half, dtype=f) * f(1.0 / half))
        ang = (q.astype(f)[:, None] * inv[None, :].astype(f)).astype(f)
        return tiles(np.cos(ang).astype(f)), tiles(np.sin(ang).astype(f))

    c["cos1"], c["sin1"] = rope(64)
    c["cos2"], c["sin2"] = rope(128)
    def bucket(rel):
        n = np.maximum(rel, 0)
        nf = np.maximum(n, 1).astype(f)
        large = 16 + (np.log(nf / f(16)) / np.log(128 / 16) * 16).astype(np.int32)
        return np.where(n < 16, n, np.minimum(large, 31))

    up = np.arange(-256, 256)
    c["t5_up"] = (bucket(up)[None, :] == np.arange(32)[:, None]).astype(f)
    c["t5_ahead"] = np.broadcast_to(np.where(up >= 0, 0.0, NEG).astype(f), (8, 512)).copy()
    n = np.arange(NCMP)
    ok = (q[:, None] - (n * CMP_STRIDE + CMP_BLOCK - 1)[None, :]) >= 0
    c["cmp_mask"] = tiles(np.where(ok, 0.0, NEG).astype(f))
    c["cmp_seen"] = tiles(ok.astype(f))
    lg = np.log(1.0 - 2.0 ** (-5.0 - np.arange(RET_HEADS)))
    diff = (q[None, :] - k[:, None]).astype(np.float64)
    decay = np.where(diff >= 0, np.exp(np.maximum(diff, 0)[None] * lg[:, None, None]), 0.0)
    decay = decay * RET_D ** -0.5
    c["decay"] = np.ascontiguousarray(
        decay.reshape(RET_HEADS, NT, P, SEQ).transpose(2, 0, 1, 3)).astype(f)
    return c


CONST_NAMES = ["ident", "band", "near", "cos1", "sin1", "cos2", "sin2", "t5_up", "t5_ahead",
               "cmp_mask", "cmp_seen", "decay"]


def pack_columns(a):
    def cols(v):
        return np.asarray(v).reshape(-1, P).T

    conv = np.asarray(a["conv_w"])[0].reshape(3, 88, P).transpose(2, 1, 0).reshape(P, 88 * 3)
    parts = [cols(a["norm_mix"]), cols(a["norm_ffn"]), cols(a["norm_mix_pre_2"]), cols(a["norm_mlp_pre_2"]),
             cols(a["b_q_norm"]), cols(a["b_k_norm"]), conv, cols(a["conv_b"]),
             cols(a["cmp_b1_k_2"]), cols(a["cmp_b1_v_2"]),
             np.asarray(a["cmp_pe_k_2"])[0].T, np.asarray(a["cmp_pe_v_2"])[0].T]
    return np.ascontiguousarray(np.concatenate(parts, axis=1))


def build(nc, a, out, scratch, stop=99):
    def dram(name):
        return a[name]

    base = (nc.sbuf_base + 1023) // 1024 * 1024

    def at(name, shape, kb, dt=F32):
        return nc.alloc_sbuf_tensor_at(name, shape, dt, offset=int(base + kb * KB))

    x_rows = at("x_rows", [P, NT, D], 0)
    ot = at("ot", [P, KC, SEQ], 0)
    raw = [at(f"raw{i}", [P, 4, COLS], 16 + 8 * i) for i in range(RAW_SLOTS)]
    wh = [at(f"wh{i}", [P, 2, COLS], 48 + 4 * i, F32R) for i in range(SPLIT_SLOTS)]
    wl = [at(f"wl{i}", [P, 2, COLS], 64 + 4 * i, F32R) for i in range(SPLIT_SLOTS)]
    ha = at("ha", [P, KC, 2, SEQ], 80, F32R)
    hb = at("hb", [P, KC, 2, SEQ], 112, F32R)
    proj = at("proj", [P, IN1_BLOCKS, NT, COLS], 112)
    gates = at("gates", [P, GATE_BLOCKS, NT, COLS], 148)
    rot_a = at("rot_a", [P, 2, NT, HD], 180)
    rot_b = at("rot_b", [P, 2, NT, HD], 182)
    cos1 = at("cos1", [P, NT, 64], 184)
    sin1 = at("sin1", [P, NT, 64], 184.5)
    a_gain = at("a_gain", [P, 2, HD], 185)
    band = at("band", [P, NT, SEQ], 186)
    near = at("near", [P, NT, SEQ], 188)
    merged = [at(f"merged{i}", [P, NT, COLS], 180 + 4 * i) for i in range(2)]
    bias = [at(f"bias{i}", [P, NT, SEQ], 190 + 2 * i) for i in range(2)]
    qk_t = [at(f"qk_t{i}", [P, 2, SEQ], 194 + 2 * i) for i in range(2)]
    sco = [at(f"sco{i}", [P, NT, SEQ], 198 + 2 * i) for i in range(2)]
    prob = [at(f"prob{i}", [P, NT, SEQ], 202 + 2 * i) for i in range(2)]
    prob_t = [at(f"prob_t{i}", [P, NT, SEQ], 206 + 2 * i) for i in range(2)]
    tmp_a = at("tmp_a", [P, 4, HD], 210)
    tmp_b = at("tmp_b", [P, 4, HD], 212)
    rows = at("rows", [P, NT, D], 148)
    u_pad = [at(f"u_pad{i}", [P, 4, SEQ + 2], 164 + 4.25 * i) for i in range(2)]
    conv = [at(f"conv{i}", [P, 4, SEQ], 173 + 4 * i) for i in range(2)]
    act_f = at("act_f", [P, 4, SEQ], 181)
    u_sum = at("u_sum", [P, 4, SEQ], 164)
    u_act = at("u_act", [P, 4, SEQ], 168)
    y_rows = rows
    gain_row = at("gain_row", [P, D], 184)
    proj2 = at("proj2", [P, IN2_BLOCKS, NT, COLS], 148)
    ret = at("ret", [P, RET_BLOCKS, NT, COLS], 112)
    w1 = at("w1", [P, 2, CMP_BLOCK, HD], 112)
    w_gate = at("w_gate", [P, KC, N_GATES], 144)
    w_gate_h = at("w_gate_h", [P, KC, N_GATES], 145.5, F32R)
    w_gate_l = at("w_gate_l", [P, KC, N_GATES], 186, F32R)
    mix_t = at("mix_t", [P, 8, SEQ], 168)
    w2 = at("w2", [P, 2, HD], 176)
    cmp_bias = at("cmp_bias", [P, 8, NT, NCMP], 177)
    cmp_mask = at("cmp_mask", [P, NT, NCMP], 178)
    cmp_seen = at("cmp_seen", [P, NT, NCMP], 178.25)
    t5_tab = at("t5_tab", [T5_BUCKETS, 8], 178.5)
    gate24 = at("gate24", [P, NT, N_GATES], 178.75)
    kv_cmp_t = at("kv_cmp_t", [P, 4, SEQ], 180)
    cmp_in = at("cmp_in", [P, 2, CMP_BLOCK, 2, NCMP], 198)
    cmp_hid = at("cmp_hid", [P, 2, 2, NCMP], 184)
    cmp_g1 = at("cmp_g1", [P, 2, 2, NCMP], 184.5)
    cmp_g2 = at("cmp_g2", [P, 2, 2, NCMP], 185)
    cmp_k = at("cmp_k", [P, 2, NCMP], 185.5)
    cmp_v = at("cmp_v", [NCMP, 2, HD], 188)
    q_all = at("q_all", [P, 8, SEQ], 206)
    t5_up = at("t5_up", [T5_BUCKETS, 512], 190)
    t5_ahead = at("t5_ahead", [8, 512], 194)
    t5_rows = at("t5_rows", [8, 512], 196)
    cmp_s = at("cmp_s", [P, 8, NT, NCMP], 144)
    cmp_p = at("cmp_p", [P, 8, NT, NCMP], 145)
    cmp_m = at("cmp_m", [P, 8, NT], 146)
    cmp_n = at("cmp_n", [P, 8, NT], 146.25)
    cmp_pt = at("cmp_pt", [NCMP, 8, SEQ], 180)
    cos2 = at("cos2", [P, NT, HD], 180)
    sin2 = at("sin2", [P, NT, HD], 181)
    decay = at("decay", [P, RET_HEADS, NT, SEQ], 184)
    ret_q = [at(f"ret_q{i}", [P, 2, SEQ], 192 + 2 * i) for i in range(2)]
    ret_k = [at(f"ret_k{i}", [P, 2, SEQ], 196 + 2 * i) for i in range(2)]
    ret_p = [at(f"ret_p{i}", [P, NT, SEQ], 200 + 2 * i) for i in range(2)]
    rt = [at(f"rt{i}", [P, 2, HD], 204 + i) for i in range(4)]
    ret_o = at("ret_o", [P, NT, 1024], 148)
    small = 214
    ident = at("ident", [P, P], small)
    par = at("par", [P, Q_COLS], small + 0.5)
    sums = at("sums", [P, 16], small + 2.5)
    rstd = at("rstd", [P, 16], small + 2.5625)
    neghalf = at("neghalf", [P, 32], small + 2.625)
    ssq = at("ssq", [P, 32], small + 2.75)
    rsq = at("rsq", [P, 32], small + 2.875)
    sink = at("sink", [P, 8], small + 3)
    mx = at("mx", [P, 2, NT], small + 3.0625)
    nmx = at("nmx", [P, 2, NT], small + 3.09375)
    den = at("den", [P, 2, NT], small + 3.125)
    esink = at("esink", [P, 2, NT], small + 3.15625)
    rden = at("rden", [P, 2, NT], small + 3.1875)
    bst = at("bst", [P, 2, NT, 6], small + 3.25)
    bag = at("bag", [P, 2, NT, 2], small + 3.375)
    grs = at("grs", [P, 2, NT], small + 3.40625)
    ssb = at("ssb", [P, 2, 4], small + 3.4375)
    junk = at("junk", [P, NT, D], 112)
    unused = at("unused", [P, 4], small + 3.5625)
    rsb = at("rsb", [P, 2, 4], small + 3.5)


    psum = nc.alloc_psum_tensor("psum", [P, 8, COLS], F32)

    names = """
      x_in par_in ident_in cos1_in sin1_in again_in band_in near_in sink_in xre_in
      hi_done lo_done mm_done row_free chan_free
      act_chain dve_chain pool_chain pe_chain consts_set
      norm_ss norm_rs norm_rows tr_full tr_hi tr_lo
      an_ss an_rs a_ready bn_ss bn_rs bn_ok
      bias_ok at_qk at_qksb at_sc at_s at_nm at_p at_pn at_pt at_ptsb at_o at_osb
      sig_done merge_rows ot_hi ot_lo x_ready
      half_ok tap_done conv_mid conv_done silu_done act_ready hb_hi hb_lo usum_done
      row_done
      wg_in wg_hi wg_lo gate_mm gate_ok t5_in t5_mm t5_rows_ok t5_st cb_mm cb_ok
      kvt_mm kvt_ok qall_mm qall_ok cin_ok w1_in w2_in hid_mm hid_ok kv_mm kv_ok
      cs_mm cs_ok cs_exp cs_p cpt_mm cpt_ok
      rtab_in rope_ok silu_g rq_mm rq_ok rk_mm rk_ok rs_mm rp_ok ro_mm ro_stat ro_rs ro_ok
      post_ss post_rs post_ok grow_in out_in y_rows_ok cmask_in sync_bank
    """.split()
    sem = {n: nc.alloc_semaphore(n) for n in names}
    raw_in = [nc.alloc_semaphore(f"raw_in{i}") for i in range(RAW_SLOTS)]
    bias_in = [nc.alloc_semaphore(f"bias_in{i}") for i in range(2)]
    t5_bias_in = [nc.alloc_semaphore(f"t5_bias_in{i}") for i in range(2)]

    (hi_done, lo_done, mm_done, row_free, chan_free) = (
        sem[n] for n in ("hi_done", "lo_done", "mm_done", "row_free", "chan_free"))

    heads = []
    for h in range(8):
        heads.append(("band", h, proj, (h // 4, h % 4 * HD), (2, h // 4 * HD), (2, 256 + h // 4 * HD)))
    for h in range(8):
        heads.append(("near", h, proj, (3 + h // 4, h % 4 * HD), (5 + h // 4, h % 4 * HD),
                      (7 + h // 4, h % 4 * HD)))
    for h in range(8):
        for b, blk in (("slc", 3), ("win", 4)):
            heads.append((b, h, proj2, (h // 4, h % 4 * HD), (blk, h // 4 * HD), (blk, 256 + h // 4 * HD)))
    N1, NH = 16, len(heads)

    def outs_before(n):
        return n if n <= N1 else N1 + (n - N1) // 2

    QK_BANK, SC_BANK, PT_BANK, O_BANK = 4, 5, 6, 7

    block = nc.Block()
    block.__enter__()

    @block.sync
    def _(sp):
        def view(name):
            return a[name].rearrange("o (k p) n -> p (o k) n", p=P)

        def weight_load(u, i, src):
            if u >= RAW_SLOTS:
                sp.wait_ge(lo_done, 2 * (u - RAW_SLOTS) + 2 + 8 * i)
            sp.dma_start(raw[u % RAW_SLOTS][:], src).then_inc(raw_in[u % RAW_SLOTS], 16)

        def column_blocks(step, name, k0, groups, col, n):
            w = view(name)
            if groups == 4:
                with sp.Fori(0, n) as i:
                    for j in range(4):
                        weight_load(step // 2 + j, i, w[:, k0 + 4 * j:k0 + 4 * j + 4,
                                                        bass.ds(i * COLS + col, COLS)])
            else:
                for b in range(n):
                    for j in range(groups):
                        weight_load(step // 2 + groups * b + j, 0,
                                    w[:, k0 + 4 * j:k0 + 4 * j + 4, col + b * COLS:col + (b + 1) * COLS])

        sp.dma_start(x_rows[:], a["x"].rearrange("o (t p) n -> p (o t) n", p=P)).then_inc(sem["x_in"], 16)
        sp.dma_start(ident[:], a["ident"]).then_inc(sem["ident_in"], 16)
        sp.dma_start(par[:], a["params"]).then_inc(sem["par_in"], 16)
        w_in = view("w_in")
        for j in range(4):
            weight_load(j, 0, w_in[:, 4 * j:4 * j + 4, 0:COLS])
        for i, g in enumerate(("a_q_norm", "a_k_norm")):
            sp.dma_start(a_gain[:, i, :], a[g].partition_broadcast(P) if False else
                         bass.AP(a[g].tensor, 0, [[0, P], [1, HD]])).then_inc(sem["again_in"], 16)
        sp.dma_start(cos1[:], a["cos1"]).then_inc(sem["cos1_in"], 16)
        sp.dma_start(sin1[:], a["sin1"]).then_inc(sem["sin1_in"], 16)
        sp.dma_start(band[:], a["band"]).then_inc(sem["band_in"], 16)
        sp.dma_start(near[:], a["near"]).then_inc(sem["near_in"], 16)
        sp.dma_start(sink[:], bass.AP(a["a_sink"].tensor, 0, [[0, P], [1, 8]])).then_inc(sem["sink_in"], 16)

        def near_bias(h):
            if h >= 2:
                sp.wait_ge(sem["at_s"], 8 + h - 2 + 1)
            for t in range(NT):
                for r in range(2):
                    off = h * 15 * 31 + (4 + 2 * t + r) * 31 - 48
                    src = bass.AP(a["b_rpb"].tensor, off, [[1, 64], [31, 4], [1, 64]])
                    sp.dma_start(bias[h % 2][64 * r:64 * r + 64, 1 - t, :].rearrange("p (a c) -> p a c", a=4),
                                 src).then_inc(bias_in[h % 2], 16)

        near_bias(0)
        near_bias(1)
        column_blocks(8, "w_in", 0, 4, COLS, IN1_BLOCKS - 1)
        for u in range(4 * GATE_BLOCKS):
            b, j = u // 4, u % 4
            if u >= 2 * 8 + 7 and (u - 23) % 2 == 0 and (u - 23) // 2 + 2 < 8:
                near_bias((u - 23) // 2 + 2)
            weight_load(S_GATE // 2 + u, 0, w_in[:, 4 * j:4 * j + 4,
                                                 (IN1_BLOCKS + b) * COLS:(IN1_BLOCKS + b + 1) * COLS])
        near_bias(7)
        wa, wb = view("w_branch_a"), view("w_branch_b")
        with sp.Fori(0, 4) as i:
            for j in range(4):
                w = (wa, wb)[j // 2]
                weight_load(S_BRANCH // 2 + j, i, w[:, 4 * (j % 2):4 * (j % 2) + 4, bass.ds(i * COLS, COLS)])
        sp.wait_ge(sem["ot_lo"], 4)
        sp.dma_start(x_rows[:], a["x"].rearrange("o (t p) n -> p (o t) n", p=P)).then_inc(sem["xre_in"], 16)
        column_blocks(S_OUT1, "w_out", 0, 4, 0, 4)
        wu = view("w_up")
        for (j0, n), su, sd in zip(UP1_PASSES, S_UP1, S_DOWN1):
            with sp.Fori(0, n) as i:
                for j in range(8):
                    col = (j // 4) * DFF1 + j0 * COLS
                    u = su // 2 + j
                    sp.wait_ge(lo_done, 2 * (u - RAW_SLOTS) + 2 + 16 * i)
                    sp.dma_start(raw[u % RAW_SLOTS][:], wu[:, 4 * (j % 4):4 * (j % 4) + 4,
                                                           bass.ds(i * COLS + col, COLS)]
                                 ).then_inc(raw_in[u % RAW_SLOTS], 16)
            column_blocks(sd, "w_down", 4 * j0, n, 0, 4)
        column_blocks(S_IN2, "w_in_2", 0, 4, 0, 1)
        sp.wait_ge(mm_done, S_IN2)
        sp.dma_start(w_gate[:], a["w_in_2"].rearrange("o (k p) n -> p (o k) n", p=P)
                     [:, :, IN2_BLOCKS * COLS:IN2_BLOCKS * COLS + N_GATES]).then_inc(sem["wg_in"], 16)
        sp.dma_start(t5_tab[:], a["t5_bias_2"]).then_inc(sem["t5_in"], 16)
        sp.dma_start(t5_up[:], a["t5_up"]).then_inc(sem["t5_in"], 16)
        sp.dma_start(t5_ahead[:], a["t5_ahead"]).then_inc(sem["t5_in"], 16)
        sp.dma_start(cmp_mask[:], a["cmp_mask"]).then_inc(sem["t5_in"], 16)
        sp.dma_start(cmp_seen[:], a["cmp_seen"]).then_inc(sem["t5_in"], 16)
        sp.dma_start(w2[:, 0, :], a["cmp_w2_k_2"][0]).then_inc(sem["w2_in"], 16)
        sp.dma_start(w2[:, 1, :], a["cmp_w2_v_2"][0]).then_inc(sem["w2_in"], 16)
        for s, n in enumerate(("cmp_w1_k_2", "cmp_w1_v_2")):
            sp.dma_start(w1[:, s, :, :], a[n].rearrange("o (l p) n -> p (o l) n", p=P)).then_inc(sem["w1_in"], 16)
        column_blocks(S_IN2 + 8, "w_in_2", 0, 4, COLS, IN2_BLOCKS - 1)
        w_in2 = view("w_in_2")

        def retention_load(u):
            c0 = IN2_BLOCKS * COLS + N_GATES + u // 4 * COLS
            weight_load(S_RET // 2 + u, 0, w_in2[:, 4 * (u % 4):4 * (u % 4) + 4, c0:c0 + COLS])

        for u in range(4):
            retention_load(u)
        sp.wait_ge(sem["t5_rows_ok"], 1)
        sp.dma_start(scratch, t5_rows[:]).then_inc(sem["t5_st"], 16)
        sp.wait_ge(sem["t5_st"], 16)

        def t5_bias(h):
            if h >= 2:
                sp.wait_ge(sem["at_s"], N1 + 2 * (h - 2) + 2)
            else:
                sp.wait_ge(sem["cb_ok"], 1)
            for t in range(NT):
                src = bass.AP(scratch.tensor, 512 * h + P * t + 1, [[1, P], [1, SEQ]])
                sp.dma_start(bias[h % 2][:, 1 - t, :], src).then_inc(t5_bias_in[h % 2], 16)

        t5_bias(0)
        t5_bias(1)
        for u in range(4, 4 * RET_BLOCKS):
            if u >= 11 and (u - 11) % 4 == 0 and (u - 11) // 4 + 2 < 8:
                t5_bias((u - 11) // 4 + 2)
            retention_load(u)
        w_out2 = view("w_out_2")
        for j in range(4):
            weight_load(S_OUT2 // 2 + j, 0, w_out2[:, 4 * j:4 * j + 4, 0:COLS])
        sp.wait_ge(sem["at_osb"], outs_before(NH))
        sp.dma_start(cos2[:], a["cos2"]).then_inc(sem["rtab_in"], 16)
        sp.dma_start(sin2[:], a["sin2"]).then_inc(sem["rtab_in"], 16)
        sp.dma_start(decay[:], a["decay"]).then_inc(sem["rtab_in"], 16)
        column_blocks(S_OUT2 + 8, "w_out_2", 0, 4, COLS, 3)
        sp.wait_ge(sem["rp_ok"], RET_HEADS)
        sp.dma_start(gain_row[:], bass.AP(a["norm_mix_post_2"].tensor, 0, [[0, P], [1, D]])
                     ).then_inc(sem["grow_in"], 16)
        for p in range(UP2_PASSES):
            column_blocks(S_UP2[p], "w_up_2", 0, 4, 4 * p * COLS, 4)
            if p == UP2_PASSES - 1:
                sp.wait_ge(sem["post_ok"], NT)
                sp.dma_start(gain_row[:], bass.AP(a["norm_mlp_post_2"].tensor, 0, [[0, P], [1, D]])
                             ).then_inc(sem["grow_in"], 16)
            column_blocks(S_DOWN2[p], "w_down_2", 16 * p, 4, 0, 4)
        o = out.rearrange("o (t p) n -> p (o t) n", p=P)
        for t in range(NT):
            sp.wait_ge(sem["post_ok"], NT + t + 1)
            sp.dma_start(o[:, t, :], x_rows[:, t, :]).then_inc(sem["out_in"], 16)
        sp.wait_ge(sem["out_in"], 16 * NT)

    @block.gpsimd
    def _(pool):
        chain = Chain(pool, sem["pool_chain"])
        pool.memset(neghalf[:], -0.5).then_inc(sem["consts_set"], 1)
        for i in range(FREE):
            pool.memset(unused[:, i:i + 1], 0.0).then_inc(row_free, 1)
            pool.memset(unused[:, 2 + i:3 + i], 0.0).then_inc(chan_free, 1)
        pool.wait_ge(sem["consts_set"], 1)

        def inverse_root(dst, src, scale, n, done):
            chain.link(pool.tensor_scalar(dst, src, scale, EPS, ALU.mult, ALU.add))
            pool.tensor_tensor(dst, dst, neghalf[:, 0:n], ALU.pow).then_inc(done, 1)

        def norm(n):
            pool.wait_ge(sem["norm_ss"], 2 * n + 2)
            inverse_root(rstd[:, 2 * n:2 * n + 2], sums[:, 2 * n:2 * n + 2], 1.0 / D, 2, sem["norm_rs"])

        norm(0)
        pool.wait_ge(sem["an_ss"], 1)
        inverse_root(rsq[:, 0:24], ssq[:, 0:24], 1.0 / HD, 24, sem["an_rs"])
        pool.wait_ge(sem["near_in"], 16)

        def masked_bias(h):
            pool.wait_ge(bias_in[h % 2], 64 * (h // 2 + 1))
            pool.tensor_tensor(bias[h % 2][:], bias[h % 2][:], near[:], ALU.add).then_inc(sem["bias_ok"], 1)

        masked_bias(0)
        masked_bias(1)
        for h in range(8):
            pool.wait_ge(sem["bn_ss"], h + 1)
            inverse_root(rsb[:, h % 2, :], ssb[:, h % 2, :], 1.0 / HD, 4, sem["bn_rs"])
        for h in range(2, 8):
            masked_bias(h)
        norm(1)
        for p in range(2):
            pool.memset(u_pad[p][:, :, 0:1], 0.0).then_inc(sem["cmask_in"], 1)
            pool.memset(u_pad[p][:, :, SEQ + 1:SEQ + 2], 0.0).then_inc(sem["cmask_in"], 1)
        norm(2)
        for r in range(RET_HEADS):
            pool.wait_ge(sem["ro_stat"], r + 1)
            inverse_root(grs[:, r % 2, :], bag[:, r % 2, :, 1], 1.0, 2, sem["ro_rs"])
        for n in (3, 4, 5):
            norm(n)

    @block.scalar
    def _(act):
        chain = Chain(act, sem["act_chain"])

        def ahead(step, i=0, m=0):
            q = step + AHEAD
            act.wait_ge(raw_in[q // 2 % RAW_SLOTS], 16 * (q // 8 + 1) + 16 * m * i)
            if q >= SPLIT_SLOTS:
                act.wait_ge(mm_done, q - SPLIT_SLOTS + 1 + 8 * m * i)
            act.activation(wh[q % SPLIT_SLOTS][:], raw[q // 2 % RAW_SLOTS][:, 2 * (q % 2):2 * (q % 2) + 2, :],
                           ACT.Copy).then_inc(hi_done, 1)

        def row_blocks(step0, g0, n, per, evac, last=False, extra=None):
            if per != 8 or last or extra:
                for b in range(n):
                    for j in range(per):
                        if step0 + per * b + j + AHEAD < N_STEPS:
                            ahead(step0 + per * b + j)
                        if extra and b == 0:
                            extra(j)
                    evac(b, g0 + b, step0 + per * (b + 1), 0, 0)
                return
            if n % 2:
                for j in range(8):
                    ahead(step0 + j)
                evac(0, g0, step0 + 8, 0, 0)
            with act.Fori(0, n // 2) as i:
                for b in (n % 2, n % 2 + 1):
                    for j in range(8):
                        ahead(step0 + 8 * b + j, i, 2)
                    evac(b, g0 + b, step0 + 8 * (b + 1), i, 2)

        def copy_rows(dst):
            def evac(b, g, end, i, m):
                act.wait_ge(mm_done, end + 8 * m * i)
                act.activation(dst[:, b + m * i, :, :], psum[:, 2 * (g % 2):2 * (g % 2) + 2, :],
                               ACT.Copy).then_inc(row_free, 1)
            return evac

        def no_evac(b, g, end, i, m):
            pass

        def norm_sums(n, src, ready, value, done=None):
            for t in range(NT):
                if ready is not None:
                    act.wait_ge(ready, value)
                act.activation(rows[:, t, :], src[:, t, :], ACT.Square,
                               accum_out=sums[:, 2 * n + t:2 * n + t + 1]).then_inc(sem["norm_ss"], 1)

        def transposed_hi(dst, fill0, chunk0, gain):
            for f in range(8):
                F = fill0 + f
                act.wait_ge(sem["tr_full"], F + 1)
                for c in range(2):
                    ins = act.activation(dst[:, 2 * f + c, 0, :], psum[:, 4 + F % 4, 256 * c:256 * c + 256],
                                         ACT.Copy, scale=par[:, Q_GAIN[gain] + 2 * f + c:Q_GAIN[gain] + 2 * f + c + 1])
                ins.then_inc(sem["tr_hi"], 1)

        def head_stage(j, k, last):
            if j == 0 and k < last:
                n = k
                act.wait_ge(sem["at_qk"], n + 1)
                if n >= 2:
                    act.wait_ge(sem["at_sc"], n - 1)
                if heads[n][0] == "near":
                    for i, g in enumerate((Q_BQ, Q_BK)):
                        ins = act.activation(qk_t[n % 2][:, i, :], psum[:, QK_BANK, 256 * i:256 * i + 256],
                                             ACT.Copy, scale=par[:, g:g + 1])
                else:
                    ins = act.activation(qk_t[n % 2][:], psum[:, QK_BANK, :].rearrange("p (a b) -> p a b", a=2),
                                         ACT.Copy)
                ins.then_inc(sem["at_qksb"], 1)
            n = k - 1
            if j == 1 and n >= first[0]:
                act.wait_ge(sem["at_pt"], n + 1)
                if n >= 2:
                    act.wait_ge(sem["at_o"], n - 1)
                act.activation(prob_t[n % 2][:], psum[:, PT_BANK, :].rearrange("p (a b) -> p a b", a=2),
                               ACT.Copy).then_inc(sem["at_ptsb"], 1)
            if j == 2 and k < last:
                n = k
                act.wait_ge(sem["at_nm"], n + 1)
                if n >= 2:
                    act.wait_ge(sem["at_pt"], n - 1)
                if heads[n][0] == "band":
                    h = heads[n][1]
                    act.activation(esink[:, n % 2, :], nmx[:, n % 2, :], ACT.Exp, bias=sink[:, h:h + 1])
                for t in range(NT):
                    ins = act.activation(prob[n % 2][:, t, :], sco[n % 2][:, t, :], ACT.Exp,
                                         bias=nmx[:, n % 2, t:t + 1], accum_out=den[:, n % 2, t:t + 1])
                ins.then_inc(sem["at_p"], 1)
            n = k - 1
            if j == 3 and n >= first[0] and heads[n][0] != "slc":
                act.wait_ge(sem["at_o"], n + 1)
                kind, h = heads[n][:2]
                dst = mix_t[:, h, :] if kind == "win" else ot[:, h + (8 if kind == "near" else 0), :]
                act.activation(dst, psum[:, O_BANK, 0:SEQ], ACT.Copy).then_inc(sem["at_osb"], 1)

        first = [0]

        act.wait_ge(sem["x_in"], 16)
        norm_sums(0, x_rows, None, 0)
        for q in range(AHEAD):
            ahead(q - AHEAD)
        act.wait_ge(sem["par_in"], 16)
        transposed_hi(ha, T_MIX1, 0, "mix1")
        row_blocks(S_IN1, R_IN1, IN1_BLOCKS, 8, copy_rows(proj))

        act.wait_ge(sem["sink_in"], 16)
        for s in range(8 * GATE_BLOCKS):
            ahead(S_GATE + s)
            head_stage(s % 4, s // 4, N1)
            if s % 8 == 7:
                copy_rows(gates)(s // 8, R_GATE + s // 8, S_GATE + s + 1, 0, 0)
        for j in range(4):
            head_stage(j, N1, N1)
        act.wait_ge(mm_done, S_BRANCH)
        act.wait_ge(sem["at_osb"], N1)
        for c in range(4):
            act.activation(ha[:, 4 * c:4 * c + 4, 0, :], ot[:, 4 * c:4 * c + 4, :], ACT.Copy
                           ).then_inc(sem["ot_hi"], 1)

        def merged_hi(n):
            for f in range(2):
                F = T_MERGE + 2 * n + f
                act.wait_ge(sem["tr_full"], F + 1)
                act.activation(hb[:, 2 * (F - T_MERGE):2 * (F - T_MERGE) + 2, 0, :],
                               psum[:, 4 + F % 4, :].rearrange("p (a b) -> p a b", a=2), ACT.Copy
                               ).then_inc(sem["tr_hi"], 1)

        act.wait_ge(row_free, FREE + R_GATE + GATE_BLOCKS)
        for n in range(4):
            for b in range(2):
                ins = act.activation(gates[:, 4 * b + n, :, :], gates[:, 4 * b + n, :, :], ACT.Sigmoid)
            ins.then_inc(sem["sig_done"], 1)
            for j in range(8):
                if j == 4 and n:
                    merged_hi(n - 1)
                ahead(S_BRANCH + 8 * n + j)
        merged_hi(3)
        row_blocks(S_OUT1, R_OUT1, 4, 8, no_evac)
        norm_sums(1, x_rows, row_free, FREE + R_OUT1 + 4)
        transposed_hi(ha, T_FFN1, 0, "ffn1")

        act.wait_ge(sem["cmask_in"], 4)
        def up1_stage(p, j, v, pair, i):
            if j == 0:
                act.wait_ge(mm_done, S_UP1[p] + 8 * v + 8 + 16 * i)
                act.activation(u_pad[v][:, :, 1:SEQ + 1], psum[:, 4 * v:4 * v + 4, 0:SEQ], ACT.Copy
                               ).then_inc(sem["half_ok"], 1)
            if j == 1:
                act.wait_ge(chan_free, FREE + v + 1 + 2 * pair)
                for s in range(4):
                    chunk = 44 * v + 4 * pair + s
                    w = Q_CONVW + 3 * chunk + 1
                    ins = act.activation(conv[v][:, s, :], u_pad[v][:, s, 1:SEQ + 1], ACT.Identity,
                                         scale=par[:, bass.ds(w, 1)], bias=par[:, bass.ds(Q_CONVB + chunk, 1)])
                ins.then_inc(sem["conv_mid"], 1)
            if j == 3 and v == 0:
                act.wait_ge(sem["conv_done"], 1 + 2 * pair)
                act.activation(conv[0][:], conv[0][:], ACT.Silu).then_inc(sem["silu_done"], 1)
            if j == 4 and v == 1:
                act.wait_ge(sem["act_ready"], pair + 1)
                act.activation(hb[:, bass.ds(4 * i, 4), 0, :], act_f[:], ACT.Copy).then_inc(sem["hb_hi"], 1)

        for p, (j0, n) in enumerate(UP1_PASSES):
            for j in range(8):
                ahead(S_UP1[p] + j)
            with act.Fori(0, n - 1) as i:
                for j in range(8):
                    ahead(S_UP1[p] + 8 + j, i, 2)
                    up1_stage(p, j, 0, j0 + i, i)
                for j in range(8):
                    ahead(S_UP1[p] + 16 + j, i, 2)
                    up1_stage(p, j, 1, j0 + i, i)
            for j in range(8):
                ahead(S_UP1[p] + 16 * n - 8 + j)
                up1_stage(p, j, 0, j0 + n - 1, n - 1)

            def tail(j):
                for stage in range(8) if n == 4 else ([0], [1, 2], [3], [4, 5], [], [])[j]:
                    if n < 4 or stage == j:
                        up1_stage(p, stage, 1, j0 + n - 1, n - 1)

            row_blocks(S_DOWN1[p], R_DOWN1[p], 4, 2 * n, no_evac, extra=tail)

        norm_sums(2, x_rows, row_free, FREE + R_DOWN1[-1] + 4)
        transposed_hi(ha, T_MIX2, 0, "mix2")
        row_blocks(S_IN2, R_IN2, IN2_BLOCKS, 8, copy_rows(proj2))
        act.wait_ge(sem["wg_in"], 16)
        act.activation(w_gate_h[:], w_gate[:], ACT.Copy).then_inc(sem["wg_hi"], 1)
        act.wait_ge(sem["gate_mm"], 1)
        act.activation(gate24[:], psum[:, 6, 0:2 * N_GATES].rearrange("p (a b) -> p a b", a=2), ACT.Sigmoid
                       ).then_inc(sem["gate_ok"], 1)
        for f in range(2):
            act.wait_ge(sem["kvt_mm"], f + 1)
            act.activation(kv_cmp_t[:, 2 * f:2 * f + 2, :], psum[:, 4 + f, :].rearrange("p (a b) -> p a b", a=2),
                           ACT.Copy).then_inc(sem["kvt_ok"], 1)
        for f in range(4):
            act.wait_ge(sem["qall_mm"], f + 1)
            act.activation(q_all[:, 2 * f:2 * f + 2, :], psum[:, 4 + (f + 2) % 4, :].rearrange("p (a b) -> p a b", a=2),
                           ACT.Copy).then_inc(sem["qall_ok"], 1)
        for s in range(2):
            act.wait_ge(sem["hid_mm"], s + 1)
            act.activation(cmp_hid[:, s, :, :], psum[:, 4 + s, 0:2 * NCMP].rearrange("p (a b) -> p a b", a=2),
                           ACT.Gelu_apprx_tanh, bias=par[:, Q_B1K + s:Q_B1K + s + 1]).then_inc(sem["hid_ok"], 1)
        act.wait_ge(sem["kv_mm"], 1)
        act.activation(cmp_k[:], psum[:, 6, 0:2 * NCMP].rearrange("p (a b) -> p a b", a=2), ACT.Copy
                       ).then_inc(sem["kv_ok"], 1)
        act.wait_ge(sem["kv_mm"], 2)
        act.activation(cmp_v[:], psum[0:NCMP, 7, 0:2 * HD].rearrange("p (a b) -> p a b", a=2), ACT.Copy
                       ).then_inc(sem["kv_ok"], 1)
        act.wait_ge(sem["cs_ok"], 1)
        act.activation(cmp_p[:], cmp_s[:], ACT.Exp).then_inc(sem["cs_exp"], 1)
        for f in range(4):
            act.wait_ge(sem["cpt_mm"], f + 1)
            act.activation(cmp_pt[:, 2 * f:2 * f + 2, :], psum[0:NCMP, 4 + f, :].rearrange("p (a b) -> p a b", a=2),
                           ACT.Copy).then_inc(sem["cpt_ok"], 1)
        act.wait_ge(sem["t5_st"], 16)
        first[0] = N1
        for s in range(8 * RET_BLOCKS):
            ahead(S_RET + s)
            head_stage(s % 4, N1 + s // 4, NH)
            if s % 8 == 7:
                copy_rows(ret)(s // 8, R_RET + s // 8, S_RET + s + 1, 0, 0)
        for j in range(4):
            head_stage(j, NH, NH)
        act.wait_ge(mm_done, S_OUT2)
        act.wait_ge(sem["at_osb"], outs_before(NH))
        for c in range(2):
            act.activation(ha[:, 4 * c:4 * c + 4, 0, :], mix_t[:, 4 * c:4 * c + 4, :], ACT.Copy
                           ).then_inc(sem["ot_hi"], 1)
        act.wait_ge(row_free, FREE + R_RET + RET_BLOCKS)
        for b in (6, 7):
            ins = act.activation(ret[:, b, :, :], ret[:, b, :, :], ACT.Silu)
        ins.then_inc(sem["silu_g"], 1)
        for r in range(RET_HEADS):
            act.wait_ge(sem["rq_mm"], r + 1)
            if r >= 2:
                act.wait_ge(sem["rs_mm"], r - 1)
            act.activation(ret_q[r % 2][:], psum[:, 4, :].rearrange("p (a b) -> p a b", a=2), ACT.Copy
                           ).then_inc(sem["rq_ok"], 1)
            act.wait_ge(sem["rk_mm"], r + 1)
            act.activation(ret_k[r % 2][:], psum[:, 5, :].rearrange("p (a b) -> p a b", a=2), ACT.Copy
                           ).then_inc(sem["rk_ok"], 1)
        for f in range(4):
            F = T_RETO + f
            act.wait_ge(sem["tr_full"], F + 1)
            act.activation(ha[:, 8 + 2 * f:10 + 2 * f, 0, :], psum[:, 4 + F % 4, :].rearrange("p (a b) -> p a b", a=2),
                           ACT.Copy).then_inc(sem["tr_hi"], 1)

        def mix_rows(b, g, end, i, m):
            act.wait_ge(mm_done, end + 8 * m * i)
            act.activation(rows[:, :, bass.ds((b + m * i) * COLS, COLS)], psum[:, 2 * (g % 2):2 * (g % 2) + 2, :],
                           ACT.Copy).then_inc(row_free, 1)

        row_blocks(S_OUT2, R_OUT2, 4, 8, mix_rows)
        for t in range(NT):
            act.wait_ge(row_free, FREE + R_OUT2 + 4)
            act.activation(junk[:, t, :], rows[:, t, :], ACT.Square,
                           accum_out=sums[:, 6 + t:7 + t]).then_inc(sem["norm_ss"], 1)
        for t in range(NT):
            act.wait_ge(sem["post_ok"], t + 1)
            act.activation(rows[:, t, :], x_rows[:, t, :], ACT.Square,
                           accum_out=sums[:, 8 + t:9 + t]).then_inc(sem["norm_ss"], 1)
        transposed_hi(ha, T_MLP2, 0, "mlp2")
        for p in range(UP2_PASSES):
            with act.Fori(0, 2) as i:
                for v in range(2):
                    for j in range(8):
                        ahead(S_UP2[p] + 8 * v + j, i, 2)
                    c = C_UP2[p] - C_UP2[0] + v
                    act.wait_ge(mm_done, S_UP2[p] + 8 * v + 8 + 16 * i)
                    act.activation(u_sum[:], psum[:, 4 * v:4 * v + 4, 0:SEQ], ACT.Copy
                                   ).then_inc(sem["usum_done"], 1)
                    act.wait_ge(sem["act_ready"], 11 + c + 1 + 2 * i)
                    act.activation(hb[:, bass.ds(8 * i + 4 * v, 4), 0, :], u_act[:], ACT.Copy
                                   ).then_inc(sem["hb_hi"], 1)
            row_blocks(S_DOWN2[p], R_DOWN2[p], 4, 8, no_evac, last=p == UP2_PASSES - 1)
        for t in range(NT):
            act.wait_ge(row_free, FREE + R_DOWN2[-1] + 4)
            act.activation(junk[:, t, :], rows[:, t, :], ACT.Square,
                           accum_out=sums[:, 10 + t:11 + t]).then_inc(sem["norm_ss"], 1)

    @block.vector
    def _(dve):
        chain = Chain(dve, sem["dve_chain"])

        def ahead(step, i=0, m=0):
            q = step + AHEAD
            dve.wait_ge(hi_done, q + 1 + 8 * m * i)
            dve.tensor_tensor(wl[q % SPLIT_SLOTS][:], raw[q // 2 % RAW_SLOTS][:, 2 * (q % 2):2 * (q % 2) + 2, :],
                              wh[q % SPLIT_SLOTS][:].bitcast(F32), ALU.subtract).then_inc(lo_done, 1)

        def row_blocks(step0, g0, n, per, evac, last=False, extra=None):
            if per != 8 or last or extra:
                for b in range(n):
                    for j in range(per):
                        if step0 + per * b + j + AHEAD < N_STEPS:
                            ahead(step0 + per * b + j)
                        if extra and b == 0:
                            extra(j)
                    evac(b, g0 + b, step0 + per * (b + 1), 0, 0)
                return
            if n % 2:
                for j in range(8):
                    ahead(step0 + j)
                evac(0, g0, step0 + 8, 0, 0)
            with dve.Fori(0, n // 2) as i:
                for b in (n % 2, n % 2 + 1):
                    for j in range(8):
                        ahead(step0 + 8 * b + j, i, 2)
                    evac(b, g0 + b, step0 + 8 * (b + 1), i, 2)

        def no_evac(b, g, end, i, m):
            pass

        def scaled_rows(n, src):
            dve.wait_ge(sem["norm_rs"], n + 1)
            for t in range(NT):
                dve.tensor_scalar(rows[:, t, :], src[:, t, :], rstd[:, 2 * n + t:2 * n + t + 1], None, ALU.mult
                                  ).then_inc(sem["norm_rows"], 1)

        def transposed_lo(dst, fill0, gain):
            for f in range(8):
                F = fill0 + f
                dve.wait_ge(sem["tr_hi"], F + 1)
                for c in range(2):
                    col = Q_GAIN[gain] + 2 * f + c
                    ins = dve.scalar_tensor_tensor(
                        dst[:, 2 * f + c, 1, :], psum[:, 4 + F % 4, 256 * c:256 * c + 256], par[:, col:col + 1],
                        dst[:, 2 * f + c, 0, :].bitcast(F32), ALU.mult, ALU.subtract)
                ins.then_inc(sem["tr_lo"], 1)

        def plain_lo(dst, F):
            dve.wait_ge(sem["tr_hi"], F + 1)
            dve.tensor_tensor(dst[:, :, 1, :], psum[:, 4 + F % 4, :].rearrange("p (a b) -> p a b", a=2),
                              dst[:, :, 0, :].bitcast(F32), ALU.subtract).then_inc(sem["tr_lo"], 1)

        def head_stage(j, k, last):
            if k >= last:
                return
            n = k
            kind, h = heads[n][:2]
            if j == 2:
                dve.wait_ge(sem["at_sc"], n + 1)
                if n >= 2:
                    dve.wait_ge(sem["at_p"], n - 1)
                if kind == "near":
                    dve.wait_ge(sem["bias_ok"], h + 1)
                elif kind != "band":
                    dve.wait_ge(t5_bias_in[h % 2], 32 * (h // 2 + 1))
                b = (band if kind == "band" else bias[h % 2])[:].rearrange("p a b -> p (a b)")
                if kind != "band":
                    b = bass.AP(b.tensor, b.offset + NT * SEQ - 1, [list(b.ap[0]), [-1, NT * SEQ]])
                dve.scalar_tensor_tensor(sco[n % 2][:].rearrange("p a b -> p (a b)"), psum[:, SC_BANK, :], SCALE,
                                         b, ALU.mult, ALU.add
                                         ).then_inc(sem["at_s"], 1)
                dve.wait_ge(sem["at_s"], n + 1)
                chain.link(dve.reduce_max(mx[:, n % 2, :], sco[n % 2][:], AX.X))
                if kind == "band":
                    dve.tensor_scalar(nmx[:, n % 2, :], mx[:, n % 2, :], sink[:, h:h + 1], -1.0, ALU.max, ALU.mult
                                      ).then_inc(sem["at_nm"], 1)
                else:
                    dve.tensor_scalar(nmx[:, n % 2, :], mx[:, n % 2, :], -1.0, None, ALU.mult
                                      ).then_inc(sem["at_nm"], 1)
            if j == 3:
                dve.wait_ge(sem["at_p"], n + 1)
                if kind == "band":
                    chain.link(dve.tensor_tensor(den[:, n % 2, :], den[:, n % 2, :], esink[:, n % 2, :], ALU.add))
                chain.link(dve.reciprocal(rden[:, n % 2, :], den[:, n % 2, :]))
                if kind in ("slc", "win"):
                    g = 3 * h + (1 if kind == "slc" else 2)
                    chain.link(dve.tensor_tensor(rden[:, n % 2, :], rden[:, n % 2, :], gate24[:, :, g], ALU.mult))
                for t in range(NT):
                    ins = dve.tensor_scalar(prob[n % 2][:, t, :], prob[n % 2][:, t, :], rden[:, n % 2, t:t + 1],
                                            None, ALU.mult)
                ins.then_inc(sem["at_pn"], 1)

        dve.wait_ge(sem["cos1_in"], 16)
        dve.wait_ge(sem["sin1_in"], 16)
        dve.wait_ge(sem["again_in"], 32)
        for i in range(2):
            g = [a_gain[:, i, 64 * s:64 * s + 64].unsqueeze(1).to_broadcast([P, NT, 64]) for s in range(2)]
            dve.tensor_tensor(rot_a[:, i, :, 0:64], cos1[:], g[0], ALU.mult)
            dve.tensor_tensor(rot_a[:, i, :, 64:128], cos1[:], g[1], ALU.mult)
            dve.tensor_tensor(rot_b[:, i, :, 64:128], sin1[:], g[0], ALU.mult)
            chain.link(dve.tensor_tensor(rot_b[:, i, :, 0:64], sin1[:], g[1], ALU.mult))
        chain.link(dve.tensor_scalar(rot_b[:, :, :, 0:64], rot_b[:, :, :, 0:64], -1.0, None, ALU.mult))

        dve.wait_ge(sem["x_in"], 16)
        scaled_rows(0, x_rows)
        for q in range(AHEAD):
            ahead(q - AHEAD)
        dve.wait_ge(sem["par_in"], 16)
        transposed_lo(ha, T_MIX1, "mix1")
        row_blocks(S_IN1, R_IN1, IN1_BLOCKS, 8, no_evac)

        dve.wait_ge(row_free, FREE + 3)
        pieces = [(0, 0, 0, 4), (0, 1, 0, 4), (1, 0, 0, 4), (1, 1, 0, 4), (2, 0, 1, 2), (2, 1, 1, 2)]

        def piece(b, t, nh):
            return proj[:, b, t, 0:nh * HD].rearrange("p (h d) -> p h d", d=HD)

        for i, (b, t, _, nh) in enumerate(pieces):
            x = piece(b, t, nh)
            chain.link(dve.tensor_tensor(tmp_a[:, 0:nh, :], x, x, ALU.mult))
            chain.link(dve.reduce_sum(ssq[:, 4 * i:4 * i + nh], tmp_a[:, 0:nh, :], AX.X))
        dve.memset(ssq[:, 18:20], 1.0)
        dve.memset(ssq[:, 22:24], 1.0).then_inc(sem["an_ss"], 1)
        dve.wait_ge(sem["an_rs"], 1)
        for i, (b, t, kind, nh) in enumerate(pieces):
            x = piece(b, t, nh)
            r = rsq[:, 4 * i:4 * i + nh].unsqueeze(2).to_broadcast([P, nh, HD])
            chain.link(dve.tensor_tensor(x, x, r, ALU.mult))

            def row(tab, lo, hi):
                return tab[:, kind, t, lo:hi].unsqueeze(1).to_broadcast([P, nh, hi - lo])

            dve.tensor_tensor(tmp_a[:, 0:nh, :], x, row(rot_a, 0, HD), ALU.mult)
            dve.tensor_tensor(tmp_b[:, 0:nh, 0:64], x[:, :, 64:128], row(rot_b, 0, 64), ALU.mult)
            chain.link(dve.tensor_tensor(tmp_b[:, 0:nh, 64:128], x[:, :, 0:64], row(rot_b, 64, 128), ALU.mult))
            dve.tensor_tensor(x, tmp_a[:, 0:nh, :], tmp_b[:, 0:nh, :], ALU.add).then_inc(sem["a_ready"], 1)

        def near_view(h):
            c = h % 4 * HD
            return proj[:, 3 + h // 4:6 + h // 4:2, :, c:c + HD]

        dve.wait_ge(sem["band_in"], 16)
        for s in range(8 * GATE_BLOCKS):
            j, k = s % 4, s // 4
            ahead(S_GATE + s)
            if k < 8 and j == 0:
                t4 = tmp_b[:].rearrange("p (a b) d -> p a b d", a=2)
                if k == 0:
                    dve.wait_ge(row_free, FREE + R_GATE)
                    dve.wait_ge(sem["a_ready"], len(pieces))
                chain.link(dve.tensor_tensor(t4, near_view(k), near_view(k), ALU.mult))
                dve.reduce_sum(ssb[:, k % 2, :], tmp_b[:], AX.X).then_inc(sem["bn_ss"], 1)
            if k < 8 and j == 1:
                dve.wait_ge(sem["bn_rs"], k + 1)
                r = rsb[:, k % 2, :].rearrange("p (a b) -> p a b", a=2).unsqueeze(3).to_broadcast([P, 2, NT, HD])
                dve.tensor_tensor(near_view(k), near_view(k), r, ALU.mult).then_inc(sem["bn_ok"], 1)
            head_stage(j, k, N1)
        for c in range(4):
            dve.wait_ge(sem["ot_hi"], c + 1)
            dve.tensor_tensor(ha[:, 4 * c:4 * c + 4, 1, :], ot[:, 4 * c:4 * c + 4, :],
                              ha[:, 4 * c:4 * c + 4, 0, :].bitcast(F32), ALU.subtract).then_inc(sem["ot_lo"], 1)

        def merged_lo(n):
            for f in range(2):
                plain_lo(hb[:, 4 * n + 2 * f:4 * n + 2 * f + 2], T_MERGE + 2 * n + f)

        for n in range(4):
            for j in range(4):
                ahead(S_BRANCH + 8 * n + j)
            dve.wait_ge(mm_done, S_BRANCH + 8 * n + 4)
            dve.wait_ge(sem["sig_done"], n + 1)
            if n >= 2:
                dve.wait_ge(sem["tr_full"], T_MERGE + 2 * n - 2)
            dve.tensor_tensor(merged[n % 2][:], psum[:, 2:4, :], gates[:, n, :, :], ALU.mult).then_inc(row_free, 1)
            if n:
                merged_lo(n - 1)
            for j in range(4, 8):
                ahead(S_BRANCH + 8 * n + j)
            dve.wait_ge(mm_done, S_BRANCH + 8 * n + 8)
            dve.tensor_tensor(gates[:, 4 + n, :, :], psum[:, 0:2, :], gates[:, 4 + n, :, :], ALU.mult
                              ).then_inc(row_free, 1)
            dve.wait_ge(row_free, FREE + R_BRANCH + 2 * n + 2)
            dve.tensor_tensor(merged[n % 2][:], merged[n % 2][:], gates[:, 4 + n, :, :], ALU.add
                              ).then_inc(sem["merge_rows"], 1)
        merged_lo(3)

        def add_rows(dst, add=True):
            def evac(b, g, end, i, m):
                dve.wait_ge(mm_done, end + 8 * m * i)
                d = dst[:, :, bass.ds((b + m * i) * COLS, COLS)]
                if add:
                    dve.tensor_tensor(d, psum[:, 2 * (g % 2):2 * (g % 2) + 2, :], d, ALU.add).then_inc(row_free, 1)
                else:
                    dve.tensor_copy(d, psum[:, 2 * (g % 2):2 * (g % 2) + 2, :]).then_inc(row_free, 1)
            return evac

        dve.wait_ge(sem["xre_in"], 16)
        row_blocks(S_OUT1, R_OUT1, 4, 8, add_rows(x_rows))
        scaled_rows(1, x_rows)
        transposed_lo(ha, T_FFN1, "ffn1")

        def up1_stage(p, j, v, pair, i):
            count = 2 * pair + v + 1
            if j == 0:
                dve.wait_ge(sem["half_ok"], count)
                u = u_pad[v][:, :, 1:SEQ + 1]
                dve.tensor_tensor(u, psum[:, 4 * v:4 * v + 4, SEQ:2 * SEQ], u, ALU.add).then_inc(chan_free, 1)
            if j in (2, 3):
                if j == 2:
                    dve.wait_ge(sem["conv_mid"], count)
                else:
                    dve.wait_ge(sem["tap_done"], count)
                tap = 0 if j == 2 else 2
                for s in range(4):
                    w = Q_CONVW + 3 * (44 * v + 4 * pair + s) + tap
                    ins = dve.scalar_tensor_tensor(conv[v][:, s, :], u_pad[v][:, s, tap:tap + SEQ],
                                                   par[:, bass.ds(w, 1)], conv[v][:, s, :], ALU.mult, ALU.add)
                ins.then_inc(sem["tap_done" if j == 2 else "conv_done"], 1)
            if j == 4 and v == 1:
                dve.wait_ge(sem["conv_done"], count)
                dve.wait_ge(sem["silu_done"], pair + 1)
                dve.tensor_tensor(act_f[:], conv[0][:], conv[1][:], ALU.mult).then_inc(sem["act_ready"], 1)
            if j == 5 and v == 1:
                dve.wait_ge(sem["hb_hi"], pair + 1)
                h = hb[:, bass.ds(4 * i, 4), :, :]
                dve.tensor_tensor(h[:, :, 1, :], act_f[:], h[:, :, 0, :].bitcast(F32), ALU.subtract
                                  ).then_inc(sem["hb_lo"], 1)

        for p, (j0, n) in enumerate(UP1_PASSES):
            for j in range(8):
                ahead(S_UP1[p] + j)
            with dve.Fori(0, n - 1) as i:
                for j in range(8):
                    ahead(S_UP1[p] + 8 + j, i, 2)
                    up1_stage(p, j, 0, j0 + i, i)
                for j in range(8):
                    ahead(S_UP1[p] + 16 + j, i, 2)
                    up1_stage(p, j, 1, j0 + i, i)
            for j in range(8):
                ahead(S_UP1[p] + 16 * n - 8 + j)
                up1_stage(p, j, 0, j0 + n - 1, n - 1)

            def tail(j):
                for stage in range(8) if n == 4 else ([0], [1, 2], [3], [4, 5], [], [])[j]:
                    if n < 4 or stage == j:
                        up1_stage(p, stage, 1, j0 + n - 1, n - 1)

            row_blocks(S_DOWN1[p], R_DOWN1[p], 4, 2 * n, add_rows(x_rows), extra=tail)

        scaled_rows(2, x_rows)
        transposed_lo(ha, T_MIX2, "mix2")
        row_blocks(S_IN2, R_IN2, IN2_BLOCKS, 8, no_evac)
        dve.wait_ge(sem["wg_hi"], 1)
        dve.tensor_tensor(w_gate_l[:], w_gate[:], w_gate_h[:].bitcast(F32), ALU.subtract).then_inc(sem["wg_lo"], 1)
        dve.wait_ge(sem["t5_in"], 80)
        dve.wait_ge(sem["t5_mm"], 1)
        dve.tensor_tensor(t5_rows[:], psum[0:8, 7, :], t5_ahead[:], ALU.add).then_inc(sem["t5_rows_ok"], 1)
        dve.wait_ge(sem["cb_mm"], 1)
        for t in range(NT):
            ins = dve.tensor_tensor(cmp_bias[:, :, t, :],
                                    psum[:, 6, 120 * t:120 * t + 120].rearrange("p (n h) -> p h n", h=8),
                                    cmp_mask[:, t, :].unsqueeze(1).to_broadcast([P, 8, NCMP]), ALU.add)
        ins.then_inc(sem["cb_ok"], 1)
        dve.wait_ge(sem["kvt_ok"], 2)
        for s in range(2):
            for g in range(2):
                src = kv_cmp_t[:, 2 * s + g, :]
                win = bass.AP(src.tensor, src.offset, [list(src.ap[0]), [1, CMP_BLOCK], [CMP_STRIDE, NCMP]])
                pe_col = (Q_PEK, Q_PEV)[s]
                pe_in = par[:, pe_col:pe_col + CMP_BLOCK].unsqueeze(2).to_broadcast([P, CMP_BLOCK, NCMP])
                ins = dve.tensor_tensor(cmp_in[:, s, :, g, :], win, pe_in, ALU.add)
            ins.then_inc(sem["cin_ok"], 1)
        dve.wait_ge(sem["cs_mm"], 1)
        dve.wait_ge(sem["cb_ok"], 1)
        flat = cmp_s[:].rearrange("p h t n -> p (h t n)")
        chain.link(dve.scalar_tensor_tensor(flat, psum[:, 4, 0:240], SCALE,
                                            cmp_bias[:].rearrange("p h t n -> p (h t n)"), ALU.mult, ALU.add))
        r16 = cmp_s[:].rearrange("p h t n -> p (h t) n")
        m16 = cmp_m[:].rearrange("p h t -> p (h t)")
        n16 = cmp_n[:].rearrange("p h t -> p (h t)")
        chain.link(dve.reduce_max(m16, r16, AX.X))
        dve.tensor_tensor(r16, r16, m16.unsqueeze(2).to_broadcast([P, 16, NCMP]), ALU.subtract
                          ).then_inc(sem["cs_ok"], 1)
        dve.wait_ge(sem["cs_exp"], 1)
        dve.wait_ge(sem["gate_ok"], 1)
        p16 = cmp_p[:].rearrange("p h t n -> p (h t) n")
        chain.link(dve.reduce_sum(n16, p16, AX.X))
        chain.link(dve.reciprocal(n16, n16))
        chain.link(dve.tensor_tensor(cmp_n[:], cmp_n[:], gate24[:].rearrange("p t (h b) -> p h t b", b=3)[:, :, :, 0],
                                     ALU.mult))
        for t in range(NT):
            ins = dve.tensor_tensor(cmp_p[:, :, t, :], cmp_p[:, :, t, :],
                                    cmp_seen[:, t, :].unsqueeze(1).to_broadcast([P, 8, NCMP]), ALU.mult)
        chain.link(ins)
        dve.tensor_tensor(p16, p16, n16.unsqueeze(2).to_broadcast([P, 16, NCMP]), ALU.mult).then_inc(sem["cs_p"], 1)
        for s in range(8 * RET_BLOCKS):
            ahead(S_RET + s)
            head_stage(s % 4, N1 + s // 4, NH)
        for c in range(2):
            dve.wait_ge(sem["ot_hi"], 4 + c + 1)
            dve.tensor_tensor(ha[:, 4 * c:4 * c + 4, 1, :], mix_t[:, 4 * c:4 * c + 4, :],
                              ha[:, 4 * c:4 * c + 4, 0, :].bitcast(F32), ALU.subtract).then_inc(sem["ot_lo"], 1)
        dve.wait_ge(sem["rtab_in"], 48)
        dve.wait_ge(row_free, FREE + R_RET + RET_BLOCKS)
        for blk in range(4):
            for t in range(NT):
                x = ret[:, blk, t, :].rearrange("p (h d) -> p h d", h=2)
                x1, x2 = x[:, :, 0:HD], x[:, :, HD:2 * HD]
                c = cos2[:, t, :].unsqueeze(1).to_broadcast([P, 2, HD])
                s = sin2[:, t, :].unsqueeze(1).to_broadcast([P, 2, HD])
                dve.tensor_tensor(rt[0][:], x1, c, ALU.mult)
                dve.tensor_tensor(rt[1][:], x2, s, ALU.mult)
                dve.tensor_tensor(rt[2][:], x2, c, ALU.mult)
                chain.link(dve.tensor_tensor(rt[3][:], x1, s, ALU.mult))
                dve.tensor_tensor(x1, rt[0][:], rt[1][:], ALU.subtract)
                dve.tensor_tensor(x2, rt[2][:], rt[3][:], ALU.add).then_inc(sem["rope_ok"], 1)
                dve.wait_ge(sem["rope_ok"], 2 * blk + t + 1)
        for r in range(RET_HEADS):
            dve.wait_ge(sem["rs_mm"], r + 1)
            if r >= 2:
                dve.wait_ge(sem["ro_mm"], r - 1)
            dve.tensor_tensor(ret_p[r % 2][:], psum[:, 6, :].rearrange("p (a b) -> p a b", a=2), decay[:, r, :, :],
                              ALU.mult).then_inc(sem["rp_ok"], 1)
            dve.wait_ge(sem["ro_mm"], r + 1)
            for t in range(NT):
                ins = dve.bn_stats(bst[:, r % 2, t, :], psum[:, 7, RET_D * t:RET_D * t + RET_D])
            chain.link(ins)
            for t in range(NT):
                ins = dve.bn_aggr(bag[:, r % 2, t, :], bst[:, r % 2, t, :])
            ins.then_inc(sem["ro_stat"], 1)
            dve.wait_ge(sem["ro_rs"], r + 1)
            dve.wait_ge(sem["silu_g"], 1)
            o = [ret_o[:, t, RET_D * r:RET_D * r + RET_D] for t in range(NT)]
            for t in range(NT):
                ins = dve.tensor_scalar(o[t], psum[:, 7, RET_D * t:RET_D * t + RET_D], bag[:, r % 2, t, 0:1],
                                        grs[:, r % 2, t:t + 1], ALU.subtract, ALU.mult)
            chain.link(ins)
            for t in range(NT):
                ins = dve.tensor_tensor(o[t], o[t], ret[:, 6 + r // 2, t, RET_D * (r % 2):RET_D * (r % 2) + RET_D],
                                        ALU.mult)
            ins.then_inc(sem["ro_ok"], 1)
        for f in range(4):
            plain_lo(ha[:, 8 + 2 * f:10 + 2 * f], T_RETO + f)
        row_blocks(S_OUT2, R_OUT2, 4, 8, no_evac)

        def add_normed(n, loads):
            dve.wait_ge(sem["norm_rs"], n + 1)
            dve.wait_ge(sem["grow_in"], 16 * loads)
            for t in range(NT):
                chain.link(dve.scalar_tensor_tensor(rows[:, t, :], rows[:, t, :], rstd[:, 2 * n + t:2 * n + t + 1],
                                                    gain_row[:], ALU.mult, ALU.mult))
                dve.tensor_tensor(x_rows[:, t, :], x_rows[:, t, :], rows[:, t, :], ALU.add
                                  ).then_inc(sem["post_ok"], 1)

        add_normed(3, 1)
        scaled_rows(4, x_rows)
        transposed_lo(ha, T_MLP2, "mlp2")
        for p in range(UP2_PASSES):
            with dve.Fori(0, 2) as i:
                chain.enter(i, 0)
                for v in range(2):
                    for j in range(8):
                        ahead(S_UP2[p] + 8 * v + j, i, 2)
                    c = C_UP2[p] - C_UP2[0] + v
                    dve.wait_ge(sem["usum_done"], c + 1 + 2 * i)
                    dve.tensor_tensor(u_sum[:], psum[:, 4 * v:4 * v + 4, SEQ:2 * SEQ], u_sum[:], ALU.add
                                      ).then_inc(chan_free, 1)
                    dve.wait_ge(chan_free, FREE + C_UP2[p] + v + 1 + 2 * i)
                    dve.scalar_tensor_tensor(u_act[:], u_sum[:], 0.0, u_sum[:], ALU.max, ALU.mult
                                             ).then_inc(sem["act_ready"], 1)
                    dve.wait_ge(sem["hb_hi"], 11 + c + 1 + 2 * i)
                    d = hb[:, bass.ds(8 * i + 4 * v, 4), :, :]
                    dve.tensor_tensor(d[:, :, 1, :], u_act[:], d[:, :, 0, :].bitcast(F32), ALU.subtract
                                      ).then_inc(sem["hb_lo"], 1)
            chain.leave(2)
            row_blocks(S_DOWN2[p], R_DOWN2[p], 4, 8, add_rows(y_rows, p > 0), last=p == UP2_PASSES - 1)
        add_normed(5, 2)

    @block.tensor
    def _(pe):
        def rows_step(q, i, m, src, chunks, g, first, last):
            pe.wait_ge(lo_done, q + 1 + 8 * m * i)
            s = q % SPLIT_SLOTS
            for c in range(2):
                for t in range(NT):
                    acc = psum[:, 2 * (g % 2) + t, :]
                    hi = src[:, chunks[c], 0, t * P:(t + 1) * P]
                    lo = src[:, chunks[c], 1, t * P:(t + 1) * P]
                    pe.matmul(acc, hi, wh[s][:, c, :], start=first and c == 0, stop=False)
                    pe.matmul(acc, hi, wl[s][:, c, :], start=False, stop=False)
                    ins = pe.matmul(acc, lo, wh[s][:, c, :], start=False, stop=last and c == 1)
            ins.then_inc(mm_done, 1)

        def row_blocks(step0, g0, n, per, src, ready=None):
            def one(b, g, q0, i, m):
                pe.wait_ge(row_free, g + 1 + m * i)
                for j in range(per):
                    if ready:
                        ready(j)
                    rows_step(q0 + j, i, m, src, (2 * j, 2 * j + 1), g, j == 0, j == per - 1)
            if per != 8:
                for b in range(n):
                    one(b, g0 + b, step0 + per * b, 0, 0)
                return
            if n % 2:
                one(0, g0, step0, 0, 0)
            with pe.Fori(0, n // 2) as i:
                for b in (n % 2, n % 2 + 1):
                    one(b, g0 + b, step0 + 8 * b, i, 2)

        def channel_step(q, i, m, v, j):
            pe.wait_ge(lo_done, q + 1 + 8 * m * i)
            s = q % SPLIT_SLOTS
            for c in range(2):
                k = 2 * j + c
                both = ha[:, k, :, :].rearrange("p a b -> p (a b)")
                for d in range(4):
                    acc = psum[:, 4 * v + d, :]
                    hi, lo = (w[s][:, c, P * d:P * d + P] for w in (wh, wl))
                    if k < KC - 1:
                        pe.matmul(acc, hi, both, start=k == 0, stop=False)
                        ins = pe.matmul(acc[:, 0:SEQ], lo, ha[:, k, 0, :], start=False, stop=False)
                    else:
                        pe.matmul(acc[:, 0:SEQ], lo, ha[:, k, 0, :], start=False, stop=False)
                        ins = pe.matmul(acc, hi, both, start=False, stop=True)
            ins.then_inc(mm_done, 1)

        def transposes(F, src, done=None):
            if F >= 4:
                pe.wait_ge(sem["tr_lo"], F - 3)
            for c in range(2):
                for t in range(NT):
                    ins = pe.transpose(psum[:, 4 + F % 4, SEQ * c + P * t:SEQ * c + P * t + P], src(c, t), ident[:])
            ins.then_inc(sem["tr_full"], 1)

        def norm_transposes(n, fill0):
            rows_value = {0: 2, 1: 4, 2: 6, 4: 8}[n]
            pe.wait_ge(sem["norm_rows"], rows_value)
            for f in range(8):
                transposes(fill0 + f, lambda c, t: rows[:, t, (2 * f + c) * P:(2 * f + c + 1) * P])

        def split_by(fill0):
            return lambda j: pe.wait_ge(sem["tr_lo"], fill0 + j + 1)

        def head_stage(j, k, last):
            if j == 0 and k < last:
                n = k
                kind, h, x, (qb, qc), (kb, kc_), _ = heads[n]
                if kind == "band":
                    pe.wait_ge(sem["a_ready"], 6)
                if kind == "near":
                    pe.wait_ge(sem["bn_ok"], h + 1)
                if n:
                    pe.wait_ge(sem["at_qksb"], n)
                for i, (b, c) in enumerate(((qb, qc), (kb, kc_))):
                    for t in range(NT):
                        ins = pe.transpose(psum[:, QK_BANK, SEQ * i + P * t:SEQ * i + P * t + P],
                                           x[:, b, t, c:c + HD], ident[:])
                ins.then_inc(sem["at_qk"], 1)
            if j == 1 and k - 1 >= first[0]:
                n = k - 1
                pe.wait_ge(sem["at_pn"], n + 1)
                if n:
                    pe.wait_ge(sem["at_ptsb"], n)
                for kt in range(NT):
                    for t in range(NT):
                        ins = pe.transpose(psum[:, PT_BANK, SEQ * kt + P * t:SEQ * kt + P * t + P],
                                           prob[n % 2][:, t, P * kt:P * kt + P], ident[:])
                ins.then_inc(sem["at_pt"], 1)
            if j == 2 and k < last:
                n = k
                pe.wait_ge(sem["at_qksb"], n + 1)
                if n:
                    pe.wait_ge(sem["at_s"], n)
                for t in range(NT):
                    ins = pe.matmul(psum[:, SC_BANK, SEQ * t:SEQ * t + SEQ], qk_t[n % 2][:, 0, P * t:P * t + P],
                                    qk_t[n % 2][:, 1, :], start=True, stop=True)
                ins.then_inc(sem["at_sc"], 1)
            if j == 3 and k - 1 >= first[0]:
                n = k - 1
                kind, h, x, _, _, (vb, vc) = heads[n]
                pe.wait_ge(sem["at_ptsb"], n + 1)
                if outs_before(n):
                    pe.wait_ge(sem["at_osb"], outs_before(n))
                acc = psum[:, O_BANK, 0:SEQ]
                if kind == "slc":
                    pe.matmul(acc, cmp_v[:, h // 4, :], cmp_pt[:, h, :], start=True, stop=False)
                for kt in range(NT):
                    ins = pe.matmul(acc, x[:, vb, kt, vc:vc + HD], prob_t[n % 2][:, kt, :],
                                    start=kind in ("band", "near") and kt == 0, stop=kind != "slc" and kt == 1)
                ins.then_inc(sem["at_o"], 1)

        first = [0]

        pe.wait_ge(sem["ident_in"], 16)
        norm_transposes(0, T_MIX1)
        row_blocks(S_IN1, R_IN1, IN1_BLOCKS, 8, ha, split_by(T_MIX1))
        for s in range(8 * GATE_BLOCKS):
            b, j = s // 8, s % 8
            g = R_GATE + b
            if j == 0:
                pe.wait_ge(row_free, g + 1)
            rows_step(S_GATE + s, 0, 0, ha, (2 * j, 2 * j + 1), g, j == 0, j == 7)
            head_stage(s % 4, s // 4, N1)
        for j in range(4):
            head_stage(j, N1, N1)
        pe.wait_ge(sem["at_osb"], N1)
        for n in range(4):
            for br in range(2):
                g = R_BRANCH + 2 * n + br
                pe.wait_ge(row_free, g + 1)
                for j in range(4):
                    if n == 0:
                        pe.wait_ge(sem["ot_lo"], 2 * br + j // 2 + 1)
                    rows_step(S_BRANCH + 8 * n + 4 * br + j, 0, 0, ha, (8 * br + 2 * j, 8 * br + 2 * j + 1), g,
                              j == 0, j == 3)
                if br == 0 and n:
                    pe.wait_ge(sem["merge_rows"], n)
                    for f in range(2):
                        transposes(T_MERGE + 2 * (n - 1) + f,
                                   lambda c, t: merged[(n - 1) % 2][:, t, (2 * f + c) * P:(2 * f + c + 1) * P])
        pe.wait_ge(sem["merge_rows"], 4)
        for f in range(2):
            transposes(T_MERGE + 6 + f, lambda c, t: merged[1][:, t, (2 * f + c) * P:(2 * f + c + 1) * P])
        row_blocks(S_OUT1, R_OUT1, 4, 8, hb, split_by(T_MERGE))
        norm_transposes(1, T_FFN1)

        def channel_blocks(step0, c0, n, ready, rows_before):
            pe.wait_ge(row_free, FREE + rows_before)
            with pe.Fori(0, n) as i:
                for v in range(2):
                    pe.wait_ge(chan_free, FREE + c0 + v - 1 + 2 * i)
                    for j in range(8):
                        if v == 0:
                            ready(j)
                        channel_step(step0 + 8 * v + j, i, 2, v, j)

        def hb_by(base, per_count):
            return lambda j: pe.wait_ge(sem["hb_lo"], base + (2 * j + 1) // 4 + 1)

        rows_before = R_DOWN1[0]
        for p, (j0, n) in enumerate(UP1_PASSES):
            pe.wait_ge(sem["tr_lo"], T_FFN1 + 8)
            channel_blocks(S_UP1[p], C_UP1[p], n, split_by(T_FFN1), rows_before)
            pe.wait_ge(chan_free, FREE + C_UP1[p] + 2 * n - 1)
            row_blocks(S_DOWN1[p], R_DOWN1[p], 4, 2 * n, hb, hb_by(j0, 4))
            rows_before = R_DOWN1[p] + 4

        norm_transposes(2, T_MIX2)
        row_blocks(S_IN2, R_IN2, IN2_BLOCKS, 8, ha, split_by(T_MIX2))
        pe.wait_ge(sem["tr_lo"], T_MIX2 + 8)
        pe.wait_ge(sem["wg_lo"], 1)
        for t in range(NT):
            acc = psum[:, 6, N_GATES * t:N_GATES * t + N_GATES]
            for k in range(KC):
                hi, lo = (ha[:, k, x, t * P:(t + 1) * P] for x in range(2))
                pe.matmul(acc, hi, w_gate_h[:, k, :], start=k == 0, stop=False)
                pe.matmul(acc, hi, w_gate_l[:, k, :], start=False, stop=False)
                ins = pe.matmul(acc, lo, w_gate_h[:, k, :], start=False, stop=k == KC - 1)
        ins.then_inc(sem["gate_mm"], 1)
        pe.wait_ge(sem["t5_in"], 80)
        pe.matmul(psum[0:8, 7, :], t5_tab[:], t5_up[:], start=True, stop=True).then_inc(sem["t5_mm"], 1)
        pe.wait_ge(row_free, FREE + R_IN2 + IN2_BLOCKS)
        for f in range(2):
            for c in range(2):
                for t in range(NT):
                    col = (2 * f + c) * HD
                    ins = pe.transpose(psum[:, 4 + f, SEQ * c + P * t:SEQ * c + P * t + P],
                                       proj2[:, 2, t, col:col + HD], ident[:])
            ins.then_inc(sem["kvt_mm"], 1)
        for f in range(4):
            if f == 0:
                pe.wait_ge(sem["gate_ok"], 1)
            elif f == 1:
                pe.wait_ge(sem["t5_rows_ok"], 1)
            else:
                pe.wait_ge(sem["kvt_ok"], f - 1)
            for c in range(2):
                for t in range(NT):
                    h = 2 * f + c
                    ins = pe.transpose(psum[:, 4 + (f + 2) % 4, SEQ * c + P * t:SEQ * c + P * t + P],
                                       proj2[:, h // 4, t, h % 4 * HD:h % 4 * HD + HD], ident[:])
            ins.then_inc(sem["qall_mm"], 1)
        pe.wait_ge(sem["qall_ok"], 1)
        for t in range(NT):
            for n in range(NCMP):
                off = 256 + P * t - CMP_STRIDE * n - (CMP_BLOCK - 1)
                ins = pe.matmul(psum[:, 6, 120 * t + 8 * n:120 * t + 8 * n + 8], t5_up[:, off:off + P], t5_tab[:],
                                start=True, stop=True)
        ins.then_inc(sem["cb_mm"], 1)
        pe.wait_ge(sem["w1_in"], 32)
        pe.wait_ge(sem["w2_in"], 32)
        for s in range(2):
            pe.wait_ge(sem["qall_ok"], 3 + s)
            pe.wait_ge(sem["cin_ok"], s + 1)
            for l in range(CMP_BLOCK):
                ins = pe.matmul(psum[:, 4 + s, 0:2 * NCMP], w1[:, s, l, :],
                                cmp_in[:, s, l, :, :].rearrange("p g n -> p (g n)"),
                                start=l == 0, stop=l == CMP_BLOCK - 1)
            ins.then_inc(sem["hid_mm"], 1)
        pe.wait_ge(sem["hid_ok"], 1)
        pe.wait_ge(sem["cb_ok"], 1)
        pe.matmul(psum[:, 6, 0:2 * NCMP], w2[:, 0, :], cmp_hid[:, 0, :, :].rearrange("p g n -> p (g n)"),
                  start=True, stop=True).then_inc(sem["kv_mm"], 1)
        pe.wait_ge(sem["hid_ok"], 2)
        for g in range(2):
            ins = pe.matmul(psum[0:NCMP, 7, HD * g:HD * g + HD], cmp_hid[:, 1, g, :], w2[:, 1, :],
                            start=True, stop=True)
        ins.then_inc(sem["kv_mm"], 1)
        pe.wait_ge(sem["kv_ok"], 1)
        for h in range(8):
            for t in range(NT):
                c = (h * NT + t) * NCMP
                ins = pe.matmul(psum[:, 4, c:c + NCMP], q_all[:, h, P * t:P * t + P], cmp_k[:, h // 4, :],
                                start=True, stop=True)
        ins.then_inc(sem["cs_mm"], 1)
        pe.wait_ge(sem["cs_p"], 1)
        pe.wait_ge(sem["kv_ok"], 2)
        for f in range(4):
            for c in range(2):
                for t in range(NT):
                    ins = pe.transpose(psum[0:NCMP, 4 + f, SEQ * c + P * t:SEQ * c + P * t + P],
                                       cmp_p[:, 2 * f + c, t, :], ident[:])
            ins.then_inc(sem["cpt_mm"], 1)
        pe.wait_ge(sem["cpt_ok"], 4)
        first[0] = N1
        for s in range(8 * RET_BLOCKS):
            b, j = s // 8, s % 8
            g = R_RET + b
            if j == 0:
                pe.wait_ge(row_free, g + 1)
            rows_step(S_RET + s, 0, 0, ha, (2 * j, 2 * j + 1), g, j == 0, j == 7)
            head_stage(s % 4, N1 + s // 4, NH)
        for j in range(4):
            head_stage(j, NH, NH)
        pe.wait_ge(sem["at_osb"], outs_before(NH))

        def ret_transposes(r):
            for i, (mm, ok) in enumerate((("rq_mm", "rq_ok"), ("rk_mm", "rk_ok"))):
                pe.wait_ge(sem["rope_ok"], 4 * i + 2 * (r // 2) + 2)
                if r:
                    pe.wait_ge(sem[ok], r)
                for c in range(2):
                    for t in range(NT):
                        col = RET_D * (r % 2) + P * c
                        ins = pe.transpose(psum[:, 4 + i, SEQ * c + P * t:SEQ * c + P * t + P],
                                           ret[:, 2 * i + r // 2, t, col:col + P], ident[:])
                ins.then_inc(sem[mm], 1)

        ret_transposes(0)
        for r in range(RET_HEADS):
            pe.wait_ge(sem["rk_ok"], r + 1)
            pe.wait_ge(sem["rq_ok"], r + 1)
            if r:
                pe.wait_ge(sem["rp_ok"], r)
            for kt in range(NT):
                for c in range(2):
                    ins = pe.matmul(psum[:, 6, SEQ * kt:SEQ * kt + SEQ], ret_k[r % 2][:, c, P * kt:P * kt + P],
                                    ret_q[r % 2][:, c, :], start=c == 0, stop=c == 1)
            ins.then_inc(sem["rs_mm"], 1)
            if r + 1 < RET_HEADS:
                ret_transposes(r + 1)
            pe.wait_ge(sem["rp_ok"], r + 1)
            if r:
                pe.wait_ge(sem["ro_ok"], r)
            for t in range(NT):
                for kt in range(NT):
                    ins = pe.matmul(psum[:, 7, RET_D * t:RET_D * t + RET_D], ret_p[r % 2][:, kt, P * t:P * t + P],
                                    ret[:, 4 + r // 2, kt, RET_D * (r % 2):RET_D * (r % 2) + RET_D],
                                    start=kt == 0, stop=kt == 1)
            ins.then_inc(sem["ro_mm"], 1)
        pe.wait_ge(sem["ro_ok"], RET_HEADS)
        for f in range(4):
            transposes(T_RETO + f, lambda c, t: ret_o[:, t, (2 * f + c) * P:(2 * f + c + 1) * P])

        def mix_ready(j):
            if j < 4:
                pe.wait_ge(sem["ot_lo"], 4 + j // 2 + 1)
            else:
                pe.wait_ge(sem["tr_lo"], T_RETO + j - 4 + 1)

        row_blocks(S_OUT2, R_OUT2, 4, 8, ha, mix_ready)
        norm_transposes(4, T_MLP2)
        rows_before = R_OUT2 + 4
        pe.wait_ge(sem["tr_lo"], T_MLP2 + 8)
        for p in range(UP2_PASSES):
            channel_blocks(S_UP2[p], C_UP2[p], 2, split_by(T_MLP2), rows_before)
            pe.wait_ge(chan_free, FREE + C_UP2[p] + 3)
            row_blocks(S_DOWN2[p], R_DOWN2[p], 4, 8, hb, hb_by(11 + 4 * p, 4))
            rows_before = R_DOWN2[p] + 4

    block.__exit__(None, None, None)


CONST_SHAPES = shape_constants()
DRAM_INPUTS = ["x", "w_in", "a_q_norm", "a_k_norm", "a_sink", "b_rpb", "w_branch_a", "w_branch_b", "w_out", "w_up",
               "w_down", "w_in_2", "cmp_w1_k_2", "cmp_w2_k_2", "cmp_w1_v_2", "cmp_w2_v_2", "t5_bias_2", "w_out_2",
               "norm_mix_post_2", "w_up_2", "w_down_2", "norm_mlp_post_2"]


def kernel(**inputs):
    import concourse.bacc as bacc
    from concourse.bass_utils import run_bass_kernel_spmd

    nc = bacc.Bacc("TRN2", target_bir_lowering=False, num_devices=1, dynamic_dma_scratch_size=1024)
    arrays = {n: np.ascontiguousarray(inputs[n]) for n in DRAM_INPUTS}
    arrays["b_rpb"] = np.ascontiguousarray(arrays["b_rpb"][:, :, ::-1, ::-1])
    arrays.update(CONST_SHAPES)
    arrays["params"] = pack_columns(inputs)
    aps = {n: nc.dram_tensor(f"in_{n}", v.shape, mybir.dt.from_np(v.dtype), kind="ExternalInput").ap()
           for n, v in arrays.items()}
    out = nc.dram_tensor("out", (1, SEQ, D), F32, kind="ExternalOutput").ap()
    scratch = nc.dram_tensor("distance_rows", (8, 512), F32, kind="Internal").ap()
    build(nc, aps, out, scratch)
    r = run_bass_kernel_spmd(nc, [{f"in_{n}": v for n, v in arrays.items()}], core_ids=[0])
    return r.results[0]["out"]
```

```python
import math

import numpy as np

import concourse.bass as bass
from concourse import mybir

F32 = mybir.dt.float32
F32R = mybir.dt.float32r
ACT = mybir.ActivationFunctionType
ALU = mybir.AluOpType
AX = mybir.AxisListType

P = 128
SEQ = 256
NT = SEQ // P
D = 2048
KC = D // P
DFF1 = 5632
DFF2 = 8192
EPS = 1e-6
NEG = -1e30
HD = 128
SCALE = 1.0 / math.sqrt(HD)
COLS = 512
RAW_SLOTS = 4
SPLIT_SLOTS = 4
AHEAD = 3

IN1_BLOCKS = 9
GATE_BLOCKS = 8
IN2_BLOCKS = 5
IN2_ORDER = [2, 0, 1, 3, 4]
RET_BLOCKS = 8
N_GATES = 24
RET_HEADS, RET_D = 4, 256
NCMP, CMP_BLOCK, CMP_STRIDE = 15, 32, 16
UP1_PASSES = [(0, 4), (4, 4), (8, 3)]
UP2_PASSES = 4
T5_BUCKETS = 32

S_IN1 = 0
S_GATE = S_IN1 + 8 * IN1_BLOCKS
S_BRANCH = S_GATE + 8 * GATE_BLOCKS
S_OUT1 = S_BRANCH + 8 * 4
S_FF1 = S_OUT1 + 8 * 4
S_UP1, S_DOWN1 = [], []
_s = S_FF1
for _, _n in UP1_PASSES:
    S_UP1.append(_s)
    _s += 16 * _n
    S_DOWN1.append(_s)
    _s += 8 * _n
S_IN2 = _s
S_RET = S_IN2 + 8 * IN2_BLOCKS
S_OUT2 = S_RET + 8 * RET_BLOCKS
S_UP2, S_DOWN2 = [], []
_s = S_OUT2 + 8 * 4
for _ in range(UP2_PASSES):
    S_UP2.append(_s)
    S_DOWN2.append(_s + 32)
    _s += 64
N_STEPS = _s

R_IN1 = 0
R_GATE = R_IN1 + IN1_BLOCKS
R_BRANCH = R_GATE + GATE_BLOCKS
R_OUT1 = R_BRANCH + 8
R_DOWN1 = [R_OUT1 + 4 + 4 * i for i in range(3)]
R_IN2 = R_DOWN1[-1] + 4
R_RET = R_IN2 + IN2_BLOCKS
R_OUT2 = R_RET + RET_BLOCKS
R_DOWN2 = [R_OUT2 + 4 + 4 * i for i in range(UP2_PASSES)]
C_UP1 = [0, 8, 16]
C_UP2 = [22 + 4 * i for i in range(UP2_PASSES)]

T_MIX1, T_MERGE, T_FFN1, T_MIX2, T_RETO, T_MLP2 = 0, 8, 16, 24, 32, 36

Q_GAIN = {"mix1": 0, "ffn1": 16, "mix2": 32, "mlp2": 48}
Q_BQ, Q_BK = 64, 65
Q_CONVW = 66
Q_CONVB = Q_CONVW + 3 * 88
Q_B1K = Q_CONVB + 88
Q_B1V = Q_B1K + 1
Q_PEK = Q_B1V + 1
Q_PEV = Q_PEK + CMP_BLOCK
Q_COLS = Q_PEV + CMP_BLOCK

FREE = 2

KB = 1024


class Chain:

    def __init__(self, eng, sem):
        self.eng, self.sem, self.n, self.past = eng, sem, 0, 0

    def enter(self, i, links):
        self.past, self.start, self.links = i * links, self.n, links

    def leave(self, passes):
        assert self.n - self.start == self.links, (self.n - self.start, self.links)
        self.n, self.past = self.start + self.links * passes, 0

    def link(self, ins):
        self.n += 1
        ins.then_inc(self.sem, 1)
        self.eng.wait_ge(self.sem, self.past + self.n)


def shape_constants():
    f = np.float32
    q = np.arange(SEQ)
    k = np.arange(SEQ)
    c = {}
    c["ident"] = np.eye(P, dtype=f)

    def tiles(m):
        return np.ascontiguousarray(m.reshape(NT, P, -1).transpose(1, 0, 2))

    band = np.where(np.abs(q[:, None] - k[None, :]) <= 128, 0.0, NEG).astype(f)
    c["band"] = tiles(band)
    qc, kc = q % 64, k % 64
    cs = np.clip(qc - 8, 0, 48)
    near = (kc[None, :] >= cs[:, None]) & (kc[None, :] < cs[:, None] + 16)
    c["near"] = np.ascontiguousarray(tiles(np.where(near, 0.0, NEG).astype(f))[:, ::-1, ::-1])

    def rope(half):
        inv = f(10000.0) ** (-np.arange(half, dtype=f) * f(1.0 / half))
        ang = (q.astype(f)[:, None] * inv[None, :].astype(f)).astype(f)
        return tiles(np.cos(ang).astype(f)), tiles(np.sin(ang).astype(f))

    c["cos1"], c["sin1"] = rope(64)
    c["cos2"], c["sin2"] = rope(128)
    def bucket(rel):
        n = np.maximum(rel, 0)
        nf = np.maximum(n, 1).astype(f)
        large = 16 + (np.log(nf / f(16)) / np.log(128 / 16) * 16).astype(np.int32)
        return np.where(n < 16, n, np.minimum(large, 31))

    up = np.arange(-256, 256)
    c["t5_up"] = (bucket(up)[None, :] == np.arange(32)[:, None]).astype(f)
    c["t5_ahead"] = np.broadcast_to(np.where(up >= 0, 0.0, NEG).astype(f), (8, 512)).copy()
    n = np.arange(NCMP)
    ok = (q[:, None] - (n * CMP_STRIDE + CMP_BLOCK - 1)[None, :]) >= 0
    c["cmp_mask"] = tiles(np.where(ok, 0.0, NEG).astype(f))
    c["cmp_seen"] = tiles(ok.astype(f))
    lg = np.log(1.0 - 2.0 ** (-5.0 - np.arange(RET_HEADS)))
    diff = (q[None, :] - k[:, None]).astype(np.float64)
    decay = np.where(diff >= 0, np.exp(np.maximum(diff, 0)[None] * lg[:, None, None]), 0.0)
    decay = decay * RET_D ** -0.5
    c["decay"] = np.ascontiguousarray(
        decay.reshape(RET_HEADS, NT, P, SEQ).transpose(2, 0, 1, 3)).astype(f)
    return c


CONST_NAMES = ["ident", "band", "near", "cos1", "sin1", "cos2", "sin2", "t5_up", "t5_ahead",
               "cmp_mask", "cmp_seen", "decay"]


def pack_columns(a):
    def cols(v):
        return np.asarray(v).reshape(-1, P).T

    conv = np.asarray(a["conv_w"])[0].reshape(3, 88, P).transpose(2, 1, 0).reshape(P, 88 * 3)
    parts = [cols(a["norm_mix"]), cols(a["norm_ffn"]), cols(a["norm_mix_pre_2"]), cols(a["norm_mlp_pre_2"]),
             cols(a["b_q_norm"]), cols(a["b_k_norm"]), conv, cols(a["conv_b"]),
             cols(a["cmp_b1_k_2"]), cols(a["cmp_b1_v_2"]),
             np.asarray(a["cmp_pe_k_2"])[0].T, np.asarray(a["cmp_pe_v_2"])[0].T]
    return np.ascontiguousarray(np.concatenate(parts, axis=1))


def build(nc, a, out, scratch, scratch_cols):
    def dram(name):
        return a[name]

    base = (nc.sbuf_base + 1023) // 1024 * 1024

    def at(name, shape, kb, dt=F32):
        return nc.alloc_sbuf_tensor_at(name, shape, dt, offset=int(base + kb * KB))

    x_rows = at("x_rows", [P, NT, D], 0)
    ot = at("ot", [P, KC, SEQ], 0)
    raw = [at(f"raw{i}", [P, 4, COLS], 16 + 8 * i) for i in range(RAW_SLOTS)]
    wh = [at(f"wh{i}", [P, 2, COLS], 48 + 4 * i, F32R) for i in range(SPLIT_SLOTS)]
    wl = [at(f"wl{i}", [P, 2, COLS], 64 + 4 * i, F32R) for i in range(SPLIT_SLOTS)]
    ha = at("ha", [P, KC, 2, SEQ], 80, F32R)
    hb = at("hb", [P, KC, 2, SEQ], 112, F32R)
    proj = at("proj", [P, IN1_BLOCKS, NT, COLS], 112)
    gates = at("gates", [P, GATE_BLOCKS, NT, COLS], 148)
    rot_a = at("rot_a", [P, 2, NT, HD], 180)
    rot_b = at("rot_b", [P, 2, NT, HD], 182)
    cos1 = at("cos1", [P, NT, 64], 184)
    sin1 = at("sin1", [P, NT, 64], 184.5)
    a_gain = at("a_gain", [P, 2, HD], 185)
    band = at("band", [P, NT, SEQ], 186)
    near = at("near", [P, NT, SEQ], 188)
    merged = [at(f"merged{i}", [P, NT, COLS], 180 + 4 * i) for i in range(2)]
    bias = [at(f"bias{i}", [P, NT, SEQ], 190 + 2 * i) for i in range(2)]
    qk_t = [at(f"qk_t{i}", [P, 2, SEQ], 194 + 2 * i) for i in range(2)]
    sco = [at(f"sco{i}", [P, NT, SEQ], 198 + 2 * i) for i in range(2)]
    prob = [at(f"prob{i}", [P, NT, SEQ], 202 + 2 * i) for i in range(2)]
    prob_t = [at(f"prob_t{i}", [P, NT, SEQ], 206 + 2 * i) for i in range(2)]
    tmp_a = at("tmp_a", [P, 4, HD], 210)
    tmp_b = at("tmp_b", [P, 4, HD], 212)
    rows = at("rows", [P, NT, D], 148)
    u_pad = [at(f"u_pad{i}", [P, 4, SEQ + 2], 164 + 4.25 * i) for i in range(2)]
    conv = [at(f"conv{i}", [P, 4, SEQ], 173 + 4 * i) for i in range(2)]
    act_f = at("act_f", [P, 4, SEQ], 181)
    u_sum = at("u_sum", [P, 4, SEQ], 164)
    u_act = at("u_act", [P, 4, SEQ], 168)
    y_rows = rows
    gain_row = at("gain_row", [P, D], 184)
    proj2 = at("proj2", [P, IN2_BLOCKS, NT, COLS], 148)
    ret = at("ret", [P, RET_BLOCKS, NT, COLS], 112)
    w1 = at("w1", [P, 2, CMP_BLOCK, HD], 112)
    w_gate = at("w_gate", [P, KC, N_GATES], 144)
    w_gate_h = at("w_gate_h", [P, KC, N_GATES], 145.5, F32R)
    w_gate_l = at("w_gate_l", [P, KC, N_GATES], 186, F32R)
    mix_t = at("mix_t", [P, 8, SEQ], 168)
    w2 = at("w2", [P, 2, HD], 176)
    cmp_bias = at("cmp_bias", [P, 8, NT, NCMP], 177)
    cmp_mask = at("cmp_mask", [P, NT, NCMP], 178)
    cmp_seen = at("cmp_seen", [P, NT, NCMP], 178.25)
    t5_tab = at("t5_tab", [T5_BUCKETS, 8], 178.5)
    gate24 = at("gate24", [P, NT, N_GATES], 178.75)
    kv_cmp_t = at("kv_cmp_t", [P, 4, SEQ], 180)
    cmp_in = at("cmp_in", [P, 2, CMP_BLOCK, 2, NCMP], 198)
    cmp_hid = at("cmp_hid", [P, 2, 2, NCMP], 184)
    hid_t = at("hid_t", [2 * NCMP, 2, HD], 147)
    gate_t = at("gate_t", [N_GATES, SEQ], 189)
    t5_cols = at("t5_cols", [P, 4, 8], 179.75)
    cmp_dist = at("cmp_dist", [P, 23, 8], 179)
    cmp_k = at("cmp_k", [P, 2, NCMP], 185.5)
    cmp_v = at("cmp_v", [NCMP, 2, HD], 188)
    q_all = [at(f"q_all{i}", [P, 4, SEQ], kb) for i, kb in enumerate((156, 210))]
    k_all = at("k_all", [P, 4, SEQ], 194)
    t5_up = at("t5_up", [T5_BUCKETS, 512], 190)
    t5_ahead = at("t5_ahead", [8, 512], 194)
    t5_rows = at("t5_rows", [8, 512], 196)
    cmp_s = at("cmp_s", [P, 8, NT, NCMP], 144)
    cmp_p = at("cmp_p", [P, 8, NT, NCMP], 145)
    cmp_m = at("cmp_m", [P, 8, NT], 146)
    cmp_n = at("cmp_n", [P, 8, NT], 146.25)
    cmp_pt = at("cmp_pt", [NCMP, 8, SEQ], 180)
    cos2 = at("cos2", [P, NT, HD], 180)
    sin2 = at("sin2", [P, NT, HD], 181)
    decay = at("decay", [P, RET_HEADS, NT, SEQ], 184)
    ret_q = [at(f"ret_q{i}", [P, 2, SEQ], 192 + 2 * i) for i in range(2)]
    ret_k = [at(f"ret_k{i}", [P, 2, SEQ], 196 + 2 * i) for i in range(2)]
    ret_p = [at(f"ret_p{i}", [P, NT, SEQ], 200 + 2 * i) for i in range(2)]
    rt = [at(f"rt{i}", [P, 2, HD], 204 + i) for i in range(4)]
    ret_o = at("ret_o", [P, NT, 1024], 148)
    small = 214
    ident = at("ident", [P, P], small)
    par = at("par", [P, Q_COLS], small + 0.5)
    sums = at("sums", [P, 16], small + 2.5)
    rstd = at("rstd", [P, 16], small + 2.5625)
    neghalf = at("neghalf", [P, 32], small + 2.625)
    ssq = at("ssq", [P, 32], small + 2.75)
    rsq = at("rsq", [P, 32], small + 2.875)
    sink = at("sink", [P, 8], small + 3)
    mx = at("mx", [P, 2, NT], small + 3.0625)
    nmx = at("nmx", [P, 2, NT], small + 3.09375)
    den = at("den", [P, 2, NT], small + 3.125)
    esink = at("esink", [P, 2, NT], small + 3.15625)
    rden = at("rden", [P, 2, NT], small + 3.1875)
    bst = at("bst", [P, 2, NT, 6], small + 3.25)
    bag = at("bag", [P, 2, NT, 2], small + 3.375)
    grs = at("grs", [P, 2, NT], small + 3.40625)
    ssb = at("ssb", [P, 2, 4], small + 3.4375)
    junk = at("junk", [P, NT, D], 112)
    unused = at("unused", [P, 4], small + 3.5625)
    rsb = at("rsb", [P, 2, 4], small + 3.5)


    psum = nc.alloc_psum_tensor("psum", [P, 8, COLS], F32)

    names = """
      x_in par_in ident_in cos1_in sin1_in again_in band_in near_in sink_in xre_in
      hi_done lo_done mm_done row_free chan_free
      act_chain dve_chain pool_chain pe_chain consts_set
      norm_ss norm_rs norm_rows tr_full tr_hi tr_lo
      an_ss an_rs a_ready bn_ss bn_rs bn_ok
      bias_ok at_qk at_qksb at_sc at_s at_nm at_p at_pn at_pt at_ptsb at_o at_osb
      sig_done merge_rows ot_hi ot_lo x_ready
      half_ok tap_done conv_mid conv_done silu_done act_ready hb_hi hb_lo usum_done
      row_done
      wg_in wg_hi wg_lo gate_mm gate_half gate_sum gate_tr gate_ok
      t5_in t5_mm t5_rows_ok t5_cols_ok t5_st cmp_dist_in cb_ok hid_copied hid_tr kall_mm kall_ok
      kvt_mm kvt_ok qall_mm qall_ok cin_ok w2_in hid_mm hid_ok kv_mm kv_ok
      cs_mm cs_ok cs_exp cs_p cpt_mm cpt_ok
      rtab_in rope_ok silu_g rq_mm rq_ok rk_mm rk_ok rs_mm rp_ok ro_mm ro_stat ro_rs ro_ok
      post_ss post_rs post_ok grow_in out_in y_rows_ok cmask_in sync_bank
    """.split()
    sem = {n: nc.alloc_semaphore(n) for n in names}
    raw_in = [nc.alloc_semaphore(f"raw_in{i}") for i in range(RAW_SLOTS)]
    bias_in = [nc.alloc_semaphore(f"bias_in{i}") for i in range(2)]
    t5_bias_in = [nc.alloc_semaphore(f"t5_bias_in{i}") for i in range(2)]

    w1_in = [nc.alloc_semaphore(f"w1_in{i}") for i in range(2)]

    (hi_done, lo_done, mm_done, row_free, chan_free) = (
        sem[n] for n in ("hi_done", "lo_done", "mm_done", "row_free", "chan_free"))

    heads = []
    for h in range(8):
        heads.append(("band", h, proj, (h // 4, h % 4 * HD), (2, h // 4 * HD), (2, 256 + h // 4 * HD)))
    for h in range(8):
        heads.append(("near", h, proj, (3 + h // 4, h % 4 * HD), (5 + h // 4, h % 4 * HD),
                      (7 + h // 4, h % 4 * HD)))
    for h in range(8):
        for b, blk in (("slc", 3), ("win", 4)):
            heads.append((b, h, proj2, (h // 4, h % 4 * HD), (blk, h // 4 * HD), (blk, 256 + h // 4 * HD)))
    N1, NH = 16, len(heads)

    def outs_before(n):
        return n if n <= N1 else N1 + (n - N1) // 2

    QK_BANK, SC_BANK, PT_BANK, O_BANK = 4, 5, 6, 7

    block = nc.Block()
    block.__enter__()

    @block.sync
    def _(sp):
        def view(name):
            return a[name].rearrange("o (k p) n -> p (o k) n", p=P)

        def weight_load(u, i, src):
            if u >= RAW_SLOTS:
                sp.wait_ge(lo_done, 2 * (u - RAW_SLOTS) + 2 + 8 * i)
            sp.dma_start(raw[u % RAW_SLOTS][:], src).then_inc(raw_in[u % RAW_SLOTS], 16)

        def column_blocks(step, name, k0, groups, col, n):
            w = view(name)
            if groups == 4:
                with sp.Fori(0, n) as i:
                    for j in range(4):
                        weight_load(step // 2 + j, i, w[:, k0 + 4 * j:k0 + 4 * j + 4,
                                                        bass.ds(i * COLS + col, COLS)])
            else:
                for b in range(n):
                    for j in range(groups):
                        weight_load(step // 2 + groups * b + j, 0,
                                    w[:, k0 + 4 * j:k0 + 4 * j + 4, col + b * COLS:col + (b + 1) * COLS])

        sp.dma_start(x_rows[:], a["x"].rearrange("o (t p) n -> p (o t) n", p=P)).then_inc(sem["x_in"], 16)
        sp.dma_start(ident[:], a["ident"]).then_inc(sem["ident_in"], 16)
        sp.dma_start(par[:], a["params"]).then_inc(sem["par_in"], 16)
        w_in = view("w_in")
        for j in range(4):
            weight_load(j, 0, w_in[:, 4 * j:4 * j + 4, 0:COLS])
        for i, g in enumerate(("a_q_norm", "a_k_norm")):
            sp.dma_start(a_gain[:, i, :], a[g].partition_broadcast(P) if False else
                         bass.AP(a[g].tensor, 0, [[0, P], [1, HD]])).then_inc(sem["again_in"], 16)
        sp.dma_start(cos1[:], a["cos1"]).then_inc(sem["cos1_in"], 16)
        sp.dma_start(sin1[:], a["sin1"]).then_inc(sem["sin1_in"], 16)
        sp.dma_start(band[:], a["band"]).then_inc(sem["band_in"], 16)
        sp.dma_start(near[:], a["near"]).then_inc(sem["near_in"], 16)
        sp.dma_start(sink[:], bass.AP(a["a_sink"].tensor, 0, [[0, P], [1, 8]])).then_inc(sem["sink_in"], 16)

        def near_bias(h):
            if h >= 2:
                sp.wait_ge(sem["at_s"], 8 + h - 2 + 1)
            for t in range(NT):
                for r in range(2):
                    off = h * 15 * 31 + (4 + 2 * t + r) * 31 - 48
                    src = bass.AP(a["b_rpb"].tensor, off, [[1, 64], [31, 4], [1, 64]])
                    sp.dma_start(bias[h % 2][64 * r:64 * r + 64, 1 - t, :].rearrange("p (a c) -> p a c", a=4),
                                 src).then_inc(bias_in[h % 2], 16)

        near_bias(0)
        near_bias(1)
        column_blocks(8, "w_in", 0, 4, COLS, IN1_BLOCKS - 1)
        for u in range(4 * GATE_BLOCKS):
            b, j = u // 4, u % 4
            if u >= 2 * 8 + 7 and (u - 23) % 2 == 0 and (u - 23) // 2 + 2 < 8:
                near_bias((u - 23) // 2 + 2)
            weight_load(S_GATE // 2 + u, 0, w_in[:, 4 * j:4 * j + 4,
                                                 (IN1_BLOCKS + b) * COLS:(IN1_BLOCKS + b + 1) * COLS])
        near_bias(7)
        wa, wb = view("w_branch_a"), view("w_branch_b")
        with sp.Fori(0, 4) as i:
            for j in range(4):
                w = (wa, wb)[j // 2]
                weight_load(S_BRANCH // 2 + j, i, w[:, 4 * (j % 2):4 * (j % 2) + 4, bass.ds(i * COLS, COLS)])
        sp.wait_ge(sem["ot_lo"], 4)
        sp.dma_start(x_rows[:], a["x"].rearrange("o (t p) n -> p (o t) n", p=P)).then_inc(sem["xre_in"], 16)
        column_blocks(S_OUT1, "w_out", 0, 4, 0, 4)
        wu = view("w_up")
        for (j0, n), su, sd in zip(UP1_PASSES, S_UP1, S_DOWN1):
            with sp.Fori(0, n) as i:
                for j in range(8):
                    col = (j // 4) * DFF1 + j0 * COLS
                    u = su // 2 + j
                    sp.wait_ge(lo_done, 2 * (u - RAW_SLOTS) + 2 + 16 * i)
                    sp.dma_start(raw[u % RAW_SLOTS][:], wu[:, 4 * (j % 4):4 * (j % 4) + 4,
                                                           bass.ds(i * COLS + col, COLS)]
                                 ).then_inc(raw_in[u % RAW_SLOTS], 16)
            column_blocks(sd, "w_down", 4 * j0, n, 0, 4)
        w_in2 = view("w_in_2")

        def in2_load(u):
            c0 = IN2_ORDER[u // 4] * COLS
            weight_load(S_IN2 // 2 + u, 0, w_in2[:, 4 * (u % 4):4 * (u % 4) + 4, c0:c0 + COLS])

        for u in range(4):
            in2_load(u)
        sp.wait_ge(mm_done, S_IN2)
        sp.dma_start(w_gate[:], a["w_in_2"].rearrange("o (k p) n -> p (o k) n", p=P)
                     [:, :, IN2_BLOCKS * COLS:IN2_BLOCKS * COLS + N_GATES]).then_inc(sem["wg_in"], 16)
        sp.dma_start(t5_tab[:], a["t5_bias_2"]).then_inc(sem["t5_in"], 16)
        sp.dma_start(t5_up[:], a["t5_up"]).then_inc(sem["t5_in"], 16)
        sp.dma_start(t5_ahead[:], a["t5_ahead"]).then_inc(sem["t5_in"], 16)
        sp.dma_start(cmp_mask[:], a["cmp_mask"]).then_inc(sem["t5_in"], 16)
        sp.dma_start(cmp_seen[:], a["cmp_seen"]).then_inc(sem["t5_in"], 16)
        w1_views = [a[n].rearrange("o (l p) n -> p (o l) n", p=P) for n in ("cmp_w1_k_2", "cmp_w1_v_2")]
        for u in range(4, 4 * IN2_BLOCKS):
            in2_load(u)
            if u < 8:
                kv, l = (u - 4) // 2, CMP_BLOCK // 2 * (u % 2)
                sp.dma_start(w1[:, kv, l:l + CMP_BLOCK // 2, :], w1_views[kv][:, l:l + CMP_BLOCK // 2, :]
                             ).then_inc(w1_in[kv], 16)
            if u == 8:
                sp.dma_start(w2[:, 0, :], a["cmp_w2_k_2"][0]).then_inc(sem["w2_in"], 16)
                sp.dma_start(w2[:, 1, :], a["cmp_w2_v_2"][0]).then_inc(sem["w2_in"], 16)
            if u == 11:
                sp.wait_ge(sem["t5_rows_ok"], 1)
                sp.dma_start(scratch, t5_rows[:]).then_inc(sem["t5_st"], 16)
                sp.wait_ge(sem["t5_cols_ok"], 1)
                sp.dma_start(scratch_cols.rearrange("(c p) h -> p c h", p=P), t5_cols[:]).then_inc(sem["t5_st"], 16)
            if u == 12:
                sp.wait_ge(sem["t5_st"], 32)
                sp.dma_start(cmp_dist[:], bass.AP(scratch_cols.tensor, 8, [[8, P], [128, 23], [1, 8]])
                             ).then_inc(sem["cmp_dist_in"], 16)

        def retention_load(u):
            c0 = IN2_BLOCKS * COLS + N_GATES + u // 4 * COLS
            weight_load(S_RET // 2 + u, 0, w_in2[:, 4 * (u % 4):4 * (u % 4) + 4, c0:c0 + COLS])

        for u in range(4):
            retention_load(u)

        def t5_bias(h):
            if h >= 2:
                sp.wait_ge(sem["at_s"], N1 + 2 * (h - 2) + 2)
            else:
                sp.wait_ge(sem["t5_mm"], 2)
            for t in range(NT):
                src = bass.AP(scratch.tensor, 512 * h + P * t + 1, [[1, P], [1, SEQ]])
                sp.dma_start(bias[h % 2][:, 1 - t, :], src).then_inc(t5_bias_in[h % 2], 16)

        t5_bias(0)
        t5_bias(1)
        for u in range(4, 4 * RET_BLOCKS):
            if u >= 11 and (u - 11) % 4 == 0 and (u - 11) // 4 + 2 < 8:
                t5_bias((u - 11) // 4 + 2)
            retention_load(u)
        w_out2 = view("w_out_2")
        for j in range(4):
            weight_load(S_OUT2 // 2 + j, 0, w_out2[:, 4 * j:4 * j + 4, 0:COLS])
        sp.wait_ge(sem["at_osb"], outs_before(NH))
        sp.dma_start(cos2[:], a["cos2"]).then_inc(sem["rtab_in"], 16)
        sp.dma_start(sin2[:], a["sin2"]).then_inc(sem["rtab_in"], 16)
        sp.dma_start(decay[:], a["decay"]).then_inc(sem["rtab_in"], 16)
        column_blocks(S_OUT2 + 8, "w_out_2", 0, 4, COLS, 3)
        sp.wait_ge(sem["rp_ok"], RET_HEADS)
        sp.dma_start(gain_row[:], bass.AP(a["norm_mix_post_2"].tensor, 0, [[0, P], [1, D]])
                     ).then_inc(sem["grow_in"], 16)
        for p in range(UP2_PASSES):
            column_blocks(S_UP2[p], "w_up_2", 0, 4, 4 * p * COLS, 4)
            if p == UP2_PASSES - 1:
                sp.wait_ge(sem["post_ok"], NT)
                sp.dma_start(gain_row[:], bass.AP(a["norm_mlp_post_2"].tensor, 0, [[0, P], [1, D]])
                             ).then_inc(sem["grow_in"], 16)
            column_blocks(S_DOWN2[p], "w_down_2", 16 * p, 4, 0, 4)
        o = out.rearrange("o (t p) n -> p (o t) n", p=P)
        for t in range(NT):
            sp.wait_ge(sem["post_ok"], NT + t + 1)
            sp.dma_start(o[:, t, :], x_rows[:, t, :]).then_inc(sem["out_in"], 16)
        sp.wait_ge(sem["out_in"], 16 * NT)

    @block.gpsimd
    def _(pool):
        chain = Chain(pool, sem["pool_chain"])
        pool.memset(neghalf[:], -0.5).then_inc(sem["consts_set"], 1)
        for i in range(FREE):
            pool.memset(unused[:, i:i + 1], 0.0).then_inc(row_free, 1)
            pool.memset(unused[:, 2 + i:3 + i], 0.0).then_inc(chan_free, 1)
        pool.wait_ge(sem["consts_set"], 1)

        def inverse_root(dst, src, scale, n, done):
            chain.link(pool.tensor_scalar(dst, src, scale, EPS, ALU.mult, ALU.add))
            pool.tensor_tensor(dst, dst, neghalf[:, 0:n], ALU.pow).then_inc(done, 1)

        def norm(n):
            pool.wait_ge(sem["norm_ss"], 2 * n + 2)
            inverse_root(rstd[:, 2 * n:2 * n + 2], sums[:, 2 * n:2 * n + 2], 1.0 / D, 2, sem["norm_rs"])

        norm(0)
        pool.wait_ge(sem["an_ss"], 1)
        inverse_root(rsq[:, 0:24], ssq[:, 0:24], 1.0 / HD, 24, sem["an_rs"])
        pool.wait_ge(sem["near_in"], 16)

        def masked_bias(h):
            pool.wait_ge(bias_in[h % 2], 64 * (h // 2 + 1))
            pool.tensor_tensor(bias[h % 2][:], bias[h % 2][:], near[:], ALU.add).then_inc(sem["bias_ok"], 1)

        masked_bias(0)
        masked_bias(1)
        for h in range(8):
            pool.wait_ge(sem["bn_ss"], h + 1)
            inverse_root(rsb[:, h % 2, :], ssb[:, h % 2, :], 1.0 / HD, 4, sem["bn_rs"])
        for h in range(2, 8):
            masked_bias(h)
        norm(1)
        for p in range(2):
            pool.memset(u_pad[p][:, :, 0:1], 0.0).then_inc(sem["cmask_in"], 1)
            pool.memset(u_pad[p][:, :, SEQ + 1:SEQ + 2], 0.0).then_inc(sem["cmask_in"], 1)
        norm(2)
        for r in range(RET_HEADS):
            pool.wait_ge(sem["ro_stat"], r + 1)
            inverse_root(grs[:, r % 2, :], bag[:, r % 2, :, 1], 1.0, 2, sem["ro_rs"])
        for n in (3, 4, 5):
            norm(n)

    @block.scalar
    def _(act):
        chain = Chain(act, sem["act_chain"])

        def ahead(step, i=0, m=0):
            q = step + AHEAD
            act.wait_ge(raw_in[q // 2 % RAW_SLOTS], 16 * (q // 8 + 1) + 16 * m * i)
            if q >= SPLIT_SLOTS:
                act.wait_ge(mm_done, q - SPLIT_SLOTS + 1 + 8 * m * i)
            act.activation(wh[q % SPLIT_SLOTS][:], raw[q // 2 % RAW_SLOTS][:, 2 * (q % 2):2 * (q % 2) + 2, :],
                           ACT.Copy).then_inc(hi_done, 1)

        def row_blocks(step0, g0, n, per, evac, last=False, extra=None):
            if per != 8 or last or extra:
                for b in range(n):
                    for j in range(per):
                        if step0 + per * b + j + AHEAD < N_STEPS:
                            ahead(step0 + per * b + j)
                        if extra and b == 0:
                            extra(j)
                    evac(b, g0 + b, step0 + per * (b + 1), 0, 0)
                return
            if n % 2:
                for j in range(8):
                    ahead(step0 + j)
                evac(0, g0, step0 + 8, 0, 0)
            with act.Fori(0, n // 2) as i:
                for b in (n % 2, n % 2 + 1):
                    for j in range(8):
                        ahead(step0 + 8 * b + j, i, 2)
                    evac(b, g0 + b, step0 + 8 * (b + 1), i, 2)

        def copy_rows(dst):
            def evac(b, g, end, i, m):
                act.wait_ge(mm_done, end + 8 * m * i)
                act.activation(dst[:, b + m * i, :, :], psum[:, 2 * (g % 2):2 * (g % 2) + 2, :],
                               ACT.Copy).then_inc(row_free, 1)
            return evac

        def no_evac(b, g, end, i, m):
            pass

        def norm_sums(n, src, ready, value, done=None):
            for t in range(NT):
                if ready is not None:
                    act.wait_ge(ready, value)
                act.activation(rows[:, t, :], src[:, t, :], ACT.Square,
                               accum_out=sums[:, 2 * n + t:2 * n + t + 1]).then_inc(sem["norm_ss"], 1)

        def transposed_hi(dst, fill0, chunk0, gain):
            for f in range(8):
                F = fill0 + f
                act.wait_ge(sem["tr_full"], F + 1)
                for c in range(2):
                    ins = act.activation(dst[:, 2 * f + c, 0, :], psum[:, 4 + F % 4, 256 * c:256 * c + 256],
                                         ACT.Copy, scale=par[:, Q_GAIN[gain] + 2 * f + c:Q_GAIN[gain] + 2 * f + c + 1])
                ins.then_inc(sem["tr_hi"], 1)

        def head_stage(j, k, last):
            if j == 0 and k < last and k < N1:
                n = k
                act.wait_ge(sem["at_qk"], n + 1)
                if n >= 2:
                    act.wait_ge(sem["at_sc"], n - 1)
                if heads[n][0] == "near":
                    for i, g in enumerate((Q_BQ, Q_BK)):
                        ins = act.activation(qk_t[n % 2][:, i, :], psum[:, QK_BANK, 256 * i:256 * i + 256],
                                             ACT.Copy, scale=par[:, g:g + 1])
                else:
                    ins = act.activation(qk_t[n % 2][:], psum[:, QK_BANK, :].rearrange("p (a b) -> p a b", a=2),
                                         ACT.Copy)
                ins.then_inc(sem["at_qksb"], 1)
            n = k - 1
            if j == 1 and n >= first[0]:
                act.wait_ge(sem["at_pt"], n + 1)
                if n >= 2:
                    act.wait_ge(sem["at_o"], n - 1)
                act.activation(prob_t[n % 2][:], psum[:, PT_BANK, :].rearrange("p (a b) -> p a b", a=2),
                               ACT.Copy).then_inc(sem["at_ptsb"], 1)
            if j == 2 and k < last:
                n = k
                act.wait_ge(sem["at_nm"], n + 1)
                if n >= 2:
                    act.wait_ge(sem["at_pt"], n - 1)
                if heads[n][0] == "band":
                    h = heads[n][1]
                    act.activation(esink[:, n % 2, :], nmx[:, n % 2, :], ACT.Exp, bias=sink[:, h:h + 1])
                for t in range(NT):
                    ins = act.activation(prob[n % 2][:, t, :], sco[n % 2][:, t, :], ACT.Exp,
                                         bias=nmx[:, n % 2, t:t + 1], accum_out=den[:, n % 2, t:t + 1])
                ins.then_inc(sem["at_p"], 1)
            n = k - 1
            if j == 3 and n >= first[0] and heads[n][0] != "slc":
                act.wait_ge(sem["at_o"], n + 1)
                kind, h = heads[n][:2]
                dst = mix_t[:, h, :] if kind == "win" else ot[:, h + (8 if kind == "near" else 0), :]
                act.activation(dst, psum[:, O_BANK, 0:SEQ], ACT.Copy).then_inc(sem["at_osb"], 1)

        first = [0]

        act.wait_ge(sem["x_in"], 16)
        norm_sums(0, x_rows, None, 0)
        for q in range(AHEAD):
            ahead(q - AHEAD)
        act.wait_ge(sem["par_in"], 16)
        transposed_hi(ha, T_MIX1, 0, "mix1")
        row_blocks(S_IN1, R_IN1, IN1_BLOCKS, 8, copy_rows(proj))

        act.wait_ge(sem["sink_in"], 16)
        for s in range(8 * GATE_BLOCKS):
            ahead(S_GATE + s)
            head_stage(s % 4, s // 4, N1)
            if s % 8 == 7:
                copy_rows(gates)(s // 8, R_GATE + s // 8, S_GATE + s + 1, 0, 0)
        for j in range(4):
            head_stage(j, N1, N1)
        act.wait_ge(mm_done, S_BRANCH)
        act.wait_ge(sem["at_osb"], N1)
        for c in range(4):
            act.activation(ha[:, 4 * c:4 * c + 4, 0, :], ot[:, 4 * c:4 * c + 4, :], ACT.Copy
                           ).then_inc(sem["ot_hi"], 1)

        def merged_hi(n):
            for f in range(2):
                F = T_MERGE + 2 * n + f
                act.wait_ge(sem["tr_full"], F + 1)
                act.activation(hb[:, 2 * (F - T_MERGE):2 * (F - T_MERGE) + 2, 0, :],
                               psum[:, 4 + F % 4, :].rearrange("p (a b) -> p a b", a=2), ACT.Copy
                               ).then_inc(sem["tr_hi"], 1)

        act.wait_ge(row_free, FREE + R_GATE + GATE_BLOCKS)
        for n in range(4):
            for b in range(2):
                ins = act.activation(gates[:, 4 * b + n, :, :], gates[:, 4 * b + n, :, :], ACT.Sigmoid)
            ins.then_inc(sem["sig_done"], 1)
            for j in range(8):
                if j == 4 and n:
                    merged_hi(n - 1)
                ahead(S_BRANCH + 8 * n + j)
        merged_hi(3)
        row_blocks(S_OUT1, R_OUT1, 4, 8, no_evac)
        norm_sums(1, x_rows, row_free, FREE + R_OUT1 + 4)
        transposed_hi(ha, T_FFN1, 0, "ffn1")

        act.wait_ge(sem["cmask_in"], 4)
        def up1_stage(p, j, v, pair, i):
            if j == 0:
                act.wait_ge(mm_done, S_UP1[p] + 8 * v + 8 + 16 * i)
                act.activation(u_pad[v][:, :, 1:SEQ + 1], psum[:, 4 * v:4 * v + 4, 0:SEQ], ACT.Copy
                               ).then_inc(sem["half_ok"], 1)
            if j == 1:
                act.wait_ge(chan_free, FREE + v + 1 + 2 * pair)
                for s in range(4):
                    chunk = 44 * v + 4 * pair + s
                    w = Q_CONVW + 3 * chunk + 1
                    ins = act.activation(conv[v][:, s, :], u_pad[v][:, s, 1:SEQ + 1], ACT.Identity,
                                         scale=par[:, bass.ds(w, 1)], bias=par[:, bass.ds(Q_CONVB + chunk, 1)])
                ins.then_inc(sem["conv_mid"], 1)
            if j == 3 and v == 0:
                act.wait_ge(sem["conv_done"], 1 + 2 * pair)
                act.activation(conv[0][:], conv[0][:], ACT.Silu).then_inc(sem["silu_done"], 1)
            if j == 4 and v == 1:
                act.wait_ge(sem["act_ready"], pair + 1)
                act.activation(hb[:, bass.ds(4 * i, 4), 0, :], act_f[:], ACT.Copy).then_inc(sem["hb_hi"], 1)

        for p, (j0, n) in enumerate(UP1_PASSES):
            for j in range(8):
                ahead(S_UP1[p] + j)
            with act.Fori(0, n - 1) as i:
                for j in range(8):
                    ahead(S_UP1[p] + 8 + j, i, 2)
                    up1_stage(p, j, 0, j0 + i, i)
                for j in range(8):
                    ahead(S_UP1[p] + 16 + j, i, 2)
                    up1_stage(p, j, 1, j0 + i, i)
            for j in range(8):
                ahead(S_UP1[p] + 16 * n - 8 + j)
                up1_stage(p, j, 0, j0 + n - 1, n - 1)

            def tail(j):
                for stage in range(8) if n == 4 else ([0], [1, 2], [3], [4, 5], [], [])[j]:
                    if n < 4 or stage == j:
                        up1_stage(p, stage, 1, j0 + n - 1, n - 1)

            row_blocks(S_DOWN1[p], R_DOWN1[p], 4, 2 * n, no_evac, extra=tail)

        norm_sums(2, x_rows, row_free, FREE + R_DOWN1[-1] + 4)
        transposed_hi(ha, T_MIX2, 0, "mix2")

        def pair(bank, n=2 * SEQ, rows=P):
            return psum[0:rows, bank, 0:n].rearrange("p (a b) -> p a b", a=2)

        for s in range(8 * IN2_BLOCKS):
            ahead(S_IN2 + s)
            if s == 5:
                act.wait_ge(sem["wg_in"], 16)
                act.activation(w_gate_h[:], w_gate[:], ACT.Copy).then_inc(sem["wg_hi"], 1)
            if s == 10:
                act.wait_ge(sem["t5_mm"], 2)
                act.activation(t5_cols[:].rearrange("p c h -> p (c h)"), psum[:, 6, 0:32], ACT.Copy
                               ).then_inc(sem["t5_cols_ok"], 1)
            if s == 12:
                for f in range(2):
                    act.wait_ge(sem["kvt_mm"], f + 1)
                    act.activation(kv_cmp_t[:, 2 * f:2 * f + 2, :], pair(4 + f), ACT.Copy).then_inc(sem["kvt_ok"], 1)
            if s == 14:
                act.wait_ge(sem["gate_mm"], 1)
                act.activation(gate_t[:], psum[0:N_GATES, 7, 0:SEQ], ACT.Copy).then_inc(sem["gate_half"], 1)
            if s in (17, 19):
                kv = (s - 17) // 2
                act.wait_ge(sem["hid_mm"], kv + 1)
                act.activation(hid_t[:, kv, :], psum[0:2 * NCMP, 4 + kv, 0:HD], ACT.Copy
                               ).then_inc(sem["hid_copied"], 1)
            if s == 18:
                act.wait_ge(sem["gate_tr"], 1)
                act.activation(gate24[:], pair(6, 2 * N_GATES), ACT.Sigmoid).then_inc(sem["gate_ok"], 1)
            if s == 21:
                act.wait_ge(sem["hid_tr"], 1)
                for kv in range(2):
                    act.activation(cmp_hid[:, kv, :, :].rearrange("p g n -> p (g n)"),
                                   psum[:, 7, 2 * NCMP * kv:2 * NCMP * (kv + 1)],
                                   ACT.Gelu_apprx_tanh, bias=par[:, Q_B1K + kv:Q_B1K + kv + 1]
                                   ).then_inc(sem["hid_ok"], 1)
            if s in (23, 28):
                for f in range(2):
                    i = (s == 28)
                    act.wait_ge(sem["qall_mm"], 2 * i + f + 1)
                    act.activation(q_all[i][:, 2 * f:2 * f + 2, :], pair(4 + f), ACT.Copy).then_inc(sem["qall_ok"], 1)
            if s == 24:
                act.wait_ge(sem["kv_mm"], 1)
                act.activation(cmp_k[:], pair(6, 2 * NCMP), ACT.Copy).then_inc(sem["kv_ok"], 1)
                act.wait_ge(sem["kv_mm"], 2)
                act.activation(cmp_v[:].rearrange("p g d -> p (g d)"), psum[0:NCMP, 6, SEQ:2 * SEQ], ACT.Copy
                               ).then_inc(sem["kv_ok"], 1)
            if s == 32:
                act.wait_ge(sem["cs_ok"], 1)
                act.activation(cmp_p[:], cmp_s[:], ACT.Exp).then_inc(sem["cs_exp"], 1)
            if s == 36:
                act.wait_ge(sem["kall_mm"], 1)
                act.wait_ge(sem["t5_st"], 32)
                act.activation(k_all[:, 0:2, :], pair(4), ACT.Copy).then_inc(sem["kall_ok"], 1)
            if s == 38:
                for f in range(4):
                    act.wait_ge(sem["cpt_mm"], f + 1)
                    act.activation(cmp_pt[:, 2 * f:2 * f + 2, :], pair(4 + (f + 1) % 4, rows=NCMP), ACT.Copy
                                   ).then_inc(sem["cpt_ok"], 1)
            if s % 8 == 7:
                g = R_IN2 + s // 8
                act.wait_ge(mm_done, S_IN2 + s + 1)
                act.activation(proj2[:, IN2_ORDER[s // 8], :, :], psum[:, 2 * (g % 2):2 * (g % 2) + 2, :], ACT.Copy
                               ).then_inc(row_free, 1)
        first[0] = N1
        for s in range(8 * RET_BLOCKS):
            ahead(S_RET + s)
            if s == 2:
                act.wait_ge(sem["kall_mm"], 2)
                act.activation(k_all[:, 2:4, :], pair(4), ACT.Copy).then_inc(sem["kall_ok"], 1)
            head_stage(s % 4, N1 + s // 4, NH)
            if s % 8 == 7:
                copy_rows(ret)(s // 8, R_RET + s // 8, S_RET + s + 1, 0, 0)
        for j in range(4):
            head_stage(j, NH, NH)
        act.wait_ge(mm_done, S_OUT2)
        act.wait_ge(sem["at_osb"], outs_before(NH))
        for c in range(2):
            act.activation(ha[:, 4 * c:4 * c + 4, 0, :], mix_t[:, 4 * c:4 * c + 4, :], ACT.Copy
                           ).then_inc(sem["ot_hi"], 1)
        act.wait_ge(row_free, FREE + R_RET + RET_BLOCKS)
        for b in (6, 7):
            ins = act.activation(ret[:, b, :, :], ret[:, b, :, :], ACT.Silu)
        ins.then_inc(sem["silu_g"], 1)
        for r in range(RET_HEADS):
            act.wait_ge(sem["rq_mm"], r + 1)
            if r >= 2:
                act.wait_ge(sem["rs_mm"], r - 1)
            act.activation(ret_q[r % 2][:], psum[:, 4, :].rearrange("p (a b) -> p a b", a=2), ACT.Copy
                           ).then_inc(sem["rq_ok"], 1)
            act.wait_ge(sem["rk_mm"], r + 1)
            act.activation(ret_k[r % 2][:], psum[:, 5, :].rearrange("p (a b) -> p a b", a=2), ACT.Copy
                           ).then_inc(sem["rk_ok"], 1)
        for f in range(4):
            F = T_RETO + f
            act.wait_ge(sem["tr_full"], F + 1)
            act.activation(ha[:, 8 + 2 * f:10 + 2 * f, 0, :], psum[:, 4 + F % 4, :].rearrange("p (a b) -> p a b", a=2),
                           ACT.Copy).then_inc(sem["tr_hi"], 1)

        def mix_rows(b, g, end, i, m):
            act.wait_ge(mm_done, end + 8 * m * i)
            act.activation(rows[:, :, bass.ds((b + m * i) * COLS, COLS)], psum[:, 2 * (g % 2):2 * (g % 2) + 2, :],
                           ACT.Copy).then_inc(row_free, 1)

        row_blocks(S_OUT2, R_OUT2, 4, 8, mix_rows)
        for t in range(NT):
            act.wait_ge(row_free, FREE + R_OUT2 + 4)
            act.activation(junk[:, t, :], rows[:, t, :], ACT.Square,
                           accum_out=sums[:, 6 + t:7 + t]).then_inc(sem["norm_ss"], 1)
        for t in range(NT):
            act.wait_ge(sem["post_ok"], t + 1)
            act.activation(rows[:, t, :], x_rows[:, t, :], ACT.Square,
                           accum_out=sums[:, 8 + t:9 + t]).then_inc(sem["norm_ss"], 1)
        transposed_hi(ha, T_MLP2, 0, "mlp2")
        for p in range(UP2_PASSES):
            with act.Fori(0, 2) as i:
                for v in range(2):
                    for j in range(8):
                        ahead(S_UP2[p] + 8 * v + j, i, 2)
                    c = C_UP2[p] - C_UP2[0] + v
                    act.wait_ge(mm_done, S_UP2[p] + 8 * v + 8 + 16 * i)
                    act.activation(u_sum[:], psum[:, 4 * v:4 * v + 4, 0:SEQ], ACT.Copy
                                   ).then_inc(sem["usum_done"], 1)
                    act.wait_ge(sem["act_ready"], 11 + c + 1 + 2 * i)
                    act.activation(hb[:, bass.ds(8 * i + 4 * v, 4), 0, :], u_act[:], ACT.Copy
                                   ).then_inc(sem["hb_hi"], 1)
            row_blocks(S_DOWN2[p], R_DOWN2[p], 4, 8, no_evac, last=p == UP2_PASSES - 1)
        for t in range(NT):
            act.wait_ge(row_free, FREE + R_DOWN2[-1] + 4)
            act.activation(junk[:, t, :], rows[:, t, :], ACT.Square,
                           accum_out=sums[:, 10 + t:11 + t]).then_inc(sem["norm_ss"], 1)

    @block.vector
    def _(dve):
        chain = Chain(dve, sem["dve_chain"])

        def ahead(step, i=0, m=0):
            q = step + AHEAD
            dve.wait_ge(hi_done, q + 1 + 8 * m * i)
            dve.tensor_tensor(wl[q % SPLIT_SLOTS][:], raw[q // 2 % RAW_SLOTS][:, 2 * (q % 2):2 * (q % 2) + 2, :],
                              wh[q % SPLIT_SLOTS][:].bitcast(F32), ALU.subtract).then_inc(lo_done, 1)

        def row_blocks(step0, g0, n, per, evac, last=False, extra=None):
            if per != 8 or last or extra:
                for b in range(n):
                    for j in range(per):
                        if step0 + per * b + j + AHEAD < N_STEPS:
                            ahead(step0 + per * b + j)
                        if extra and b == 0:
                            extra(j)
                    evac(b, g0 + b, step0 + per * (b + 1), 0, 0)
                return
            if n % 2:
                for j in range(8):
                    ahead(step0 + j)
                evac(0, g0, step0 + 8, 0, 0)
            with dve.Fori(0, n // 2) as i:
                for b in (n % 2, n % 2 + 1):
                    for j in range(8):
                        ahead(step0 + 8 * b + j, i, 2)
                    evac(b, g0 + b, step0 + 8 * (b + 1), i, 2)

        def no_evac(b, g, end, i, m):
            pass

        def scaled_rows(n, src):
            dve.wait_ge(sem["norm_rs"], n + 1)
            for t in range(NT):
                dve.tensor_scalar(rows[:, t, :], src[:, t, :], rstd[:, 2 * n + t:2 * n + t + 1], None, ALU.mult
                                  ).then_inc(sem["norm_rows"], 1)

        def transposed_lo(dst, fill0, gain):
            for f in range(8):
                F = fill0 + f
                dve.wait_ge(sem["tr_hi"], F + 1)
                for c in range(2):
                    col = Q_GAIN[gain] + 2 * f + c
                    ins = dve.scalar_tensor_tensor(
                        dst[:, 2 * f + c, 1, :], psum[:, 4 + F % 4, 256 * c:256 * c + 256], par[:, col:col + 1],
                        dst[:, 2 * f + c, 0, :].bitcast(F32), ALU.mult, ALU.subtract)
                ins.then_inc(sem["tr_lo"], 1)

        def plain_lo(dst, F):
            dve.wait_ge(sem["tr_hi"], F + 1)
            dve.tensor_tensor(dst[:, :, 1, :], psum[:, 4 + F % 4, :].rearrange("p (a b) -> p a b", a=2),
                              dst[:, :, 0, :].bitcast(F32), ALU.subtract).then_inc(sem["tr_lo"], 1)

        def head_stage(j, k, last):
            if k >= last:
                return
            n = k
            kind, h = heads[n][:2]
            if j == 2:
                dve.wait_ge(sem["at_sc"], n + 1)
                if n >= 2:
                    dve.wait_ge(sem["at_p"], n - 1)
                if kind == "near":
                    dve.wait_ge(sem["bias_ok"], h + 1)
                elif kind != "band":
                    dve.wait_ge(t5_bias_in[h % 2], 32 * (h // 2 + 1))
                b = (band if kind == "band" else bias[h % 2])[:].rearrange("p a b -> p (a b)")
                if kind != "band":
                    b = bass.AP(b.tensor, b.offset + NT * SEQ - 1, [list(b.ap[0]), [-1, NT * SEQ]])
                dve.scalar_tensor_tensor(sco[n % 2][:].rearrange("p a b -> p (a b)"), psum[:, SC_BANK, :], SCALE,
                                         b, ALU.mult, ALU.add
                                         ).then_inc(sem["at_s"], 1)
                dve.wait_ge(sem["at_s"], n + 1)
                chain.link(dve.reduce_max(mx[:, n % 2, :], sco[n % 2][:], AX.X))
                if kind == "band":
                    dve.tensor_scalar(nmx[:, n % 2, :], mx[:, n % 2, :], sink[:, h:h + 1], -1.0, ALU.max, ALU.mult
                                      ).then_inc(sem["at_nm"], 1)
                else:
                    dve.tensor_scalar(nmx[:, n % 2, :], mx[:, n % 2, :], -1.0, None, ALU.mult
                                      ).then_inc(sem["at_nm"], 1)
            if j == 3:
                dve.wait_ge(sem["at_p"], n + 1)
                if kind == "band":
                    chain.link(dve.tensor_tensor(den[:, n % 2, :], den[:, n % 2, :], esink[:, n % 2, :], ALU.add))
                chain.link(dve.reciprocal(rden[:, n % 2, :], den[:, n % 2, :]))
                if kind in ("slc", "win"):
                    g = 3 * h + (1 if kind == "slc" else 2)
                    chain.link(dve.tensor_tensor(rden[:, n % 2, :], rden[:, n % 2, :], gate24[:, :, g], ALU.mult))
                for t in range(NT):
                    ins = dve.tensor_scalar(prob[n % 2][:, t, :], prob[n % 2][:, t, :], rden[:, n % 2, t:t + 1],
                                            None, ALU.mult)
                ins.then_inc(sem["at_pn"], 1)

        dve.wait_ge(sem["cos1_in"], 16)
        dve.wait_ge(sem["sin1_in"], 16)
        dve.wait_ge(sem["again_in"], 32)
        for i in range(2):
            g = [a_gain[:, i, 64 * s:64 * s + 64].unsqueeze(1).to_broadcast([P, NT, 64]) for s in range(2)]
            dve.tensor_tensor(rot_a[:, i, :, 0:64], cos1[:], g[0], ALU.mult)
            dve.tensor_tensor(rot_a[:, i, :, 64:128], cos1[:], g[1], ALU.mult)
            dve.tensor_tensor(rot_b[:, i, :, 64:128], sin1[:], g[0], ALU.mult)
            chain.link(dve.tensor_tensor(rot_b[:, i, :, 0:64], sin1[:], g[1], ALU.mult))
        chain.link(dve.tensor_scalar(rot_b[:, :, :, 0:64], rot_b[:, :, :, 0:64], -1.0, None, ALU.mult))

        dve.wait_ge(sem["x_in"], 16)
        scaled_rows(0, x_rows)
        for q in range(AHEAD):
            ahead(q - AHEAD)
        dve.wait_ge(sem["par_in"], 16)
        transposed_lo(ha, T_MIX1, "mix1")
        row_blocks(S_IN1, R_IN1, IN1_BLOCKS, 8, no_evac)

        dve.wait_ge(row_free, FREE + 3)
        pieces = [(0, 0, 0, 4), (0, 1, 0, 4), (1, 0, 0, 4), (1, 1, 0, 4), (2, 0, 1, 2), (2, 1, 1, 2)]

        def piece(b, t, nh):
            return proj[:, b, t, 0:nh * HD].rearrange("p (h d) -> p h d", d=HD)

        for i, (b, t, _, nh) in enumerate(pieces):
            x = piece(b, t, nh)
            chain.link(dve.tensor_tensor(tmp_a[:, 0:nh, :], x, x, ALU.mult))
            chain.link(dve.reduce_sum(ssq[:, 4 * i:4 * i + nh], tmp_a[:, 0:nh, :], AX.X))
        dve.memset(ssq[:, 18:20], 1.0)
        dve.memset(ssq[:, 22:24], 1.0).then_inc(sem["an_ss"], 1)
        dve.wait_ge(sem["an_rs"], 1)
        for i, (b, t, kind, nh) in enumerate(pieces):
            x = piece(b, t, nh)
            r = rsq[:, 4 * i:4 * i + nh].unsqueeze(2).to_broadcast([P, nh, HD])
            chain.link(dve.tensor_tensor(x, x, r, ALU.mult))

            def row(tab, lo, hi):
                return tab[:, kind, t, lo:hi].unsqueeze(1).to_broadcast([P, nh, hi - lo])

            dve.tensor_tensor(tmp_a[:, 0:nh, :], x, row(rot_a, 0, HD), ALU.mult)
            dve.tensor_tensor(tmp_b[:, 0:nh, 0:64], x[:, :, 64:128], row(rot_b, 0, 64), ALU.mult)
            chain.link(dve.tensor_tensor(tmp_b[:, 0:nh, 64:128], x[:, :, 0:64], row(rot_b, 64, 128), ALU.mult))
            dve.tensor_tensor(x, tmp_a[:, 0:nh, :], tmp_b[:, 0:nh, :], ALU.add).then_inc(sem["a_ready"], 1)

        def near_view(h):
            c = h % 4 * HD
            return proj[:, 3 + h // 4:6 + h // 4:2, :, c:c + HD]

        dve.wait_ge(sem["band_in"], 16)
        for s in range(8 * GATE_BLOCKS):
            j, k = s % 4, s // 4
            ahead(S_GATE + s)
            if k < 8 and j == 0:
                t4 = tmp_b[:].rearrange("p (a b) d -> p a b d", a=2)
                if k == 0:
                    dve.wait_ge(row_free, FREE + R_GATE)
                    dve.wait_ge(sem["a_ready"], len(pieces))
                chain.link(dve.tensor_tensor(t4, near_view(k), near_view(k), ALU.mult))
                dve.reduce_sum(ssb[:, k % 2, :], tmp_b[:], AX.X).then_inc(sem["bn_ss"], 1)
            if k < 8 and j == 1:
                dve.wait_ge(sem["bn_rs"], k + 1)
                r = rsb[:, k % 2, :].rearrange("p (a b) -> p a b", a=2).unsqueeze(3).to_broadcast([P, 2, NT, HD])
                dve.tensor_tensor(near_view(k), near_view(k), r, ALU.mult).then_inc(sem["bn_ok"], 1)
            head_stage(j, k, N1)
        for c in range(4):
            dve.wait_ge(sem["ot_hi"], c + 1)
            dve.tensor_tensor(ha[:, 4 * c:4 * c + 4, 1, :], ot[:, 4 * c:4 * c + 4, :],
                              ha[:, 4 * c:4 * c + 4, 0, :].bitcast(F32), ALU.subtract).then_inc(sem["ot_lo"], 1)

        def merged_lo(n):
            for f in range(2):
                plain_lo(hb[:, 4 * n + 2 * f:4 * n + 2 * f + 2], T_MERGE + 2 * n + f)

        for n in range(4):
            for j in range(4):
                ahead(S_BRANCH + 8 * n + j)
            dve.wait_ge(mm_done, S_BRANCH + 8 * n + 4)
            dve.wait_ge(sem["sig_done"], n + 1)
            if n >= 2:
                dve.wait_ge(sem["tr_full"], T_MERGE + 2 * n - 2)
            dve.tensor_tensor(merged[n % 2][:], psum[:, 2:4, :], gates[:, n, :, :], ALU.mult).then_inc(row_free, 1)
            if n:
                merged_lo(n - 1)
            for j in range(4, 8):
                ahead(S_BRANCH + 8 * n + j)
            dve.wait_ge(mm_done, S_BRANCH + 8 * n + 8)
            dve.tensor_tensor(gates[:, 4 + n, :, :], psum[:, 0:2, :], gates[:, 4 + n, :, :], ALU.mult
                              ).then_inc(row_free, 1)
            dve.wait_ge(row_free, FREE + R_BRANCH + 2 * n + 2)
            dve.tensor_tensor(merged[n % 2][:], merged[n % 2][:], gates[:, 4 + n, :, :], ALU.add
                              ).then_inc(sem["merge_rows"], 1)
        merged_lo(3)

        def add_rows(dst, add=True):
            def evac(b, g, end, i, m):
                dve.wait_ge(mm_done, end + 8 * m * i)
                d = dst[:, :, bass.ds((b + m * i) * COLS, COLS)]
                if add:
                    dve.tensor_tensor(d, psum[:, 2 * (g % 2):2 * (g % 2) + 2, :], d, ALU.add).then_inc(row_free, 1)
                else:
                    dve.tensor_copy(d, psum[:, 2 * (g % 2):2 * (g % 2) + 2, :]).then_inc(row_free, 1)
            return evac

        dve.wait_ge(sem["xre_in"], 16)
        row_blocks(S_OUT1, R_OUT1, 4, 8, add_rows(x_rows))
        scaled_rows(1, x_rows)
        transposed_lo(ha, T_FFN1, "ffn1")

        def up1_stage(p, j, v, pair, i):
            count = 2 * pair + v + 1
            if j == 0:
                dve.wait_ge(sem["half_ok"], count)
                u = u_pad[v][:, :, 1:SEQ + 1]
                dve.tensor_tensor(u, psum[:, 4 * v:4 * v + 4, SEQ:2 * SEQ], u, ALU.add).then_inc(chan_free, 1)
            if j in (2, 3):
                if j == 2:
                    dve.wait_ge(sem["conv_mid"], count)
                else:
                    dve.wait_ge(sem["tap_done"], count)
                tap = 0 if j == 2 else 2
                for s in range(4):
                    w = Q_CONVW + 3 * (44 * v + 4 * pair + s) + tap
                    ins = dve.scalar_tensor_tensor(conv[v][:, s, :], u_pad[v][:, s, tap:tap + SEQ],
                                                   par[:, bass.ds(w, 1)], conv[v][:, s, :], ALU.mult, ALU.add)
                ins.then_inc(sem["tap_done" if j == 2 else "conv_done"], 1)
            if j == 4 and v == 1:
                dve.wait_ge(sem["conv_done"], count)
                dve.wait_ge(sem["silu_done"], pair + 1)
                dve.tensor_tensor(act_f[:], conv[0][:], conv[1][:], ALU.mult).then_inc(sem["act_ready"], 1)
            if j == 5 and v == 1:
                dve.wait_ge(sem["hb_hi"], pair + 1)
                h = hb[:, bass.ds(4 * i, 4), :, :]
                dve.tensor_tensor(h[:, :, 1, :], act_f[:], h[:, :, 0, :].bitcast(F32), ALU.subtract
                                  ).then_inc(sem["hb_lo"], 1)

        for p, (j0, n) in enumerate(UP1_PASSES):
            for j in range(8):
                ahead(S_UP1[p] + j)
            with dve.Fori(0, n - 1) as i:
                for j in range(8):
                    ahead(S_UP1[p] + 8 + j, i, 2)
                    up1_stage(p, j, 0, j0 + i, i)
                for j in range(8):
                    ahead(S_UP1[p] + 16 + j, i, 2)
                    up1_stage(p, j, 1, j0 + i, i)
            for j in range(8):
                ahead(S_UP1[p] + 16 * n - 8 + j)
                up1_stage(p, j, 0, j0 + n - 1, n - 1)

            def tail(j):
                for stage in range(8) if n == 4 else ([0], [1, 2], [3], [4, 5], [], [])[j]:
                    if n < 4 or stage == j:
                        up1_stage(p, stage, 1, j0 + n - 1, n - 1)

            row_blocks(S_DOWN1[p], R_DOWN1[p], 4, 2 * n, add_rows(x_rows), extra=tail)

        scaled_rows(2, x_rows)
        transposed_lo(ha, T_MIX2, "mix2")
        p16 = cmp_p[:].rearrange("p h t n -> p (h t) n")
        s16 = cmp_s[:].rearrange("p h t n -> p (h t) n")
        m16 = cmp_m[:].rearrange("p h t -> p (h t)")
        n16 = cmp_n[:].rearrange("p h t -> p (h t)")
        for s in range(8 * IN2_BLOCKS):
            ahead(S_IN2 + s)
            if s == 6:
                dve.wait_ge(sem["wg_hi"], 1)
                dve.tensor_tensor(w_gate_l[:], w_gate[:], w_gate_h[:].bitcast(F32), ALU.subtract
                                  ).then_inc(sem["wg_lo"], 1)
            if s == 10:
                dve.wait_ge(sem["t5_in"], 80)
                dve.wait_ge(sem["t5_mm"], 1)
                dve.tensor_tensor(t5_rows[:], psum[0:8, 7, :], t5_ahead[:], ALU.add).then_inc(sem["t5_rows_ok"], 1)
            if s in (13, 14):
                kv = s - 13
                dve.wait_ge(sem["kvt_ok"], kv + 1)
                for g in range(2):
                    src = kv_cmp_t[:, 2 * kv + g, :]
                    win = bass.AP(src.tensor, src.offset, [list(src.ap[0]), [1, CMP_BLOCK], [CMP_STRIDE, NCMP]])
                    pe_col = (Q_PEK, Q_PEV)[kv]
                    pe_in = par[:, pe_col:pe_col + CMP_BLOCK].unsqueeze(2).to_broadcast([P, CMP_BLOCK, NCMP])
                    ins = dve.tensor_tensor(cmp_in[:, kv, :, g, :], win, pe_in, ALU.add)
                ins.then_inc(sem["cin_ok"], 1)
            if s == 15:
                dve.wait_ge(sem["gate_half"], 1)
                dve.tensor_tensor(gate_t[:], psum[0:N_GATES, 7, SEQ:2 * SEQ], gate_t[:], ALU.add
                                  ).then_inc(sem["gate_sum"], 1)
            if s == 25:
                dve.wait_ge(sem["cmp_dist_in"], 16)
                for t in range(NT):
                    src = cmp_dist[:, 8 * t + NCMP - 1, :]
                    by_block = bass.AP(src.tensor, src.offset, [list(src.ap[0]), [1, 8], [-8, NCMP]])
                    ins = dve.tensor_tensor(cmp_bias[:, :, t, :], by_block,
                                            cmp_mask[:, t, :].unsqueeze(1).to_broadcast([P, 8, NCMP]), ALU.add)
                chain.link(ins)
            if s == 31:
                dve.wait_ge(sem["cs_mm"], 1)
                chain.link(dve.scalar_tensor_tensor(cmp_s[:].rearrange("p h t n -> p (h t n)"), psum[:, 7, 0:240], SCALE,
                                                    cmp_bias[:].rearrange("p h t n -> p (h t n)"), ALU.mult, ALU.add))
                chain.link(dve.reduce_max(m16, s16, AX.X))
                dve.tensor_tensor(s16, s16, m16.unsqueeze(2).to_broadcast([P, 16, NCMP]), ALU.subtract
                                  ).then_inc(sem["cs_ok"], 1)
            if s == 33:
                dve.wait_ge(sem["cs_exp"], 1)
                dve.wait_ge(sem["gate_ok"], 1)
                chain.link(dve.reduce_sum(n16, p16, AX.X))
                chain.link(dve.reciprocal(n16, n16))
                chain.link(dve.tensor_tensor(cmp_n[:], cmp_n[:],
                                             gate24[:].rearrange("p t (h b) -> p h t b", b=3)[:, :, :, 0], ALU.mult))
                for t in range(NT):
                    ins = dve.tensor_tensor(cmp_p[:, :, t, :], cmp_p[:, :, t, :],
                                            cmp_seen[:, t, :].unsqueeze(1).to_broadcast([P, 8, NCMP]), ALU.mult)
                chain.link(ins)
                dve.tensor_tensor(p16, p16, n16.unsqueeze(2).to_broadcast([P, 16, NCMP]), ALU.mult
                                  ).then_inc(sem["cs_p"], 1)
        for s in range(8 * RET_BLOCKS):
            ahead(S_RET + s)
            head_stage(s % 4, N1 + s // 4, NH)
        for c in range(2):
            dve.wait_ge(sem["ot_hi"], 4 + c + 1)
            dve.tensor_tensor(ha[:, 4 * c:4 * c + 4, 1, :], mix_t[:, 4 * c:4 * c + 4, :],
                              ha[:, 4 * c:4 * c + 4, 0, :].bitcast(F32), ALU.subtract).then_inc(sem["ot_lo"], 1)
        dve.wait_ge(sem["rtab_in"], 48)
        dve.wait_ge(row_free, FREE + R_RET + RET_BLOCKS)
        for blk in range(4):
            for t in range(NT):
                x = ret[:, blk, t, :].rearrange("p (h d) -> p h d", h=2)
                x1, x2 = x[:, :, 0:HD], x[:, :, HD:2 * HD]
                c = cos2[:, t, :].unsqueeze(1).to_broadcast([P, 2, HD])
                s = sin2[:, t, :].unsqueeze(1).to_broadcast([P, 2, HD])
                dve.tensor_tensor(rt[0][:], x1, c, ALU.mult)
                dve.tensor_tensor(rt[1][:], x2, s, ALU.mult)
                dve.tensor_tensor(rt[2][:], x2, c, ALU.mult)
                chain.link(dve.tensor_tensor(rt[3][:], x1, s, ALU.mult))
                dve.tensor_tensor(x1, rt[0][:], rt[1][:], ALU.subtract)
                dve.tensor_tensor(x2, rt[2][:], rt[3][:], ALU.add).then_inc(sem["rope_ok"], 1)
                dve.wait_ge(sem["rope_ok"], 2 * blk + t + 1)
        for r in range(RET_HEADS):
            dve.wait_ge(sem["rs_mm"], r + 1)
            if r >= 2:
                dve.wait_ge(sem["ro_mm"], r - 1)
            dve.tensor_tensor(ret_p[r % 2][:], psum[:, 6, :].rearrange("p (a b) -> p a b", a=2), decay[:, r, :, :],
                              ALU.mult).then_inc(sem["rp_ok"], 1)
            dve.wait_ge(sem["ro_mm"], r + 1)
            for t in range(NT):
                ins = dve.bn_stats(bst[:, r % 2, t, :], psum[:, 7, RET_D * t:RET_D * t + RET_D])
            chain.link(ins)
            for t in range(NT):
                ins = dve.bn_aggr(bag[:, r % 2, t, :], bst[:, r % 2, t, :])
            ins.then_inc(sem["ro_stat"], 1)
            dve.wait_ge(sem["ro_rs"], r + 1)
            dve.wait_ge(sem["silu_g"], 1)
            o = [ret_o[:, t, RET_D * r:RET_D * r + RET_D] for t in range(NT)]
            for t in range(NT):
                ins = dve.tensor_scalar(o[t], psum[:, 7, RET_D * t:RET_D * t + RET_D], bag[:, r % 2, t, 0:1],
                                        grs[:, r % 2, t:t + 1], ALU.subtract, ALU.mult)
            chain.link(ins)
            for t in range(NT):
                ins = dve.tensor_tensor(o[t], o[t], ret[:, 6 + r // 2, t, RET_D * (r % 2):RET_D * (r % 2) + RET_D],
                                        ALU.mult)
            ins.then_inc(sem["ro_ok"], 1)
        for f in range(4):
            plain_lo(ha[:, 8 + 2 * f:10 + 2 * f], T_RETO + f)
        row_blocks(S_OUT2, R_OUT2, 4, 8, no_evac)

        def add_normed(n, loads):
            dve.wait_ge(sem["norm_rs"], n + 1)
            dve.wait_ge(sem["grow_in"], 16 * loads)
            for t in range(NT):
                chain.link(dve.scalar_tensor_tensor(rows[:, t, :], rows[:, t, :], rstd[:, 2 * n + t:2 * n + t + 1],
                                                    gain_row[:], ALU.mult, ALU.mult))
                dve.tensor_tensor(x_rows[:, t, :], x_rows[:, t, :], rows[:, t, :], ALU.add
                                  ).then_inc(sem["post_ok"], 1)

        add_normed(3, 1)
        scaled_rows(4, x_rows)
        transposed_lo(ha, T_MLP2, "mlp2")
        for p in range(UP2_PASSES):
            with dve.Fori(0, 2) as i:
                chain.enter(i, 0)
                for v in range(2):
                    for j in range(8):
                        ahead(S_UP2[p] + 8 * v + j, i, 2)
                    c = C_UP2[p] - C_UP2[0] + v
                    dve.wait_ge(sem["usum_done"], c + 1 + 2 * i)
                    dve.tensor_tensor(u_sum[:], psum[:, 4 * v:4 * v + 4, SEQ:2 * SEQ], u_sum[:], ALU.add
                                      ).then_inc(chan_free, 1)
                    dve.wait_ge(chan_free, FREE + C_UP2[p] + v + 1 + 2 * i)
                    dve.scalar_tensor_tensor(u_act[:], u_sum[:], 0.0, u_sum[:], ALU.max, ALU.mult
                                             ).then_inc(sem["act_ready"], 1)
                    dve.wait_ge(sem["hb_hi"], 11 + c + 1 + 2 * i)
                    d = hb[:, bass.ds(8 * i + 4 * v, 4), :, :]
                    dve.tensor_tensor(d[:, :, 1, :], u_act[:], d[:, :, 0, :].bitcast(F32), ALU.subtract
                                      ).then_inc(sem["hb_lo"], 1)
            chain.leave(2)
            row_blocks(S_DOWN2[p], R_DOWN2[p], 4, 8, add_rows(y_rows, p > 0), last=p == UP2_PASSES - 1)
        add_normed(5, 2)

    @block.tensor
    def _(pe):
        def rows_step(q, i, m, src, chunks, g, first, last):
            pe.wait_ge(lo_done, q + 1 + 8 * m * i)
            s = q % SPLIT_SLOTS
            for c in range(2):
                for t in range(NT):
                    acc = psum[:, 2 * (g % 2) + t, :]
                    hi = src[:, chunks[c], 0, t * P:(t + 1) * P]
                    lo = src[:, chunks[c], 1, t * P:(t + 1) * P]
                    pe.matmul(acc, hi, wh[s][:, c, :], start=first and c == 0, stop=False)
                    pe.matmul(acc, hi, wl[s][:, c, :], start=False, stop=False)
                    ins = pe.matmul(acc, lo, wh[s][:, c, :], start=False, stop=last and c == 1)
            ins.then_inc(mm_done, 1)

        def row_blocks(step0, g0, n, per, src, ready=None):
            def one(b, g, q0, i, m):
                pe.wait_ge(row_free, g + 1 + m * i)
                for j in range(per):
                    if ready:
                        ready(j)
                    rows_step(q0 + j, i, m, src, (2 * j, 2 * j + 1), g, j == 0, j == per - 1)
            if per != 8:
                for b in range(n):
                    one(b, g0 + b, step0 + per * b, 0, 0)
                return
            if n % 2:
                one(0, g0, step0, 0, 0)
            with pe.Fori(0, n // 2) as i:
                for b in (n % 2, n % 2 + 1):
                    one(b, g0 + b, step0 + 8 * b, i, 2)

        def channel_step(q, i, m, v, j):
            pe.wait_ge(lo_done, q + 1 + 8 * m * i)
            s = q % SPLIT_SLOTS
            for c in range(2):
                k = 2 * j + c
                both = ha[:, k, :, :].rearrange("p a b -> p (a b)")
                for d in range(4):
                    acc = psum[:, 4 * v + d, :]
                    hi, lo = (w[s][:, c, P * d:P * d + P] for w in (wh, wl))
                    if k < KC - 1:
                        pe.matmul(acc, hi, both, start=k == 0, stop=False)
                        ins = pe.matmul(acc[:, 0:SEQ], lo, ha[:, k, 0, :], start=False, stop=False)
                    else:
                        pe.matmul(acc[:, 0:SEQ], lo, ha[:, k, 0, :], start=False, stop=False)
                        ins = pe.matmul(acc, hi, both, start=False, stop=True)
            ins.then_inc(mm_done, 1)

        def transposes(F, src, done=None):
            if F >= 4:
                pe.wait_ge(sem["tr_lo"], F - 3)
            for c in range(2):
                for t in range(NT):
                    ins = pe.transpose(psum[:, 4 + F % 4, SEQ * c + P * t:SEQ * c + P * t + P], src(c, t), ident[:])
            ins.then_inc(sem["tr_full"], 1)

        def norm_transposes(n, fill0):
            rows_value = {0: 2, 1: 4, 2: 6, 4: 8}[n]
            pe.wait_ge(sem["norm_rows"], rows_value)
            for f in range(8):
                transposes(fill0 + f, lambda c, t: rows[:, t, (2 * f + c) * P:(2 * f + c + 1) * P])

        def split_by(fill0):
            return lambda j: pe.wait_ge(sem["tr_lo"], fill0 + j + 1)

        def head_stage(j, k, last):
            if j == 0 and k < last and k < N1:
                n = k
                kind, h, x, (qb, qc), (kb, kc_), _ = heads[n]
                if kind == "band":
                    pe.wait_ge(sem["a_ready"], 6)
                if kind == "near":
                    pe.wait_ge(sem["bn_ok"], h + 1)
                if n:
                    pe.wait_ge(sem["at_qksb"], n)
                for i, (b, c) in enumerate(((qb, qc), (kb, kc_))):
                    for t in range(NT):
                        ins = pe.transpose(psum[:, QK_BANK, SEQ * i + P * t:SEQ * i + P * t + P],
                                           x[:, b, t, c:c + HD], ident[:])
                ins.then_inc(sem["at_qk"], 1)
            if j == 1 and k - 1 >= first[0]:
                n = k - 1
                pe.wait_ge(sem["at_pn"], n + 1)
                if n:
                    pe.wait_ge(sem["at_ptsb"], n)
                for kt in range(NT):
                    for t in range(NT):
                        ins = pe.transpose(psum[:, PT_BANK, SEQ * kt + P * t:SEQ * kt + P * t + P],
                                           prob[n % 2][:, t, P * kt:P * kt + P], ident[:])
                ins.then_inc(sem["at_pt"], 1)
            if j == 2 and k < last:
                n = k
                kind, h = heads[n][:2]
                if n < N1:
                    pe.wait_ge(sem["at_qksb"], n + 1)
                    q_t, k_t = qk_t[n % 2][:, 0, :], qk_t[n % 2][:, 1, :]
                else:
                    pe.wait_ge(sem["kall_ok"], 1 if kind == "slc" else 2)
                    q_t, k_t = q_all[h // 4][:, h % 4, :], k_all[:, 2 * (kind == "win") + h // 4, :]
                if n:
                    pe.wait_ge(sem["at_s"], n)
                for t in range(NT):
                    ins = pe.matmul(psum[:, SC_BANK, SEQ * t:SEQ * t + SEQ], q_t[:, P * t:P * t + P], k_t,
                                    start=True, stop=True)
                ins.then_inc(sem["at_sc"], 1)
            if j == 3 and k - 1 >= first[0]:
                n = k - 1
                kind, h, x, _, _, (vb, vc) = heads[n]
                pe.wait_ge(sem["at_ptsb"], n + 1)
                if outs_before(n):
                    pe.wait_ge(sem["at_osb"], outs_before(n))
                acc = psum[:, O_BANK, 0:SEQ]
                if kind == "slc":
                    pe.matmul(acc, cmp_v[:, h // 4, :], cmp_pt[:, h, :], start=True, stop=False)
                for kt in range(NT):
                    ins = pe.matmul(acc, x[:, vb, kt, vc:vc + HD], prob_t[n % 2][:, kt, :],
                                    start=kind in ("band", "near") and kt == 0, stop=kind != "slc" and kt == 1)
                ins.then_inc(sem["at_o"], 1)

        first = [0]

        pe.wait_ge(sem["ident_in"], 16)
        norm_transposes(0, T_MIX1)
        row_blocks(S_IN1, R_IN1, IN1_BLOCKS, 8, ha, split_by(T_MIX1))
        for s in range(8 * GATE_BLOCKS):
            b, j = s // 8, s % 8
            g = R_GATE + b
            if j == 0:
                pe.wait_ge(row_free, g + 1)
            rows_step(S_GATE + s, 0, 0, ha, (2 * j, 2 * j + 1), g, j == 0, j == 7)
            head_stage(s % 4, s // 4, N1)
        for j in range(4):
            head_stage(j, N1, N1)
        pe.wait_ge(sem["at_osb"], N1)
        for n in range(4):
            for br in range(2):
                g = R_BRANCH + 2 * n + br
                pe.wait_ge(row_free, g + 1)
                for j in range(4):
                    if n == 0:
                        pe.wait_ge(sem["ot_lo"], 2 * br + j // 2 + 1)
                    rows_step(S_BRANCH + 8 * n + 4 * br + j, 0, 0, ha, (8 * br + 2 * j, 8 * br + 2 * j + 1), g,
                              j == 0, j == 3)
                if br == 0 and n:
                    pe.wait_ge(sem["merge_rows"], n)
                    for f in range(2):
                        transposes(T_MERGE + 2 * (n - 1) + f,
                                   lambda c, t: merged[(n - 1) % 2][:, t, (2 * f + c) * P:(2 * f + c + 1) * P])
        pe.wait_ge(sem["merge_rows"], 4)
        for f in range(2):
            transposes(T_MERGE + 6 + f, lambda c, t: merged[1][:, t, (2 * f + c) * P:(2 * f + c + 1) * P])
        row_blocks(S_OUT1, R_OUT1, 4, 8, hb, split_by(T_MERGE))
        norm_transposes(1, T_FFN1)

        def channel_blocks(step0, c0, n, ready, rows_before):
            pe.wait_ge(row_free, FREE + rows_before)
            with pe.Fori(0, n) as i:
                for v in range(2):
                    pe.wait_ge(chan_free, FREE + c0 + v - 1 + 2 * i)
                    for j in range(8):
                        if v == 0:
                            ready(j)
                        channel_step(step0 + 8 * v + j, i, 2, v, j)

        def hb_by(base, per_count):
            return lambda j: pe.wait_ge(sem["hb_lo"], base + (2 * j + 1) // 4 + 1)

        rows_before = R_DOWN1[0]
        for p, (j0, n) in enumerate(UP1_PASSES):
            pe.wait_ge(sem["tr_lo"], T_FFN1 + 8)
            channel_blocks(S_UP1[p], C_UP1[p], n, split_by(T_FFN1), rows_before)
            pe.wait_ge(chan_free, FREE + C_UP1[p] + 2 * n - 1)
            row_blocks(S_DOWN1[p], R_DOWN1[p], 4, 2 * n, hb, hb_by(j0, 4))
            rows_before = R_DOWN1[p] + 4

        norm_transposes(2, T_MIX2)

        def four_transposes(bank, src, rows=P):
            for c in range(2):
                for t in range(NT):
                    ins = pe.transpose(psum[0:rows, bank, SEQ * c + P * t:SEQ * c + P * t + P], src(c, t), ident[:])
            return ins

        def in2_step(s):
            b, j = s // 8, s % 8
            g = R_IN2 + b
            if j == 0:
                pe.wait_ge(row_free, g + 1)
            if b == 0:
                pe.wait_ge(sem["tr_lo"], T_MIX2 + j + 1)
            rows_step(S_IN2 + s, 0, 0, ha, (2 * j, 2 * j + 1), g, j == 0, j == 7)

        for s in range(8 * IN2_BLOCKS):
            in2_step(s)
            if s == 8:
                pe.wait_ge(sem["t5_in"], 80)
                pe.matmul(psum[0:8, 7, :], t5_tab[:], t5_up[:], start=True, stop=True).then_inc(sem["t5_mm"], 1)
                for c in range(4):
                    ins = pe.matmul(psum[:, 6, 8 * c:8 * c + 8], t5_up[:, P * c:P * c + P], t5_tab[:],
                                    start=True, stop=True)
                ins.then_inc(sem["t5_mm"], 1)
            if s == 10:
                pe.wait_ge(row_free, FREE + R_IN2 + 1)
                for f in range(2):
                    four_transposes(4 + f, lambda c, t: proj2[:, 2, t, (2 * f + c) * HD:(2 * f + c + 1) * HD]
                                    ).then_inc(sem["kvt_mm"], 1)
            if s == 12:
                pe.wait_ge(sem["wg_lo"], 1)
                pe.wait_ge(sem["t5_rows_ok"], 1)
                acc = psum[0:N_GATES, 7, :]
                for k in range(KC):
                    both = ha[:, k, :, :].rearrange("p a b -> p (a b)")
                    if k == 0:
                        pe.matmul(acc, w_gate_h[:, k, :], both, start=True, stop=False)
                    pe.matmul(acc[:, 0:SEQ], w_gate_l[:, k, :], ha[:, k, 0, :], start=False, stop=False)
                    if k:
                        ins = pe.matmul(acc, w_gate_h[:, k, :], both, start=False, stop=k == KC - 1)
                ins.then_inc(sem["gate_mm"], 1)
            if s in (15, 17):
                kv = (s - 15) // 2
                pe.wait_ge(w1_in[kv], 32)
                pe.wait_ge(sem["cin_ok"], kv + 1)
                pe.wait_ge(sem["kvt_ok"], kv + 1)
                for l in range(CMP_BLOCK):
                    ins = pe.matmul(psum[0:2 * NCMP, 4 + kv, 0:HD], cmp_in[:, kv, l, :, :].rearrange("p g n -> p (g n)"),
                                    w1[:, kv, l, :], start=l == 0, stop=l == CMP_BLOCK - 1)
                ins.then_inc(sem["hid_mm"], 1)
            if s == 16:
                pe.wait_ge(sem["gate_sum"], 1)
                pe.wait_ge(sem["t5_cols_ok"], 1)
                for t in range(NT):
                    ins = pe.transpose(psum[:, 6, N_GATES * t:N_GATES * (t + 1)], gate_t[:, P * t:P * t + P],
                                       ident[0:N_GATES, 0:N_GATES])
                ins.then_inc(sem["gate_tr"], 1)
            if s == 20:
                pe.wait_ge(sem["hid_copied"], 2)
                for kv in range(2):
                    ins = pe.transpose(psum[:, 7, 2 * NCMP * kv:2 * NCMP * (kv + 1)], hid_t[:, kv, :],
                                       ident[0:2 * NCMP, 0:2 * NCMP])
                ins.then_inc(sem["hid_tr"], 1)
            if s in (21, 26):
                i = (s == 26)
                pe.wait_ge(row_free, FREE + R_IN2 + 2 + i)
                if i:
                    pe.wait_ge(sem["qall_ok"], 2)
                for f in range(2):
                    four_transposes(4 + f, lambda c, t: proj2[:, i, t, (2 * f + c) * HD:(2 * f + c + 1) * HD]
                                    ).then_inc(sem["qall_mm"], 1)
            if s == 22:
                pe.wait_ge(sem["w2_in"], 32)
                pe.wait_ge(sem["hid_ok"], 2)
                pe.wait_ge(sem["gate_ok"], 1)
                pe.matmul(psum[:, 6, 0:2 * NCMP], w2[:, 0, :], cmp_hid[:, 0, :, :].rearrange("p g n -> p (g n)"),
                          start=True, stop=True).then_inc(sem["kv_mm"], 1)
                for g in range(2):
                    ins = pe.matmul(psum[0:NCMP, 6, SEQ + HD * g:SEQ + HD * g + HD], cmp_hid[:, 1, g, :], w2[:, 1, :],
                                    start=True, stop=True)
                ins.then_inc(sem["kv_mm"], 1)
            if s == 29:
                pe.wait_ge(sem["kv_ok"], 1)
                pe.wait_ge(sem["qall_ok"], 4)
                for h in range(8):
                    for t in range(NT):
                        c = (h * NT + t) * NCMP
                        ins = pe.matmul(psum[:, 7, c:c + NCMP], q_all[h // 4][:, h % 4, P * t:P * t + P],
                                        cmp_k[:, h // 4, :], start=True, stop=True)
                ins.then_inc(sem["cs_mm"], 1)
            if s == 34:
                pe.wait_ge(row_free, FREE + R_IN2 + 4)
                four_transposes(4, lambda c, t: proj2[:, 3, t, c * HD:(c + 1) * HD]).then_inc(sem["kall_mm"], 1)
            if s == 36:
                pe.wait_ge(sem["cs_p"], 1)
                pe.wait_ge(sem["kv_ok"], 2)
                for f in range(4):
                    if f == 3:
                        pe.wait_ge(sem["kall_ok"], 1)
                    four_transposes(4 + (f + 1) % 4, lambda c, t: cmp_p[:, 2 * f + c, t, :], NCMP).then_inc(sem["cpt_mm"], 1)
        first[0] = N1
        for s in range(8 * RET_BLOCKS):
            b, j = s // 8, s % 8
            g = R_RET + b
            if j == 0:
                pe.wait_ge(row_free, g + 1)
            rows_step(S_RET + s, 0, 0, ha, (2 * j, 2 * j + 1), g, j == 0, j == 7)
            if s == 1:
                pe.wait_ge(row_free, FREE + R_IN2 + IN2_BLOCKS)
                pe.wait_ge(sem["cpt_ok"], 4)
                four_transposes(4, lambda c, t: proj2[:, 4, t, c * HD:(c + 1) * HD]).then_inc(sem["kall_mm"], 1)
            head_stage(s % 4, N1 + s // 4, NH)
        for j in range(4):
            head_stage(j, NH, NH)
        pe.wait_ge(sem["at_osb"], outs_before(NH))

        def ret_transposes(r):
            for i, (mm, ok) in enumerate((("rq_mm", "rq_ok"), ("rk_mm", "rk_ok"))):
                pe.wait_ge(sem["rope_ok"], 4 * i + 2 * (r // 2) + 2)
                if r:
                    pe.wait_ge(sem[ok], r)
                for c in range(2):
                    for t in range(NT):
                        col = RET_D * (r % 2) + P * c
                        ins = pe.transpose(psum[:, 4 + i, SEQ * c + P * t:SEQ * c + P * t + P],
                                           ret[:, 2 * i + r // 2, t, col:col + P], ident[:])
                ins.then_inc(sem[mm], 1)

        ret_transposes(0)
        for r in range(RET_HEADS):
            pe.wait_ge(sem["rk_ok"], r + 1)
            pe.wait_ge(sem["rq_ok"], r + 1)
            if r:
                pe.wait_ge(sem["rp_ok"], r)
            for kt in range(NT):
                for c in range(2):
                    ins = pe.matmul(psum[:, 6, SEQ * kt:SEQ * kt + SEQ], ret_k[r % 2][:, c, P * kt:P * kt + P],
                                    ret_q[r % 2][:, c, :], start=c == 0, stop=c == 1)
            ins.then_inc(sem["rs_mm"], 1)
            if r + 1 < RET_HEADS:
                ret_transposes(r + 1)
            pe.wait_ge(sem["rp_ok"], r + 1)
            if r:
                pe.wait_ge(sem["ro_ok"], r)
            for t in range(NT):
                for kt in range(NT):
                    ins = pe.matmul(psum[:, 7, RET_D * t:RET_D * t + RET_D], ret_p[r % 2][:, kt, P * t:P * t + P],
                                    ret[:, 4 + r // 2, kt, RET_D * (r % 2):RET_D * (r % 2) + RET_D],
                                    start=kt == 0, stop=kt == 1)
            ins.then_inc(sem["ro_mm"], 1)
        pe.wait_ge(sem["ro_ok"], RET_HEADS)
        for f in range(4):
            transposes(T_RETO + f, lambda c, t: ret_o[:, t, (2 * f + c) * P:(2 * f + c + 1) * P])

        def mix_ready(j):
            if j < 4:
                pe.wait_ge(sem["ot_lo"], 4 + j // 2 + 1)
            else:
                pe.wait_ge(sem["tr_lo"], T_RETO + j - 4 + 1)

        row_blocks(S_OUT2, R_OUT2, 4, 8, ha, mix_ready)
        norm_transposes(4, T_MLP2)
        rows_before = R_OUT2 + 4
        pe.wait_ge(sem["tr_lo"], T_MLP2 + 8)
        for p in range(UP2_PASSES):
            channel_blocks(S_UP2[p], C_UP2[p], 2, split_by(T_MLP2), rows_before)
            pe.wait_ge(chan_free, FREE + C_UP2[p] + 3)
            row_blocks(S_DOWN2[p], R_DOWN2[p], 4, 8, hb, hb_by(11 + 4 * p, 4))
            rows_before = R_DOWN2[p] + 4

    block.__exit__(None, None, None)


CONST_SHAPES = shape_constants()
DRAM_INPUTS = ["x", "w_in", "a_q_norm", "a_k_norm", "a_sink", "b_rpb", "w_branch_a", "w_branch_b", "w_out", "w_up",
               "w_down", "w_in_2", "cmp_w1_k_2", "cmp_w2_k_2", "cmp_w1_v_2", "cmp_w2_v_2", "t5_bias_2", "w_out_2",
               "norm_mix_post_2", "w_up_2", "w_down_2", "norm_mlp_post_2"]


def kernel(**inputs):
    import concourse.bacc as bacc
    from concourse.bass_utils import run_bass_kernel_spmd

    nc = bacc.Bacc("TRN2", target_bir_lowering=False, num_devices=1, dynamic_dma_scratch_size=1024)
    arrays = {n: np.ascontiguousarray(inputs[n]) for n in DRAM_INPUTS}
    arrays["b_rpb"] = np.ascontiguousarray(arrays["b_rpb"][:, :, ::-1, ::-1])
    arrays.update(CONST_SHAPES)
    arrays["params"] = pack_columns(inputs)
    aps = {n: nc.dram_tensor(f"in_{n}", v.shape, mybir.dt.from_np(v.dtype), kind="ExternalInput").ap()
           for n, v in arrays.items()}
    out = nc.dram_tensor("out", (1, SEQ, D), F32, kind="ExternalOutput").ap()
    scratch = nc.dram_tensor("distance_rows", (8, 512), F32, kind="Internal").ap()
    scratch_cols = nc.dram_tensor("distance_columns", (512, 8), F32, kind="Internal").ap()
    build(nc, aps, out, scratch, scratch_cols)
    r = run_bass_kernel_spmd(nc, [{f"in_{n}": v for n, v in arrays.items()}], core_ids=[0])
    return r.results[0]["out"]
```

```python
import math

import numpy as np

import concourse.bass as bass
from concourse import mybir

F32 = mybir.dt.float32
F32R = mybir.dt.float32r
ACT = mybir.ActivationFunctionType
ALU = mybir.AluOpType
AX = mybir.AxisListType

P = 128
SEQ = 256
NT = SEQ // P
D = 2048
KC = D // P
DFF1 = 5632
DFF2 = 8192
EPS = 1e-6
NEG = -1e30
HD = 128
SCALE = 1.0 / math.sqrt(HD)
COLS = 512
RAW_SLOTS = 4
SPLIT_SLOTS = 4
AHEAD = 3

IN1_BLOCKS = 9
GATE_BLOCKS = 8
IN2_BLOCKS = 5
IN2_ORDER = [2, 0, 1, 3, 4]
RET_BLOCKS = 8
N_GATES = 24
RET_HEADS, RET_D = 4, 256
NCMP, CMP_BLOCK, CMP_STRIDE = 15, 32, 16
UP1_PASSES = [(0, 4), (4, 4), (8, 3)]
UP2_PASSES = 4
T5_BUCKETS = 32

S_IN1 = 0
S_GATE = S_IN1 + 8 * IN1_BLOCKS
S_BRANCH = S_GATE + 8 * GATE_BLOCKS
S_OUT1 = S_BRANCH + 8 * 4
S_FF1 = S_OUT1 + 8 * 4
S_UP1, S_DOWN1 = [], []
_s = S_FF1
for _, _n in UP1_PASSES:
    S_UP1.append(_s)
    _s += 16 * _n
    S_DOWN1.append(_s)
    _s += 8 * _n
S_IN2 = _s
S_RET = S_IN2 + 8 * IN2_BLOCKS
S_OUT2 = S_RET + 8 * RET_BLOCKS
S_UP2, S_DOWN2 = [], []
_s = S_OUT2 + 8 * 4
for _ in range(UP2_PASSES):
    S_UP2.append(_s)
    S_DOWN2.append(_s + 32)
    _s += 64
N_STEPS = _s

R_IN1 = 0
R_GATE = R_IN1 + IN1_BLOCKS
R_BRANCH = R_GATE + GATE_BLOCKS
R_OUT1 = R_BRANCH + 8
R_DOWN1 = [R_OUT1 + 4 + 4 * i for i in range(3)]
R_IN2 = R_DOWN1[-1] + 4
R_RET = R_IN2 + IN2_BLOCKS
R_OUT2 = R_RET + RET_BLOCKS
R_DOWN2 = [R_OUT2 + 4 + 4 * i for i in range(UP2_PASSES)]
C_UP1 = [0, 8, 16]
C_UP2 = [22 + 4 * i for i in range(UP2_PASSES)]

T_MIX1, T_MERGE, T_FFN1, T_MIX2, T_RETO, T_MLP2 = 0, 8, 16, 24, 32, 36

Q_GAIN = {"mix1": 0, "ffn1": 16, "mix2": 32, "mlp2": 48}
Q_BQ, Q_BK = 64, 65
Q_CONVW = 66
Q_CONVB = Q_CONVW + 3 * 88
Q_B1K = Q_CONVB + 88
Q_B1V = Q_B1K + 1
Q_PEK = Q_B1V + 1
Q_PEV = Q_PEK + CMP_BLOCK
Q_COLS = Q_PEV + CMP_BLOCK

SLOT = 3
RET_START = SLOT * 17

FREE = 2

KB = 1024


class Chain:

    def __init__(self, eng, sem):
        self.eng, self.sem, self.n, self.past = eng, sem, 0, 0

    def enter(self, i, links):
        self.past, self.start, self.links = i * links, self.n, links

    def leave(self, passes):
        assert self.n - self.start == self.links, (self.n - self.start, self.links)
        self.n, self.past = self.start + self.links * passes, 0

    def link(self, ins):
        self.n += 1
        ins.then_inc(self.sem, 1)
        self.eng.wait_ge(self.sem, self.past + self.n)


def shape_constants():
    f = np.float32
    q = np.arange(SEQ)
    k = np.arange(SEQ)
    c = {}
    c["ident"] = np.eye(P, dtype=f)

    def tiles(m):
        return np.ascontiguousarray(m.reshape(NT, P, -1).transpose(1, 0, 2))

    band = np.where(np.abs(q[:, None] - k[None, :]) <= 128, 0.0, NEG).astype(f)
    c["band"] = tiles(band)
    qc, kc = q % 64, k % 64
    cs = np.clip(qc - 8, 0, 48)
    near = (kc[None, :] >= cs[:, None]) & (kc[None, :] < cs[:, None] + 16)
    c["near"] = np.ascontiguousarray(tiles(np.where(near, 0.0, NEG).astype(f))[:, ::-1, ::-1])

    def rope(half):
        inv = f(10000.0) ** (-np.arange(half, dtype=f) * f(1.0 / half))
        ang = (q.astype(f)[:, None] * inv[None, :].astype(f)).astype(f)
        return tiles(np.cos(ang).astype(f)), tiles(np.sin(ang).astype(f))

    c["cos1"], c["sin1"] = rope(64)
    c["cos2"], c["sin2"] = rope(128)
    def bucket(rel):
        n = np.maximum(rel, 0)
        nf = np.maximum(n, 1).astype(f)
        large = 16 + (np.log(nf / f(16)) / np.log(128 / 16) * 16).astype(np.int32)
        return np.where(n < 16, n, np.minimum(large, 31))

    up = np.arange(-256, 256)
    c["t5_up"] = (bucket(up)[None, :] == np.arange(32)[:, None]).astype(f)
    c["t5_ahead"] = np.broadcast_to(np.where(up >= 0, 0.0, NEG).astype(f), (8, 512)).copy()
    n = np.arange(NCMP)
    ok = (q[:, None] - (n * CMP_STRIDE + CMP_BLOCK - 1)[None, :]) >= 0
    c["cmp_mask"] = tiles(np.where(ok, 0.0, NEG).astype(f))
    c["cmp_seen"] = tiles(ok.astype(f))
    lg = np.log(1.0 - 2.0 ** (-5.0 - np.arange(RET_HEADS)))
    diff = (q[None, :] - k[:, None]).astype(np.float64)
    decay = np.where(diff >= 0, np.exp(np.maximum(diff, 0)[None] * lg[:, None, None]), 0.0)
    decay = decay * RET_D ** -0.5
    c["decay"] = np.ascontiguousarray(
        decay.reshape(RET_HEADS, NT, P, SEQ).transpose(2, 0, 1, 3)).astype(f)
    return c


CONST_NAMES = ["ident", "band", "near", "cos1", "sin1", "cos2", "sin2", "t5_up", "t5_ahead",
               "cmp_mask", "cmp_seen", "decay"]


def pack_columns(a):
    def cols(v):
        return np.asarray(v).reshape(-1, P).T

    conv = np.asarray(a["conv_w"])[0].reshape(3, 88, P).transpose(2, 1, 0).reshape(P, 88 * 3)
    parts = [cols(a["norm_mix"]), cols(a["norm_ffn"]), cols(a["norm_mix_pre_2"]), cols(a["norm_mlp_pre_2"]),
             cols(a["b_q_norm"]), cols(a["b_k_norm"]), conv, cols(a["conv_b"]),
             cols(a["cmp_b1_k_2"]), cols(a["cmp_b1_v_2"]),
             np.asarray(a["cmp_pe_k_2"])[0].T, np.asarray(a["cmp_pe_v_2"])[0].T]
    return np.ascontiguousarray(np.concatenate(parts, axis=1))


def build(nc, a, out, scratch, scratch_cols):
    base = (nc.sbuf_base + 1023) // 1024 * 1024

    def at(name, shape, kb, dt=F32):
        return nc.alloc_sbuf_tensor_at(name, shape, dt, offset=int(base + kb * KB))

    x_rows = at("x_rows", [P, NT, D], 0)
    ot = at("ot", [P, KC, SEQ], 0)
    raw = [at(f"raw{i}", [P, 4, COLS], 16 + 8 * i) for i in range(RAW_SLOTS)]
    wh = [at(f"wh{i}", [P, 2, COLS], 48 + 4 * i, F32R) for i in range(SPLIT_SLOTS)]
    wl = [at(f"wl{i}", [P, 2, COLS], 64 + 4 * i, F32R) for i in range(SPLIT_SLOTS)]
    ha = at("ha", [P, KC, 2, SEQ], 80, F32R)
    hb = at("hb", [P, KC, 2, SEQ], 112, F32R)
    proj = at("proj", [P, IN1_BLOCKS, NT, COLS], 112)
    gates = at("gates", [P, GATE_BLOCKS, NT, COLS], 148)
    rot_a = at("rot_a", [P, 2, NT, HD], 180)
    rot_b = at("rot_b", [P, 2, NT, HD], 182)
    cos1 = at("cos1", [P, NT, 64], 184)
    sin1 = at("sin1", [P, NT, 64], 184.5)
    a_gain = at("a_gain", [P, 2, HD], 185)
    band = at("band", [P, NT, SEQ], 186)
    near = at("near", [P, NT, SEQ], 188)
    merged = [at(f"merged{i}", [P, NT, COLS], 180 + 4 * i) for i in range(2)]
    bias = [at(f"bias{i}", [P, NT, SEQ], 190 + 2 * i) for i in range(2)]
    qk_t = [at(f"qk_t{i}", [P, 2, SEQ], 194 + 2 * i) for i in range(2)]
    sco = [at(f"sco{i}", [P, NT, SEQ], 198 + 2 * i) for i in range(2)]
    prob = [at(f"prob{i}", [P, NT, SEQ], 202 + 2 * i) for i in range(2)]
    prob_t = [at(f"prob_t{i}", [P, NT, SEQ], 206 + 2 * i) for i in range(2)]
    tmp_a = at("tmp_a", [P, 4, HD], 210)
    tmp_b = at("tmp_b", [P, 4, HD], 212)
    rows = at("rows", [P, NT, D], 148)
    u_pad = [at(f"u_pad{i}", [P, 4, SEQ + 2], 164 + 4.25 * i) for i in range(2)]
    conv = [at(f"conv{i}", [P, 4, SEQ], 173 + 4 * i) for i in range(2)]
    act_f = at("act_f", [P, 4, SEQ], 181)
    u_sum = at("u_sum", [P, 4, SEQ], 164)
    u_act = at("u_act", [P, 4, SEQ], 168)
    y_rows = rows
    gain_row = at("gain_row", [P, D], 184)
    proj2 = at("proj2", [P, IN2_BLOCKS, NT, COLS], 148)
    ret = at("ret", [P, RET_BLOCKS, NT, COLS], 112)
    w1 = at("w1", [P, 2, CMP_BLOCK, HD], 112)
    w_gate = at("w_gate", [P, KC, N_GATES], 144)
    w_gate_h = at("w_gate_h", [P, KC, N_GATES], 145.5, F32R)
    w_gate_l = at("w_gate_l", [P, KC, N_GATES], 186, F32R)
    mix_t = at("mix_t", [P, 8, SEQ], 168)
    w2 = at("w2", [P, 2, HD], 176)
    cmp_bias = at("cmp_bias", [P, 8, NT, NCMP], 177)
    cmp_mask = at("cmp_mask", [P, NT, NCMP], 178)
    cmp_seen = at("cmp_seen", [P, NT, NCMP], 178.25)
    t5_tab = at("t5_tab", [T5_BUCKETS, 8], 178.5)
    gate24 = at("gate24", [P, NT, N_GATES], 178.75)
    kv_cmp_t = at("kv_cmp_t", [P, 4, SEQ], 180)
    cmp_in = at("cmp_in", [P, 2, CMP_BLOCK, 2, NCMP], 198)
    cmp_hid = at("cmp_hid", [P, 2, 2, NCMP], 184)
    hid_t = at("hid_t", [2 * NCMP, 2, HD], 147)
    gate_t = at("gate_t", [N_GATES, SEQ], 189)
    t5_cols = at("t5_cols", [P, 4, 8], 179.75)
    cmp_dist = at("cmp_dist", [P, 23, 8], 179)
    cmp_k = at("cmp_k", [P, 2, NCMP], 185.5)
    cmp_v = at("cmp_v", [NCMP, 2, HD], 188)
    q_all = [at(f"q_all{i}", [P, 4, SEQ], kb) for i, kb in enumerate((156, 210))]
    k_all = at("k_all", [P, 4, SEQ], 194)
    t5_up = at("t5_up", [T5_BUCKETS, 512], 190)
    t5_ahead = at("t5_ahead", [8, 512], 194)
    t5_rows = at("t5_rows", [8, 512], 196)
    cmp_s = at("cmp_s", [P, 8, NT, NCMP], 144)
    cmp_p = at("cmp_p", [P, 8, NT, NCMP], 145)
    cmp_m = at("cmp_m", [P, 8, NT], 146)
    cmp_n = at("cmp_n", [P, 8, NT], 146.25)
    cmp_pt = at("cmp_pt", [NCMP, 8, SEQ], 180)
    cos2 = at("cos2", [P, NT, HD], 144)
    sin2 = at("sin2", [P, NT, HD], 145)
    decay = at("decay", [P, RET_HEADS, NT, SEQ], 148)
    ret_q = [at(f"ret_q{i}", [P, 2, SEQ], 192 + 2 * i) for i in range(2)]
    ret_k = [at(f"ret_k{i}", [P, 2, SEQ], 196 + 2 * i) for i in range(2)]
    ret_p = [at(f"ret_p{i}", [P, NT, SEQ], 200 + 2 * i) for i in range(2)]
    rt = [at(f"rt{i}", [P, 2, HD], kb) for i, kb in enumerate((146, 218, 219, 220))]
    ret_o = at("ret_o", [P, NT, 1024], 156)
    small = 214
    ident = at("ident", [P, P], small)
    par = at("par", [P, Q_COLS], small + 0.5)
    sums = at("sums", [P, 16], small + 2.5)
    rstd = at("rstd", [P, 16], small + 2.5625)
    neghalf = at("neghalf", [P, 32], small + 2.625)
    ssq = at("ssq", [P, 32], small + 2.75)
    rsq = at("rsq", [P, 32], small + 2.875)
    sink = at("sink", [P, 8], small + 3)
    mx = at("mx", [P, 2, NT], small + 3.0625)
    nmx = at("nmx", [P, 2, NT], small + 3.09375)
    den = at("den", [P, 2, NT], small + 3.125)
    esink = at("esink", [P, 2, NT], small + 3.15625)
    rden = at("rden", [P, 2, NT], small + 3.1875)
    bst = at("bst", [P, 2, NT, 6], small + 3.25)
    bag = at("bag", [P, 2, NT, 2], small + 3.375)
    grs = at("grs", [P, 2, NT], small + 3.40625)
    ssb = at("ssb", [P, 2, 4], small + 3.4375)
    squares = at("squares", [P, COLS], 218)
    part = at("part", [P, 6, NT, 4], small + 3.625)
    pairs = at("pairs", [P, NT, 2], small + 3.8125)
    rstd_row = at("rstd_row", [P, SEQ], 200)
    rstd_diag = at("rstd_diag", [P, NT, P], 202)
    ones = at("ones", [P, P], 204)
    unused = at("unused", [P, 4], small + 3.5625)
    rsb = at("rsb", [P, 2, 4], small + 3.5)


    psum = nc.alloc_psum_tensor("psum", [P, 8, COLS], F32)

    names = """
      par_in ident_in cos1_in sin1_in again_in band_in near_in sink_in xre_in
      hi_done lo_done mm_done row_free chan_free
      act_chain dve_chain pool_chain consts_set
      norm_ss norm_rs tr_full tr_hi tr_lo diag_ok rstd_row_mm rstd_row_ok gained
      an_ss an_rs a_ready bn_ss bn_rs bn_ok
      bias_ok at_qk at_qksb at_sc at_s at_nm at_p at_pn at_pt at_ptsb at_o at_osb
      sig_done merge_rows ot_hi ot_lo
      half_ok u_scaled tap_done conv_mid conv_done silu_done act_ready hb_hi hb_lo usum_done

      wg_in wg_hi wg_lo gate_mm gate_half gate_sum gate_tr gate_ok
      t5_in t5_mm t5_rows_ok t5_cols_ok t5_st cmp_dist_in hid_copied hid_tr kall_mm kall_ok
      kvt_mm kvt_ok qall_mm qall_ok cin_ok w2_in hid_mm hid_ok kv_mm kv_ok
      cs_mm cs_ok cs_exp cs_p cpt_mm cpt_ok
      rtab_in rope_ok silu_g rq_mm rq_ok rk_mm rk_ok rs_mm rp_ok ro_mm ro_stat ro_rs ro_ok ro_gated
      post_ok grow_in out_in cmask_in
    """.split()
    sem = {n: nc.alloc_semaphore(n) for n in names}
    raw_in = [nc.alloc_semaphore(f"raw_in{i}") for i in range(RAW_SLOTS)]
    bias_in = [nc.alloc_semaphore(f"bias_in{i}") for i in range(2)]
    t5_bias_in = [nc.alloc_semaphore(f"t5_bias_in{i}") for i in range(2)]

    x_in = [nc.alloc_semaphore(f"x_in{i}") for i in range(4)]
    w1_in = [nc.alloc_semaphore(f"w1_in{i}") for i in range(2)]

    (hi_done, lo_done, mm_done, row_free, chan_free) = (
        sem[n] for n in ("hi_done", "lo_done", "mm_done", "row_free", "chan_free"))

    heads = []
    for h in range(8):
        heads.append(("band", h, proj, (h // 4, h % 4 * HD), (2, h // 4 * HD), (2, 256 + h // 4 * HD)))
    for h in range(8):
        heads.append(("near", h, proj, (3 + h // 4, h % 4 * HD), (5 + h // 4, h % 4 * HD),
                      (7 + h // 4, h % 4 * HD)))
    for h in range(8):
        for b, blk in (("slc", 3), ("win", 4)):
            heads.append((b, h, proj2, (h // 4, h % 4 * HD), (blk, h // 4 * HD), (blk, 256 + h // 4 * HD)))
    N1, NH = 16, len(heads)

    def outs_before(n):
        return n if n <= N1 else N1 + (n - N1) // 2

    QK_BANK, SC_BANK, PT_BANK, O_BANK = 4, 5, 6, 7

    block = nc.Block()
    block.__enter__()

    @block.sync
    def _(sp):
        def view(name):
            return a[name].rearrange("o (k p) n -> p (o k) n", p=P)

        def weight_load(u, i, src):
            if u >= RAW_SLOTS:
                sp.wait_ge(lo_done, 2 * (u - RAW_SLOTS) + 2 + 8 * i)
            sp.dma_start(raw[u % RAW_SLOTS][:], src).then_inc(raw_in[u % RAW_SLOTS], 16)

        def column_blocks(step, name, k0, groups, col, n):
            w = view(name)
            if groups == 4:
                with sp.Fori(0, n) as i:
                    for j in range(4):
                        weight_load(step // 2 + j, i, w[:, k0 + 4 * j:k0 + 4 * j + 4,
                                                        bass.ds(i * COLS + col, COLS)])
            else:
                for b in range(n):
                    for j in range(groups):
                        weight_load(step // 2 + groups * b + j, 0,
                                    w[:, k0 + 4 * j:k0 + 4 * j + 4, col + b * COLS:col + (b + 1) * COLS])

        x_view = a["x"].rearrange("o (t p) n -> p (o t) n", p=P)
        w_in = view("w_in")
        for c in range(4):
            cols = slice(c * COLS, (c + 1) * COLS)
            sp.dma_start(x_rows[:, :, cols], x_view[:, :, cols]).then_inc(x_in[c], 16)
            if c == 0:
                sp.dma_start(ident[:], a["ident"]).then_inc(sem["ident_in"], 16)
                sp.dma_start(par[:], a["params"]).then_inc(sem["par_in"], 16)
            weight_load(c, 0, w_in[:, 4 * c:4 * c + 4, 0:COLS])
        for i, g in enumerate(("a_q_norm", "a_k_norm")):
            sp.dma_start(a_gain[:, i, :], bass.AP(a[g].tensor, 0, [[0, P], [1, HD]])).then_inc(sem["again_in"], 16)
        sp.dma_start(cos1[:], a["cos1"]).then_inc(sem["cos1_in"], 16)
        sp.dma_start(sin1[:], a["sin1"]).then_inc(sem["sin1_in"], 16)
        sp.dma_start(band[:], a["band"]).then_inc(sem["band_in"], 16)
        sp.dma_start(near[:], a["near"]).then_inc(sem["near_in"], 16)
        sp.dma_start(sink[:], bass.AP(a["a_sink"].tensor, 0, [[0, P], [1, 8]])).then_inc(sem["sink_in"], 16)

        def near_bias(h):
            if h >= 2:
                sp.wait_ge(sem["at_s"], 8 + h - 2 + 1)
            for t in range(NT):
                for r in range(2):
                    off = h * 15 * 31 + (4 + 2 * t + r) * 31 - 48
                    src = bass.AP(a["b_rpb"].tensor, off, [[1, 64], [31, 4], [1, 64]])
                    sp.dma_start(bias[h % 2][64 * r:64 * r + 64, 1 - t, :].rearrange("p (a c) -> p a c", a=4),
                                 src).then_inc(bias_in[h % 2], 16)

        near_bias(0)
        near_bias(1)
        column_blocks(8, "w_in", 0, 4, COLS, IN1_BLOCKS - 1)
        for u in range(4 * GATE_BLOCKS):
            b, j = u // 4, u % 4
            if u >= 2 * 8 + 7 and (u - 23) % 2 == 0 and (u - 23) // 2 + 2 < 8:
                near_bias((u - 23) // 2 + 2)
            weight_load(S_GATE // 2 + u, 0, w_in[:, 4 * j:4 * j + 4,
                                                 (IN1_BLOCKS + b) * COLS:(IN1_BLOCKS + b + 1) * COLS])
        near_bias(7)
        wa, wb = view("w_branch_a"), view("w_branch_b")
        with sp.Fori(0, 4) as i:
            for j in range(4):
                w = (wa, wb)[j // 2]
                weight_load(S_BRANCH // 2 + j, i, w[:, 4 * (j % 2):4 * (j % 2) + 4, bass.ds(i * COLS, COLS)])
        sp.wait_ge(sem["ot_lo"], 8)
        sp.dma_start(x_rows[:], x_view).then_inc(sem["xre_in"], 16)
        column_blocks(S_OUT1, "w_out", 0, 4, 0, 4)
        wu = view("w_up")
        for (j0, n), su, sd in zip(UP1_PASSES, S_UP1, S_DOWN1):
            with sp.Fori(0, n) as i:
                for j in range(8):
                    col = (j // 4) * DFF1 + j0 * COLS
                    u = su // 2 + j
                    sp.wait_ge(lo_done, 2 * (u - RAW_SLOTS) + 2 + 16 * i)
                    sp.dma_start(raw[u % RAW_SLOTS][:], wu[:, 4 * (j % 4):4 * (j % 4) + 4,
                                                           bass.ds(i * COLS + col, COLS)]
                                 ).then_inc(raw_in[u % RAW_SLOTS], 16)
            column_blocks(sd, "w_down", 4 * j0, n, 0, 4)
        w_in2 = view("w_in_2")

        def in2_load(u):
            c0 = IN2_ORDER[u // 4] * COLS
            weight_load(S_IN2 // 2 + u, 0, w_in2[:, 4 * (u % 4):4 * (u % 4) + 4, c0:c0 + COLS])

        for u in range(4):
            in2_load(u)
        sp.wait_ge(mm_done, S_IN2)
        sp.dma_start(w_gate[:], a["w_in_2"].rearrange("o (k p) n -> p (o k) n", p=P)
                     [:, :, IN2_BLOCKS * COLS:IN2_BLOCKS * COLS + N_GATES]).then_inc(sem["wg_in"], 16)
        sp.dma_start(t5_tab[:], a["t5_bias_2"]).then_inc(sem["t5_in"], 16)
        sp.dma_start(t5_up[:], a["t5_up"]).then_inc(sem["t5_in"], 16)
        sp.dma_start(t5_ahead[:], a["t5_ahead"]).then_inc(sem["t5_in"], 16)
        sp.dma_start(cmp_mask[:], a["cmp_mask"]).then_inc(sem["t5_in"], 16)
        sp.dma_start(cmp_seen[:], a["cmp_seen"]).then_inc(sem["t5_in"], 16)
        w1_views = [a[n].rearrange("o (l p) n -> p (o l) n", p=P) for n in ("cmp_w1_k_2", "cmp_w1_v_2")]
        for u in range(4, 4 * IN2_BLOCKS):
            in2_load(u)
            if u < 8:
                kv, l = (u - 4) // 2, CMP_BLOCK // 2 * (u % 2)
                sp.dma_start(w1[:, kv, l:l + CMP_BLOCK // 2, :], w1_views[kv][:, l:l + CMP_BLOCK // 2, :]
                             ).then_inc(w1_in[kv], 16)
            if u == 8:
                sp.dma_start(w2[:, 0, :], a["cmp_w2_k_2"][0]).then_inc(sem["w2_in"], 16)
                sp.dma_start(w2[:, 1, :], a["cmp_w2_v_2"][0]).then_inc(sem["w2_in"], 16)
            if u == 11:
                sp.wait_ge(sem["t5_rows_ok"], 1)
                sp.dma_start(scratch, t5_rows[:]).then_inc(sem["t5_st"], 16)
                sp.wait_ge(sem["t5_cols_ok"], 1)
                sp.dma_start(scratch_cols.rearrange("(c p) h -> p c h", p=P), t5_cols[:]).then_inc(sem["t5_st"], 16)
            if u == 12:
                sp.wait_ge(sem["t5_st"], 32)
                sp.dma_start(cmp_dist[:], bass.AP(scratch_cols.tensor, 8, [[8, P], [128, 23], [1, 8]])
                             ).then_inc(sem["cmp_dist_in"], 16)

        def retention_load(u):
            c0 = IN2_BLOCKS * COLS + N_GATES + u // 4 * COLS
            weight_load(S_RET // 2 + u, 0, w_in2[:, 4 * (u % 4):4 * (u % 4) + 4, c0:c0 + COLS])

        for u in range(4):
            retention_load(u)

        def t5_bias(h):
            if h >= 2:
                sp.wait_ge(sem["at_s"], N1 + 2 * (h - 2) + 2)
            else:
                sp.wait_ge(sem["t5_mm"], 2)
            for t in range(NT):
                src = bass.AP(scratch.tensor, 512 * h + P * t + 1, [[1, P], [1, SEQ]])
                sp.dma_start(bias[h % 2][:, 1 - t, :], src).then_inc(t5_bias_in[h % 2], 16)

        t5_bias(0)
        t5_bias(1)
        sp.wait_ge(sem["cpt_mm"], 4)
        sp.dma_start(cos2[:], a["cos2"]).then_inc(sem["rtab_in"], 16)
        sp.dma_start(sin2[:], a["sin2"]).then_inc(sem["rtab_in"], 16)
        sp.dma_start(decay[:], a["decay"]).then_inc(sem["rtab_in"], 16)
        for u in range(4, 4 * RET_BLOCKS):
            if u >= 9 and (u - 9) % 3 == 0 and (u - 9) // 3 + 2 < 8:
                t5_bias((u - 9) // 3 + 2)
            retention_load(u)
        w_out2 = view("w_out_2")
        for j in range(4):
            weight_load(S_OUT2 // 2 + j, 0, w_out2[:, 4 * j:4 * j + 4, 0:COLS])
        sp.wait_ge(sem["at_osb"], outs_before(NH))
        sp.dma_start(gain_row[:], bass.AP(a["norm_mix_post_2"].tensor, 0, [[0, P], [1, D]])
                     ).then_inc(sem["grow_in"], 16)
        column_blocks(S_OUT2 + 8, "w_out_2", 0, 4, COLS, 3)
        for p in range(UP2_PASSES):
            column_blocks(S_UP2[p], "w_up_2", 0, 4, 4 * p * COLS, 4)
            if p == UP2_PASSES - 1:
                sp.wait_ge(sem["gained"], 4)
                sp.dma_start(gain_row[:], bass.AP(a["norm_mlp_post_2"].tensor, 0, [[0, P], [1, D]])
                             ).then_inc(sem["grow_in"], 16)
            column_blocks(S_DOWN2[p], "w_down_2", 16 * p, 4, 0, 4)
        o = out.rearrange("o (t p) n -> p (o t) n", p=P)
        for c in range(4):
            sp.wait_ge(sem["post_ok"], 4 + c + 1)
            cols = slice(c * COLS, (c + 1) * COLS)
            sp.dma_start(o[:, :, cols], x_rows[:, :, cols]).then_inc(sem["out_in"], 16)
        sp.wait_ge(sem["out_in"], 16 * 4)

    @block.gpsimd
    def _(pool):
        chain = Chain(pool, sem["pool_chain"])
        pool.memset(neghalf[:], -0.5).then_inc(sem["consts_set"], 1)
        for i in range(FREE):
            pool.memset(unused[:, i:i + 1], 0.0).then_inc(row_free, 1)
            pool.memset(unused[:, 2 + i:3 + i], 0.0).then_inc(chan_free, 1)
        pool.wait_ge(sem["consts_set"], 1)

        def inverse_root(dst, src, scale, n, done):
            chain.link(pool.tensor_scalar(dst, src, scale, EPS, ALU.mult, ALU.add))
            pool.tensor_tensor(dst, dst, neghalf[:, 0:n], ALU.pow).then_inc(done, 1)

        def norm(n):
            pool.wait_ge(sem["norm_ss"], 8 * n + 8)
            chain.link(pool.tensor_tensor(pairs[:], part[:, n, :, 0:2], part[:, n, :, 2:4], ALU.add))
            chain.link(pool.tensor_tensor(sums[:, 2 * n:2 * n + 2], pairs[:, :, 0], pairs[:, :, 1], ALU.add))
            inverse_root(rstd[:, 2 * n:2 * n + 2], sums[:, 2 * n:2 * n + 2], 1.0 / D, 2, sem["norm_rs"])

        norm(0)
        pool.wait_ge(sem["an_ss"], 1)
        inverse_root(rsq[:, 0:24], ssq[:, 0:24], 1.0 / HD, 24, sem["an_rs"])
        pool.wait_ge(sem["near_in"], 16)

        def masked_bias(h):
            pool.wait_ge(bias_in[h % 2], 64 * (h // 2 + 1))
            pool.tensor_tensor(bias[h % 2][:], bias[h % 2][:], near[:], ALU.add).then_inc(sem["bias_ok"], 1)

        masked_bias(0)
        masked_bias(1)
        for h in range(8):
            pool.wait_ge(sem["bn_ss"], h + 1)
            inverse_root(rsb[:, h % 2, :], ssb[:, h % 2, :], 1.0 / HD, 4, sem["bn_rs"])
        for h in range(2, 8):
            masked_bias(h)
        norm(1)
        for p in range(2):
            pool.memset(u_pad[p][:, :, 0:1], 0.0).then_inc(sem["cmask_in"], 1)
            pool.memset(u_pad[p][:, :, SEQ + 1:SEQ + 2], 0.0).then_inc(sem["cmask_in"], 1)
        norm(2)
        for r in range(RET_HEADS):
            pool.wait_ge(sem["ro_stat"], r + 1)
            inverse_root(grs[:, r % 2, :], bag[:, r % 2, :, 1], 1.0, 2, sem["ro_rs"])
        for n in (3, 4, 5):
            norm(n)

    @block.scalar
    def _(act):
        chain = Chain(act, sem["act_chain"])

        def ahead(step, i=0, m=0):
            q = step + AHEAD
            act.wait_ge(raw_in[q // 2 % RAW_SLOTS], 16 * (q // 8 + 1) + 16 * m * i)
            if q >= SPLIT_SLOTS:
                act.wait_ge(mm_done, q - SPLIT_SLOTS + 1 + 8 * m * i)
            act.activation(wh[q % SPLIT_SLOTS][:], raw[q // 2 % RAW_SLOTS][:, 2 * (q % 2):2 * (q % 2) + 2, :],
                           ACT.Copy).then_inc(hi_done, 1)

        def row_blocks(step0, g0, n, per, evac, extra=None):
            if per != 8 or extra:
                for b in range(n):
                    for j in range(per):
                        ahead(step0 + per * b + j)
                        if extra:
                            extra(b, j)
                    evac(b, g0 + b, step0 + per * (b + 1), 0, 0)
                return
            if n % 2:
                for j in range(8):
                    ahead(step0 + j)
                evac(0, g0, step0 + 8, 0, 0)
            with act.Fori(0, n // 2) as i:
                for b in (n % 2, n % 2 + 1):
                    for j in range(8):
                        ahead(step0 + 8 * b + j, i, 2)
                    evac(b, g0 + b, step0 + 8 * (b + 1), i, 2)

        def copy_rows(dst, n, b0=0):
            def evac(b, g, end, i, m):
                act.wait_ge(mm_done, end + 8 * m * i)
                for t in range(NT):
                    ins = act.activation(dst[:, b + b0 + m * i, t, :], psum[:, 2 * (g % 2) + t, :], ACT.Copy,
                                         scale=rstd[:, 2 * n + t:2 * n + t + 1])
                ins.then_inc(row_free, 1)
            return evac

        def no_evac(b, g, end, i, m):
            pass

        def sum_squares(n, src, c):
            for t in range(NT):
                if 8 * n + 2 * c + t:
                    act.wait_ge(sem["norm_ss"], 8 * n + 2 * c + t)
                act.activation(squares[:], src[:, t, c * COLS:(c + 1) * COLS], ACT.Square,
                               accum_out=part[:, n, t, c:c + 1]).then_inc(sem["norm_ss"], 1)

        def group_hi(dst, fill0, c, gain):
            for f in (2 * c, 2 * c + 1):
                F = fill0 + f
                act.wait_ge(sem["tr_full"], F + 1)
                for k in (2 * f, 2 * f + 1):
                    ins = act.activation(dst[:, k, 0, :], psum[:, 4 + F % 4, SEQ * (k % 2):SEQ * (k % 2) + SEQ],
                                         ACT.Copy, scale=par[:, Q_GAIN[gain] + k:Q_GAIN[gain] + k + 1])
                ins.then_inc(sem["tr_hi"], 1)

        def next_input(n, fill0, gain, g0):
            def hook(b, j):
                if b and j == 2:
                    group_hi(ha, fill0, b - 1, gain)
                if b and j == 4:
                    act.wait_ge(row_free, FREE + g0 + b)
                    sum_squares(n, x_rows, b - 1)
            return hook

        def head_stage(j, k, last):
            if j == 0 and k < last and k < N1:
                n = k
                act.wait_ge(sem["at_qk"], n + 1)
                if n >= 2:
                    act.wait_ge(sem["at_sc"], n - 1)
                if heads[n][0] == "near":
                    for i, g in enumerate((Q_BQ, Q_BK)):
                        ins = act.activation(qk_t[n % 2][:, i, :], psum[:, QK_BANK, 256 * i:256 * i + 256],
                                             ACT.Copy, scale=par[:, g:g + 1])
                else:
                    ins = act.activation(qk_t[n % 2][:], psum[:, QK_BANK, :].rearrange("p (a b) -> p a b", a=2),
                                         ACT.Copy)
                ins.then_inc(sem["at_qksb"], 1)
            n = k - 1
            if j == 1 and n >= first[0]:
                act.wait_ge(sem["at_pt"], n + 1)
                if n >= 2:
                    act.wait_ge(sem["at_o"], n - 1)
                act.activation(prob_t[n % 2][:], psum[:, PT_BANK, :].rearrange("p (a b) -> p a b", a=2),
                               ACT.Copy).then_inc(sem["at_ptsb"], 1)
            if j == 2 and k < last:
                n = k
                act.wait_ge(sem["at_nm"], n + 1)
                if n >= 2:
                    act.wait_ge(sem["at_pt"], n - 1)
                if heads[n][0] == "band":
                    h = heads[n][1]
                    act.activation(esink[:, n % 2, :], nmx[:, n % 2, :], ACT.Exp, bias=sink[:, h:h + 1])
                for t in range(NT):
                    ins = act.activation(prob[n % 2][:, t, :], sco[n % 2][:, t, :], ACT.Exp,
                                         bias=nmx[:, n % 2, t:t + 1], accum_out=den[:, n % 2, t:t + 1])
                ins.then_inc(sem["at_p"], 1)
            n = k - 1
            if j == 3 and n >= first[0] and heads[n][0] != "slc":
                act.wait_ge(sem["at_o"], n + 1)
                kind, h = heads[n][:2]
                dst = mix_t[:, h, :] if kind == "win" else ot[:, h + (8 if kind == "near" else 0), :]
                act.activation(dst, psum[:, O_BANK, 0:SEQ], ACT.Copy).then_inc(sem["at_osb"], 1)

        first = [0]

        act.wait_ge(sem["par_in"], 16)
        group_hi(ha, T_MIX1, 0, "mix1")
        ahead(-3)
        ahead(-2)
        group_hi(ha, T_MIX1, 1, "mix1")
        ahead(-1)
        for j in range(8):
            ahead(S_IN1 + j)
            if j in (0, 2):
                group_hi(ha, T_MIX1, 2 + j // 2, "mix1")
            if 2 <= j < 6:
                act.wait_ge(x_in[j - 2], 16)
                sum_squares(0, x_rows, j - 2)
        act.wait_ge(sem["norm_rs"], 1)
        copy_rows(proj, 0)(0, R_IN1, S_IN1 + 8, 0, 0)
        row_blocks(S_IN1 + 8, R_IN1 + 1, IN1_BLOCKS - 1, 8, copy_rows(proj, 0, 1))

        def split_outputs(c):
            act.wait_ge(sem["at_osb"], 2 * c + 2)
            act.wait_ge(mm_done, S_BRANCH - 7 + c)
            act.activation(ha[:, 2 * c:2 * c + 2, 0, :], ot[:, 2 * c:2 * c + 2, :], ACT.Copy
                           ).then_inc(sem["ot_hi"], 1)

        act.wait_ge(sem["sink_in"], 16)
        for s in range(8 * GATE_BLOCKS):
            ahead(S_GATE + s)
            head_stage(s % 4, s // 4, N1)
            if s >= 57:
                split_outputs(s - 57)
            if s % 8 == 7:
                copy_rows(gates, 0)(s // 8, R_GATE + s // 8, S_GATE + s + 1, 0, 0)

        def merged_hi(n):
            for f in range(2):
                F = T_MERGE + 2 * n + f
                act.wait_ge(sem["tr_full"], F + 1)
                act.activation(hb[:, 2 * (F - T_MERGE):2 * (F - T_MERGE) + 2, 0, :],
                               psum[:, 4 + F % 4, :].rearrange("p (a b) -> p a b", a=2), ACT.Copy
                               ).then_inc(sem["tr_hi"], 1)

        for n in range(4):
            for j in range(8):
                if j == 4 and n:
                    merged_hi(n - 1)
                ahead(S_BRANCH + 8 * n + j)
                if n == 0 and j < 4:
                    head_stage(j, N1, N1)
                if n == 0 and j == 4:
                    split_outputs(7)
                if j == 1:
                    act.wait_ge(row_free, FREE + R_GATE + 5 + n)
                    for b in range(2):
                        ins = act.activation(gates[:, 4 * b + n, :, :], gates[:, 4 * b + n, :, :], ACT.Sigmoid)
                    ins.then_inc(sem["sig_done"], 1)
        merged_hi(3)
        row_blocks(S_OUT1, R_OUT1, 4, 8, no_evac, extra=next_input(1, T_FFN1, "ffn1", R_OUT1))

        def row_of_roots(count):
            act.wait_ge(sem["rstd_row_mm"], count)
            act.activation(rstd_row[:], psum[:, 4, 0:SEQ], ACT.Copy).then_inc(sem["rstd_row_ok"], 1)

        def up1_stage(p, j, v, pair, i):
            if j == 0:
                act.wait_ge(sem["cmask_in"], 4)
                act.wait_ge(mm_done, S_UP1[p] + 8 * v + 8 + 16 * i)
                act.activation(u_pad[v][:, :, 1:SEQ + 1], psum[:, 4 * v:4 * v + 4, 0:SEQ], ACT.Copy
                               ).then_inc(sem["half_ok"], 1)
            if j == 2:
                act.wait_ge(sem["u_scaled"], v + 1 + 2 * pair)
                for s in range(4):
                    chunk = 44 * v + 4 * pair + s
                    w = Q_CONVW + 3 * chunk + 1
                    ins = act.activation(conv[v][:, s, :], u_pad[v][:, s, 1:SEQ + 1], ACT.Identity,
                                         scale=par[:, bass.ds(w, 1)], bias=par[:, bass.ds(Q_CONVB + chunk, 1)])
                ins.then_inc(sem["conv_mid"], 1)
            if j == 5 and v == 0:
                act.wait_ge(sem["conv_done"], 1 + 2 * pair)
                act.activation(conv[0][:], conv[0][:], ACT.Silu).then_inc(sem["silu_done"], 1)
            if j == 6 and v == 1:
                act.wait_ge(sem["act_ready"], pair + 1)
                act.activation(hb[:, bass.ds(4 * i, 4), 0, :], act_f[:], ACT.Copy).then_inc(sem["hb_hi"], 1)

        for p, (j0, n) in enumerate(UP1_PASSES):
            for j in range(8):
                ahead(S_UP1[p] + j)
                if p == 0 and j == 2:
                    group_hi(ha, T_FFN1, 3, "ffn1")
                    act.wait_ge(row_free, FREE + R_OUT1 + 4)
                    sum_squares(1, x_rows, 3)
                if p == 0 and j == 7:
                    row_of_roots(1)
            with act.Fori(0, n - 1) as i:
                for j in range(8):
                    ahead(S_UP1[p] + 8 + j, i, 2)
                    up1_stage(p, j, 0, j0 + i, i)
                for j in range(8):
                    ahead(S_UP1[p] + 16 + j, i, 2)
                    up1_stage(p, j, 1, j0 + i, i)
            for j in range(8):
                ahead(S_UP1[p] + 16 * n - 8 + j)
                up1_stage(p, j, 0, j0 + n - 1, n - 1)

            enter = next_input(2, T_MIX2, "mix2", R_DOWN1[p])

            def tail(b, j):
                if b == 0 and j < 4:
                    for stage in ((0, 1), (2, 3), (4, 5), (6,))[j]:
                        up1_stage(p, stage, 1, j0 + n - 1, n - 1)
                if p == 2:
                    enter(b, j)

            row_blocks(S_DOWN1[p], R_DOWN1[p], 4, 2 * n, no_evac, extra=tail)


        def pair(bank, n=2 * SEQ, rows=P):
            return psum[0:rows, bank, 0:n].rearrange("p (a b) -> p a b", a=2)

        for s in range(8 * IN2_BLOCKS):
            ahead(S_IN2 + s)
            if s == 2:
                group_hi(ha, T_MIX2, 3, "mix2")
                act.wait_ge(row_free, FREE + R_DOWN1[-1] + 4)
                sum_squares(2, x_rows, 3)
            if s == 5:
                act.wait_ge(sem["wg_in"], 16)
                act.activation(w_gate_h[:], w_gate[:], ACT.Copy).then_inc(sem["wg_hi"], 1)
            if s == 10:
                act.wait_ge(sem["t5_mm"], 2)
                act.activation(t5_cols[:].rearrange("p c h -> p (c h)"), psum[:, 6, 0:32], ACT.Copy
                               ).then_inc(sem["t5_cols_ok"], 1)
            if s == 12:
                for f in range(2):
                    act.wait_ge(sem["kvt_mm"], f + 1)
                    act.activation(kv_cmp_t[:, 2 * f:2 * f + 2, :], pair(4 + f), ACT.Copy).then_inc(sem["kvt_ok"], 1)
            if s == 14:
                act.wait_ge(sem["gate_mm"], 1)
                act.activation(gate_t[:], psum[0:N_GATES, 7, 0:SEQ], ACT.Copy).then_inc(sem["gate_half"], 1)
            if s in (17, 19):
                kv = (s - 17) // 2
                act.wait_ge(sem["hid_mm"], kv + 1)
                act.activation(hid_t[:, kv, :], psum[0:2 * NCMP, 4 + kv, 0:HD], ACT.Copy
                               ).then_inc(sem["hid_copied"], 1)
            if s == 18:
                act.wait_ge(sem["gate_tr"], 1)
                for t in range(NT):
                    ins = act.activation(gate24[:, t, :], psum[:, 6, N_GATES * t:N_GATES * (t + 1)], ACT.Sigmoid,
                                         scale=rstd[:, 4 + t:5 + t])
                ins.then_inc(sem["gate_ok"], 1)
            if s == 21:
                act.wait_ge(sem["hid_tr"], 1)
                for kv in range(2):
                    act.activation(cmp_hid[:, kv, :, :].rearrange("p g n -> p (g n)"),
                                   psum[:, 7, 2 * NCMP * kv:2 * NCMP * (kv + 1)],
                                   ACT.Gelu_apprx_tanh, bias=par[:, Q_B1K + kv:Q_B1K + kv + 1]
                                   ).then_inc(sem["hid_ok"], 1)
            if s in (23, 28):
                for f in range(2):
                    i = (s == 28)
                    act.wait_ge(sem["qall_mm"], 2 * i + f + 1)
                    act.activation(q_all[i][:, 2 * f:2 * f + 2, :], pair(4 + f), ACT.Copy).then_inc(sem["qall_ok"], 1)
            if s == 24:
                act.wait_ge(sem["kv_mm"], 1)
                act.activation(cmp_k[:], pair(6, 2 * NCMP), ACT.Copy).then_inc(sem["kv_ok"], 1)
                act.wait_ge(sem["kv_mm"], 2)
                act.activation(cmp_v[:].rearrange("p g d -> p (g d)"), psum[0:NCMP, 6, SEQ:2 * SEQ], ACT.Copy
                               ).then_inc(sem["kv_ok"], 1)
            if s == 32:
                act.wait_ge(sem["cs_ok"], 1)
                act.activation(cmp_p[:], cmp_s[:], ACT.Exp).then_inc(sem["cs_exp"], 1)
            if s == 36:
                act.wait_ge(sem["kall_mm"], 1)
                act.wait_ge(sem["t5_st"], 32)
                act.activation(k_all[:, 0:2, :], pair(4), ACT.Copy).then_inc(sem["kall_ok"], 1)
            if s == 38:
                for f in range(4):
                    act.wait_ge(sem["cpt_mm"], f + 1)
                    act.activation(cmp_pt[:, 2 * f:2 * f + 2, :], pair(4 + (f + 1) % 4, rows=NCMP), ACT.Copy
                                   ).then_inc(sem["cpt_ok"], 1)
            if s % 8 == 7:
                if s == 7:
                    act.wait_ge(sem["norm_rs"], 3)
                copy_rows(proj2, 2)(IN2_ORDER[s // 8], R_IN2 + s // 8, S_IN2 + s + 1, 0, 0)
        first[0] = N1
        for s in range(8 * RET_BLOCKS):
            ahead(S_RET + s)
            if s == 2:
                act.wait_ge(sem["kall_mm"], 2)
                act.activation(k_all[:, 2:4, :], pair(4), ACT.Copy).then_inc(sem["kall_ok"], 1)
            if s < RET_START:
                head_stage(1 + s % SLOT, N1 + s // SLOT, NH)
            r, j = divmod(s - RET_START - 1, 3)
            if j == 0 and 0 <= r < RET_HEADS:
                act.wait_ge(sem["rq_mm"], r + 1)
                if r >= 2:
                    act.wait_ge(sem["rs_mm"], r - 1)
                act.activation(ret_q[r % 2][:], pair(4), ACT.Copy).then_inc(sem["rq_ok"], 1)
                act.wait_ge(sem["rk_mm"], r + 1)
                act.activation(ret_k[r % 2][:], pair(5), ACT.Copy).then_inc(sem["rk_ok"], 1)
            if s == 57:
                act.wait_ge(row_free, FREE + R_RET + 7)
                act.activation(ret[:, 6, :, :], ret[:, 6, :, :], ACT.Silu).then_inc(sem["silu_g"], 1)
            if 57 <= s < 61:
                c = s - 57
                act.wait_ge(sem["at_osb"], outs_before(NH))
                act.wait_ge(mm_done, S_RET + s)
                act.activation(ha[:, 2 * c:2 * c + 2, 0, :], mix_t[:, 2 * c:2 * c + 2, :], ACT.Copy
                               ).then_inc(sem["ot_hi"], 1)
            if s % 8 == 7:
                copy_rows(ret, 2)(s // 8, R_RET + s // 8, S_RET + s + 1, 0, 0)

        def mix_stage(b, j):
            if b:
                if j == 4:
                    sum_squares(3, rows, b - 1)
                return
            if j == 0:
                act.wait_ge(row_free, FREE + R_RET + RET_BLOCKS)
                act.activation(ret[:, 7, :, :], ret[:, 7, :, :], ACT.Silu).then_inc(sem["silu_g"], 1)
            if j in (1, 4):
                for f in range(2 * (j == 4), 2 * (j == 4) + 2):
                    F = T_RETO + f
                    act.wait_ge(sem["tr_full"], F + 1)
                    act.activation(ha[:, 8 + 2 * f:10 + 2 * f, 0, :], pair(4 + F % 4), ACT.Copy
                                   ).then_inc(sem["tr_hi"], 1)

        def mix_rows(b, g, end, i, m):
            act.wait_ge(mm_done, end)
            act.activation(rows[:, :, b * COLS:(b + 1) * COLS], psum[:, 2 * (g % 2):2 * (g % 2) + 2, :],
                           ACT.Copy).then_inc(row_free, 1)

        row_blocks(S_OUT2, R_OUT2, 4, 8, mix_rows, extra=mix_stage)
        act.wait_ge(row_free, FREE + R_OUT2 + 4)
        sum_squares(3, rows, 3)

        def up2_stage(j, c, i):
            if j == 0:
                act.wait_ge(mm_done, S_UP2[0] + 8 * (c % 4 + 1) + 64 * (c // 4) + 64 * i)
                act.activation(u_sum[:], psum[:, 4 * (c % 2):4 * (c % 2) + 4, 0:SEQ], ACT.Copy
                               ).then_inc(sem["usum_done"], 1)
            if j == 3:
                act.wait_ge(sem["act_ready"], 11 + c + 1 + 4 * i)
                act.activation(ha[:, 4 * (c % 4):4 * (c % 4) + 4, 0, :], u_act[:], ACT.Copy).then_inc(sem["hb_hi"], 1)

        def ff2_pass(p, i=0):
            for b in range(8):
                for j in range(8):
                    if S_UP2[p] + 8 * b + j + AHEAD < N_STEPS:
                        ahead(S_UP2[p] + 8 * b + j, i, 8)
                    if p == 0 and b == 0:
                        if j < 2:
                            group_hi(hb, T_MLP2, 2 + j, "mlp2")
                        if 1 <= j < 5:
                            act.wait_ge(sem["post_ok"], j)
                            sum_squares(4, x_rows, j - 1)
                        if j == 7:
                            row_of_roots(2)
                    if 1 <= b < 5:
                        up2_stage(j, 4 * p + b - 1, i)
                    if p == UP2_PASSES - 1 and b > 4 and j == 4:
                        act.wait_ge(row_free, FREE + R_DOWN2[p] + b - 4)
                        sum_squares(5, y_rows, b - 5)

        group_hi(hb, T_MLP2, 0, "mlp2")
        group_hi(hb, T_MLP2, 1, "mlp2")
        ff2_pass(0)
        with act.Fori(0, UP2_PASSES - 2) as i:
            ff2_pass(1, i)
        ff2_pass(UP2_PASSES - 1)
        act.wait_ge(row_free, FREE + R_DOWN2[-1] + 4)
        sum_squares(5, y_rows, 3)

    @block.vector
    def _(dve):
        chain = Chain(dve, sem["dve_chain"])

        def ahead(step, i=0, m=0):
            q = step + AHEAD
            dve.wait_ge(hi_done, q + 1 + 8 * m * i)
            dve.tensor_tensor(wl[q % SPLIT_SLOTS][:], raw[q // 2 % RAW_SLOTS][:, 2 * (q % 2):2 * (q % 2) + 2, :],
                              wh[q % SPLIT_SLOTS][:].bitcast(F32), ALU.subtract).then_inc(lo_done, 1)

        def row_blocks(step0, g0, n, per, evac, extra=None):
            if per != 8 or extra:
                for b in range(n):
                    for j in range(per):
                        ahead(step0 + per * b + j)
                        if extra:
                            extra(b, j)
                    evac(b, g0 + b, step0 + per * (b + 1), 0, 0)
                return
            if n % 2:
                for j in range(8):
                    ahead(step0 + j)
                evac(0, g0, step0 + 8, 0, 0)
            with dve.Fori(0, n // 2) as i:
                for b in (n % 2, n % 2 + 1):
                    for j in range(8):
                        ahead(step0 + 8 * b + j, i, 2)
                    evac(b, g0 + b, step0 + 8 * (b + 1), i, 2)

        def no_evac(b, g, end, i, m):
            pass

        def group_lo(dst, fill0, c, gain):
            for f in (2 * c, 2 * c + 1):
                F = fill0 + f
                dve.wait_ge(sem["tr_hi"], F + 1)
                for k in (2 * f, 2 * f + 1):
                    col = Q_GAIN[gain] + k
                    ins = dve.scalar_tensor_tensor(
                        dst[:, k, 1, :], psum[:, 4 + F % 4, SEQ * (k % 2):SEQ * (k % 2) + SEQ], par[:, col:col + 1],
                        dst[:, k, 0, :].bitcast(F32), ALU.mult, ALU.subtract)
                ins.then_inc(sem["tr_lo"], 1)

        def plain_lo(dst, F):
            dve.wait_ge(sem["tr_hi"], F + 1)
            dve.tensor_tensor(dst[:, :, 1, :], psum[:, 4 + F % 4, :].rearrange("p (a b) -> p a b", a=2),
                              dst[:, :, 0, :].bitcast(F32), ALU.subtract).then_inc(sem["tr_lo"], 1)

        def head_stage(j, k, last):
            if k >= last:
                return
            n = k
            kind, h = heads[n][:2]
            if j == 2:
                dve.wait_ge(sem["at_sc"], n + 1)
                if n >= 2:
                    dve.wait_ge(sem["at_p"], n - 1)
                if kind == "near":
                    dve.wait_ge(sem["bias_ok"], h + 1)
                elif kind != "band":
                    dve.wait_ge(t5_bias_in[h % 2], 32 * (h // 2 + 1))
                b = (band if kind == "band" else bias[h % 2])[:].rearrange("p a b -> p (a b)")
                if kind != "band":
                    b = bass.AP(b.tensor, b.offset + NT * SEQ - 1, [list(b.ap[0]), [-1, NT * SEQ]])
                dve.scalar_tensor_tensor(sco[n % 2][:].rearrange("p a b -> p (a b)"), psum[:, SC_BANK, :], SCALE,
                                         b, ALU.mult, ALU.add
                                         ).then_inc(sem["at_s"], 1)
                dve.wait_ge(sem["at_s"], n + 1)
                chain.link(dve.reduce_max(mx[:, n % 2, :], sco[n % 2][:], AX.X))
                if kind == "band":
                    dve.tensor_scalar(nmx[:, n % 2, :], mx[:, n % 2, :], sink[:, h:h + 1], -1.0, ALU.max, ALU.mult
                                      ).then_inc(sem["at_nm"], 1)
                else:
                    dve.tensor_scalar(nmx[:, n % 2, :], mx[:, n % 2, :], -1.0, None, ALU.mult
                                      ).then_inc(sem["at_nm"], 1)
            if j == 3:
                dve.wait_ge(sem["at_p"], n + 1)
                if kind == "band":
                    chain.link(dve.tensor_tensor(den[:, n % 2, :], den[:, n % 2, :], esink[:, n % 2, :], ALU.add))
                chain.link(dve.reciprocal(rden[:, n % 2, :], den[:, n % 2, :]))
                if kind in ("slc", "win"):
                    g = 3 * h + (1 if kind == "slc" else 2)
                    chain.link(dve.tensor_tensor(rden[:, n % 2, :], rden[:, n % 2, :], gate24[:, :, g], ALU.mult))
                for t in range(NT):
                    ins = dve.tensor_scalar(prob[n % 2][:, t, :], prob[n % 2][:, t, :], rden[:, n % 2, t:t + 1],
                                            None, ALU.mult)
                ins.then_inc(sem["at_pn"], 1)

        def rotation_tables():
            dve.wait_ge(sem["cos1_in"], 16)
            dve.wait_ge(sem["sin1_in"], 16)
            dve.wait_ge(sem["again_in"], 32)
            for i in range(2):
                g = [a_gain[:, i, 64 * s:64 * s + 64].unsqueeze(1).to_broadcast([P, NT, 64]) for s in range(2)]
                dve.tensor_tensor(rot_a[:, i, :, 0:64], cos1[:], g[0], ALU.mult)
                dve.tensor_tensor(rot_a[:, i, :, 64:128], cos1[:], g[1], ALU.mult)
                dve.tensor_tensor(rot_b[:, i, :, 64:128], sin1[:], g[0], ALU.mult)
                chain.link(dve.tensor_tensor(rot_b[:, i, :, 0:64], sin1[:], g[1], ALU.mult))
            chain.link(dve.tensor_scalar(rot_b[:, :, :, 0:64], rot_b[:, :, :, 0:64], -1.0, None, ALU.mult))

        pieces = [(0, 0, 0, 4), (0, 1, 0, 4), (1, 0, 0, 4), (1, 1, 0, 4), (2, 0, 1, 2), (2, 1, 1, 2)]

        def piece(b, t, nh):
            return proj[:, b, t, 0:nh * HD].rearrange("p (h d) -> p h d", d=HD)

        def piece_sums(i):
            b, t, _, nh = pieces[i]
            x = piece(b, t, nh)
            chain.link(dve.tensor_tensor(tmp_a[:, 0:nh, :], x, x, ALU.mult))
            chain.link(dve.reduce_sum(ssq[:, 4 * i:4 * i + nh], tmp_a[:, 0:nh, :], AX.X))

        def piece_rotated(i):
            b, t, kind, nh = pieces[i]
            x = piece(b, t, nh)
            r = rsq[:, 4 * i:4 * i + nh].unsqueeze(2).to_broadcast([P, nh, HD])
            chain.link(dve.tensor_tensor(x, x, r, ALU.mult))

            def row(tab, lo, hi):
                return tab[:, kind, t, lo:hi].unsqueeze(1).to_broadcast([P, nh, hi - lo])

            dve.tensor_tensor(tmp_a[:, 0:nh, :], x, row(rot_a, 0, HD), ALU.mult)
            dve.tensor_tensor(tmp_b[:, 0:nh, 0:64], x[:, :, 64:128], row(rot_b, 0, 64), ALU.mult)
            chain.link(dve.tensor_tensor(tmp_b[:, 0:nh, 64:128], x[:, :, 0:64], row(rot_b, 64, 128), ALU.mult))
            dve.tensor_tensor(x, tmp_a[:, 0:nh, :], tmp_b[:, 0:nh, :], ALU.add).then_inc(sem["a_ready"], 1)

        dve.wait_ge(sem["par_in"], 16)
        group_lo(ha, T_MIX1, 0, "mix1")
        ahead(-3)
        ahead(-2)
        group_lo(ha, T_MIX1, 1, "mix1")
        ahead(-1)
        for s in range(8 * IN1_BLOCKS):
            ahead(S_IN1 + s)
            if s in (0, 2):
                group_lo(ha, T_MIX1, 2 + s // 2, "mix1")
            if s == 10:
                rotation_tables()
            if 26 <= s < 32:
                if s == 26:
                    dve.wait_ge(row_free, FREE + 3)
                piece_sums(s - 26)
            if s == 32:
                dve.memset(ssq[:, 18:20], 1.0)
                dve.memset(ssq[:, 22:24], 1.0).then_inc(sem["an_ss"], 1)
            if s in range(36, 54, 3):
                if s == 36:
                    dve.wait_ge(sem["an_rs"], 1)
                piece_rotated((s - 36) // 3)

        def near_view(h):
            c = h % 4 * HD
            return proj[:, 3 + h // 4:6 + h // 4:2, :, c:c + HD]

        def split_outputs(c):
            dve.wait_ge(sem["ot_hi"], c + 1)
            dve.tensor_tensor(ha[:, 2 * c:2 * c + 2, 1, :], ot[:, 2 * c:2 * c + 2, :],
                              ha[:, 2 * c:2 * c + 2, 0, :].bitcast(F32), ALU.subtract).then_inc(sem["ot_lo"], 1)

        dve.wait_ge(sem["band_in"], 16)
        for s in range(8 * GATE_BLOCKS):
            j, k = s % 4, s // 4
            ahead(S_GATE + s)
            if k < 8 and j == 0:
                t4 = tmp_b[:].rearrange("p (a b) d -> p a b d", a=2)
                if k == 0:
                    dve.wait_ge(row_free, FREE + R_GATE)
                    dve.wait_ge(sem["a_ready"], len(pieces))
                chain.link(dve.tensor_tensor(t4, near_view(k), near_view(k), ALU.mult))
                dve.reduce_sum(ssb[:, k % 2, :], tmp_b[:], AX.X).then_inc(sem["bn_ss"], 1)
            if k < 8 and j == 1:
                dve.wait_ge(sem["bn_rs"], k + 1)
                r = rsb[:, k % 2, :].rearrange("p (a b) -> p a b", a=2).unsqueeze(3).to_broadcast([P, 2, NT, HD])
                dve.tensor_tensor(near_view(k), near_view(k), r, ALU.mult).then_inc(sem["bn_ok"], 1)
            head_stage(j, k, N1)
            if s >= 58:
                split_outputs(s - 58)

        def merged_lo(n):
            for f in range(2):
                plain_lo(hb[:, 4 * n + 2 * f:4 * n + 2 * f + 2], T_MERGE + 2 * n + f)

        for n in range(4):
            for j in range(4):
                ahead(S_BRANCH + 8 * n + j)
                if n == 0 and j == 0:
                    split_outputs(6)
            dve.wait_ge(mm_done, S_BRANCH + 8 * n + 4)
            dve.wait_ge(sem["sig_done"], n + 1)
            if n >= 2:
                dve.wait_ge(sem["tr_full"], T_MERGE + 2 * n - 2)
            dve.tensor_tensor(merged[n % 2][:], psum[:, 2:4, :], gates[:, n, :, :], ALU.mult).then_inc(row_free, 1)
            if n:
                merged_lo(n - 1)
            for j in range(4, 8):
                ahead(S_BRANCH + 8 * n + j)
                if n == 0 and j == 5:
                    split_outputs(7)
            dve.wait_ge(mm_done, S_BRANCH + 8 * n + 8)
            dve.tensor_tensor(gates[:, 4 + n, :, :], psum[:, 0:2, :], gates[:, 4 + n, :, :], ALU.mult
                              ).then_inc(row_free, 1)
            dve.wait_ge(row_free, FREE + R_BRANCH + 2 * n + 2)
            dve.tensor_tensor(merged[n % 2][:], merged[n % 2][:], gates[:, 4 + n, :, :], ALU.add
                              ).then_inc(sem["merge_rows"], 1)
        merged_lo(3)

        def add_rows(dst, add=True):
            def evac(b, g, end, i, m):
                dve.wait_ge(mm_done, end + 8 * m * i)
                d = dst[:, :, bass.ds((b + m * i) * COLS, COLS)]
                if add:
                    dve.tensor_tensor(d, psum[:, 2 * (g % 2):2 * (g % 2) + 2, :], d, ALU.add).then_inc(row_free, 1)
                else:
                    dve.tensor_copy(d, psum[:, 2 * (g % 2):2 * (g % 2) + 2, :]).then_inc(row_free, 1)
            return evac

        dve.wait_ge(sem["xre_in"], 16)

        def enter_ffn1(b, j):
            if b and j == 3:
                group_lo(ha, T_FFN1, b - 1, "ffn1")

        row_blocks(S_OUT1, R_OUT1, 4, 8, add_rows(x_rows), extra=enter_ffn1)

        def diagonal(n):
            dve.wait_ge(sem["norm_rs"], n + 1)
            dve.memset(ones[:], 1.0)
            for t in range(NT):
                ins = dve.tensor_scalar(rstd_diag[:, t, :], ident[:], rstd[:, 2 * n + t:2 * n + t + 1], None, ALU.mult)
            ins.then_inc(sem["diag_ok"], 1)

        def up1_stage(p, j, v, pair, i):
            count = 2 * pair + v + 1
            if j == 0:
                dve.wait_ge(sem["half_ok"], count)
                u = u_pad[v][:, :, 1:SEQ + 1]
                dve.tensor_tensor(u, psum[:, 4 * v:4 * v + 4, SEQ:2 * SEQ], u, ALU.add).then_inc(chan_free, 1)
            if j == 1:
                dve.wait_ge(chan_free, FREE + count)
                dve.wait_ge(sem["rstd_row_ok"], 1)
                u = u_pad[v][:, :, 1:SEQ + 1]
                dve.tensor_tensor(u, u, rstd_row[:].unsqueeze(1).to_broadcast([P, 4, SEQ]), ALU.mult
                                  ).then_inc(sem["u_scaled"], 1)
            if j in (3, 4):
                if j == 3:
                    dve.wait_ge(sem["conv_mid"], count)
                else:
                    dve.wait_ge(sem["tap_done"], count)
                tap = 0 if j == 3 else 2
                for s in range(4):
                    w = Q_CONVW + 3 * (44 * v + 4 * pair + s) + tap
                    ins = dve.scalar_tensor_tensor(conv[v][:, s, :], u_pad[v][:, s, tap:tap + SEQ],
                                                   par[:, bass.ds(w, 1)], conv[v][:, s, :], ALU.mult, ALU.add)
                ins.then_inc(sem["tap_done" if j == 3 else "conv_done"], 1)
            if j == 5 and v == 1:
                dve.wait_ge(sem["conv_done"], count)
                dve.wait_ge(sem["silu_done"], pair + 1)
                dve.tensor_tensor(act_f[:], conv[0][:], conv[1][:], ALU.mult).then_inc(sem["act_ready"], 1)
            if j == 6 and v == 1:
                dve.wait_ge(sem["hb_hi"], pair + 1)
                h = hb[:, bass.ds(4 * i, 4), :, :]
                dve.tensor_tensor(h[:, :, 1, :], act_f[:], h[:, :, 0, :].bitcast(F32), ALU.subtract
                                  ).then_inc(sem["hb_lo"], 1)

        for p, (j0, n) in enumerate(UP1_PASSES):
            for j in range(8):
                ahead(S_UP1[p] + j)
                if p == 0 and j == 3:
                    group_lo(ha, T_FFN1, 3, "ffn1")
                if p == 0 and j == 5:
                    diagonal(1)
            with dve.Fori(0, n - 1) as i:
                for j in range(8):
                    ahead(S_UP1[p] + 8 + j, i, 2)
                    up1_stage(p, j, 0, j0 + i, i)
                for j in range(8):
                    ahead(S_UP1[p] + 16 + j, i, 2)
                    up1_stage(p, j, 1, j0 + i, i)
            for j in range(8):
                ahead(S_UP1[p] + 16 * n - 8 + j)
                up1_stage(p, j, 0, j0 + n - 1, n - 1)

            def tail(b, j):
                if b == 0 and j < 4:
                    for stage in ((0, 1), (2, 3), (4, 5), (6,))[j]:
                        up1_stage(p, stage, 1, j0 + n - 1, n - 1)
                if p == 2 and b and j == 3:
                    group_lo(ha, T_MIX2, b - 1, "mix2")

            row_blocks(S_DOWN1[p], R_DOWN1[p], 4, 2 * n, add_rows(x_rows), extra=tail)

        p16 = cmp_p[:].rearrange("p h t n -> p (h t) n")
        s16 = cmp_s[:].rearrange("p h t n -> p (h t) n")
        m16 = cmp_m[:].rearrange("p h t -> p (h t)")
        n16 = cmp_n[:].rearrange("p h t -> p (h t)")
        for s in range(8 * IN2_BLOCKS):
            ahead(S_IN2 + s)
            if s == 3:
                group_lo(ha, T_MIX2, 3, "mix2")
            if s == 6:
                dve.wait_ge(sem["wg_hi"], 1)
                dve.tensor_tensor(w_gate_l[:], w_gate[:], w_gate_h[:].bitcast(F32), ALU.subtract
                                  ).then_inc(sem["wg_lo"], 1)
            if s == 10:
                dve.wait_ge(sem["t5_in"], 80)
                dve.wait_ge(sem["t5_mm"], 1)
                dve.tensor_tensor(t5_rows[:], psum[0:8, 7, :], t5_ahead[:], ALU.add).then_inc(sem["t5_rows_ok"], 1)
            if s in (13, 14):
                kv = s - 13
                dve.wait_ge(sem["kvt_ok"], kv + 1)
                for g in range(2):
                    src = kv_cmp_t[:, 2 * kv + g, :]
                    win = bass.AP(src.tensor, src.offset, [list(src.ap[0]), [1, CMP_BLOCK], [CMP_STRIDE, NCMP]])
                    pe_col = (Q_PEK, Q_PEV)[kv]
                    pe_in = par[:, pe_col:pe_col + CMP_BLOCK].unsqueeze(2).to_broadcast([P, CMP_BLOCK, NCMP])
                    ins = dve.tensor_tensor(cmp_in[:, kv, :, g, :], win, pe_in, ALU.add)
                ins.then_inc(sem["cin_ok"], 1)
            if s == 15:
                dve.wait_ge(sem["gate_half"], 1)
                dve.tensor_tensor(gate_t[:], psum[0:N_GATES, 7, SEQ:2 * SEQ], gate_t[:], ALU.add
                                  ).then_inc(sem["gate_sum"], 1)
            if s == 25:
                dve.wait_ge(sem["cmp_dist_in"], 16)
                for t in range(NT):
                    src = cmp_dist[:, 8 * t + NCMP - 1, :]
                    by_block = bass.AP(src.tensor, src.offset, [list(src.ap[0]), [1, 8], [-8, NCMP]])
                    ins = dve.tensor_tensor(cmp_bias[:, :, t, :], by_block,
                                            cmp_mask[:, t, :].unsqueeze(1).to_broadcast([P, 8, NCMP]), ALU.add)
                chain.link(ins)
            if s == 31:
                dve.wait_ge(sem["cs_mm"], 1)
                chain.link(dve.scalar_tensor_tensor(cmp_s[:].rearrange("p h t n -> p (h t n)"), psum[:, 7, 0:240], SCALE,
                                                    cmp_bias[:].rearrange("p h t n -> p (h t n)"), ALU.mult, ALU.add))
                chain.link(dve.reduce_max(m16, s16, AX.X))
                dve.tensor_tensor(s16, s16, m16.unsqueeze(2).to_broadcast([P, 16, NCMP]), ALU.subtract
                                  ).then_inc(sem["cs_ok"], 1)
            if s == 33:
                dve.wait_ge(sem["cs_exp"], 1)
                dve.wait_ge(sem["gate_ok"], 1)
                chain.link(dve.reduce_sum(n16, p16, AX.X))
                chain.link(dve.reciprocal(n16, n16))
                chain.link(dve.tensor_tensor(cmp_n[:], cmp_n[:],
                                             gate24[:].rearrange("p t (h b) -> p h t b", b=3)[:, :, :, 0], ALU.mult))
                for t in range(NT):
                    ins = dve.tensor_tensor(cmp_p[:, :, t, :], cmp_p[:, :, t, :],
                                            cmp_seen[:, t, :].unsqueeze(1).to_broadcast([P, 8, NCMP]), ALU.mult)
                chain.link(ins)
                dve.tensor_tensor(p16, p16, n16.unsqueeze(2).to_broadcast([P, 16, NCMP]), ALU.mult
                                  ).then_inc(sem["cs_p"], 1)

        def rotate(blk, t):
            dve.wait_ge(row_free, FREE + R_RET + blk + 1)
            x = ret[:, blk, t, :].rearrange("p (h d) -> p h d", h=2)
            x1, x2 = x[:, :, 0:HD], x[:, :, HD:2 * HD]
            c = cos2[:, t, :].unsqueeze(1).to_broadcast([P, 2, HD])
            s = sin2[:, t, :].unsqueeze(1).to_broadcast([P, 2, HD])
            dve.tensor_tensor(rt[0][:], x1, c, ALU.mult)
            dve.tensor_tensor(rt[1][:], x2, s, ALU.mult)
            dve.tensor_tensor(rt[2][:], x2, c, ALU.mult)
            chain.link(dve.tensor_tensor(rt[3][:], x1, s, ALU.mult))
            dve.tensor_tensor(x1, rt[0][:], rt[1][:], ALU.subtract)
            dve.tensor_tensor(x2, rt[2][:], rt[3][:], ALU.add).then_inc(sem["rope_ok"], 1)
            dve.wait_ge(sem["rope_ok"], 2 * blk + t + 1)

        def ret_head(r, t):
            return ret_o[:, t, RET_D * r:RET_D * r + RET_D]

        def normalised(r):
            dve.wait_ge(sem["ro_rs"], r + 1)
            for t in range(NT):
                ins = dve.tensor_scalar(ret_head(r, t), psum[:, 7, RET_D * t:RET_D * t + RET_D],
                                        bag[:, r % 2, t, 0:1], grs[:, r % 2, t:t + 1], ALU.subtract, ALU.mult)
            ins.then_inc(sem["ro_ok"], 1)

        def gated(r):
            dve.wait_ge(sem["ro_ok"], r + 1)
            dve.wait_ge(sem["silu_g"], 1 + r // 2)
            for t in range(NT):
                o = ret_head(r, t)
                ins = dve.tensor_tensor(o, o, ret[:, 6 + r // 2, t, RET_D * (r % 2):RET_D * (r % 2) + RET_D],
                                        ALU.mult)
            ins.then_inc(sem["ro_gated"], 1)

        rotations = {12: (0, 0), 15: (0, 1), 18: (1, 0), 21: (1, 1), 27: (2, 0), 30: (2, 1), 36: (3, 0), 39: (3, 1)}
        dve.wait_ge(sem["rtab_in"], 48)
        for s in range(8 * RET_BLOCKS):
            ahead(S_RET + s)
            if s < RET_START:
                head_stage(1 + s % SLOT, N1 + s // SLOT, NH)
            if s in rotations:
                rotate(*rotations[s])
            r, j = divmod(s - RET_START - 2, 3)
            if j == 0 and 0 <= r < RET_HEADS:
                dve.wait_ge(sem["rs_mm"], r + 1)
                if r >= 2:
                    dve.wait_ge(sem["ro_mm"], r - 1)
                dve.tensor_tensor(ret_p[r % 2][:], psum[:, 6, :].rearrange("p (a b) -> p a b", a=2),
                                  decay[:, r, :, :], ALU.mult).then_inc(sem["rp_ok"], 1)
            if j == 1 and 0 <= r < RET_HEADS:
                dve.wait_ge(sem["ro_mm"], r + 1)
                for t in range(NT):
                    ins = dve.bn_stats(bst[:, r % 2, t, :], psum[:, 7, RET_D * t:RET_D * t + RET_D])
                chain.link(ins)
                for t in range(NT):
                    ins = dve.bn_aggr(bag[:, r % 2, t, :], bst[:, r % 2, t, :])
                ins.then_inc(sem["ro_stat"], 1)
            if j == 2 and 0 <= r < RET_HEADS:
                normalised(r)
            if s == 59:
                gated(0)
                gated(1)
            if 58 <= s < 62:
                c = s - 58
                dve.wait_ge(sem["ot_hi"], 8 + c + 1)
                dve.tensor_tensor(ha[:, 2 * c:2 * c + 2, 1, :], mix_t[:, 2 * c:2 * c + 2, :],
                                  ha[:, 2 * c:2 * c + 2, 0, :].bitcast(F32), ALU.subtract).then_inc(sem["ot_lo"], 1)

        def gain_rows(n, c, loads):
            dve.wait_ge(sem["norm_ss"], 8 * n + 2 * c + 2)
            dve.wait_ge(sem["grow_in"], 16 * loads)
            cols = slice(c * COLS, (c + 1) * COLS)
            dve.tensor_tensor(rows[:, :, cols], rows[:, :, cols],
                              gain_row[:, cols].unsqueeze(1).to_broadcast([P, NT, COLS]), ALU.mult
                              ).then_inc(sem["gained"], 1)

        def add_normed(n, c, before):
            if c == 0:
                dve.wait_ge(sem["norm_rs"], n + 1)
                dve.wait_ge(sem["gained"], before + 4)
            cols = slice(c * COLS, (c + 1) * COLS)
            for t in range(NT):
                ins = dve.scalar_tensor_tensor(x_rows[:, t, cols], rows[:, t, cols], rstd[:, 2 * n + t:2 * n + t + 1],
                                               x_rows[:, t, cols], ALU.mult, ALU.add)
            ins.then_inc(sem["post_ok"], 1)

        def mix_stage(b, j):
            if b:
                if j == 6:
                    gain_rows(3, b - 1, 1)
                return
            if j == 0:
                normalised(3)
            if j == 1:
                gated(2)
                gated(3)
            if j in (2, 5):
                for f in range(2 * (j == 5), 2 * (j == 5) + 2):
                    plain_lo(ha[:, 8 + 2 * f:10 + 2 * f], T_RETO + f)

        row_blocks(S_OUT2, R_OUT2, 4, 8, no_evac, extra=mix_stage)

        gain_rows(3, 3, 1)
        add_normed(3, 0, 0)
        add_normed(3, 1, 0)
        group_lo(hb, T_MLP2, 0, "mlp2")
        add_normed(3, 2, 0)
        group_lo(hb, T_MLP2, 1, "mlp2")

        def up2_stage(j, c, i):
            if j == 0:
                dve.wait_ge(sem["usum_done"], c + 1 + 4 * i)
                dve.tensor_tensor(u_sum[:], psum[:, 4 * (c % 2):4 * (c % 2) + 4, SEQ:2 * SEQ], u_sum[:], ALU.add
                                  ).then_inc(chan_free, 1)
            if j == 1:
                dve.wait_ge(chan_free, FREE + C_UP2[0] + c + 1 + 4 * i)
                dve.wait_ge(sem["rstd_row_ok"], 2)
                dve.tensor_tensor(u_sum[:], u_sum[:], rstd_row[:].unsqueeze(1).to_broadcast([P, 4, SEQ]), ALU.mult
                                  ).then_inc(sem["u_scaled"], 1)
            if j == 2:
                dve.wait_ge(sem["u_scaled"], 22 + c + 1 + 4 * i)
                dve.scalar_tensor_tensor(u_act[:], u_sum[:], 0.0, u_sum[:], ALU.max, ALU.mult
                                         ).then_inc(sem["act_ready"], 1)
            if j == 4:
                dve.wait_ge(sem["hb_hi"], 11 + c + 1 + 4 * i)
                h = ha[:, 4 * (c % 4):4 * (c % 4) + 4, :, :]
                dve.tensor_tensor(h[:, :, 1, :], u_act[:], h[:, :, 0, :].bitcast(F32), ALU.subtract
                                  ).then_inc(sem["hb_lo"], 1)

        def ff2_pass(p, i=0):
            for b in range(8):
                for j in range(8):
                    if S_UP2[p] + 8 * b + j + AHEAD < N_STEPS:
                        ahead(S_UP2[p] + 8 * b + j, i, 8)
                    if p == 0 and b == 0:
                        if j == 0:
                            add_normed(3, 3, 0)
                        if j < 2:
                            group_lo(hb, T_MLP2, 2 + j, "mlp2")
                        if j == 6:
                            diagonal(4)
                    if 1 <= b < 5:
                        up2_stage(j, 4 * p + b - 1, i)
                    if p == UP2_PASSES - 1 and b > 4 and j == 6:
                        gain_rows(5, b - 5, 2)
                if b >= 4:
                    g = R_DOWN2[p] + b - 4
                    cols = slice((b - 4) * COLS, (b - 3) * COLS)
                    dve.wait_ge(mm_done, S_UP2[p] + 8 * b + 8 + 64 * i)
                    acc = psum[:, 2 * (g % 2):2 * (g % 2) + 2, :]
                    if p == 0:
                        dve.tensor_copy(y_rows[:, :, cols], acc).then_inc(row_free, 1)
                    else:
                        dve.tensor_tensor(y_rows[:, :, cols], acc, y_rows[:, :, cols], ALU.add).then_inc(row_free, 1)

        ff2_pass(0)
        with dve.Fori(0, UP2_PASSES - 2) as i:
            ff2_pass(1, i)
        ff2_pass(UP2_PASSES - 1)
        gain_rows(5, 3, 2)
        for c in range(4):
            add_normed(5, c, 4)

    @block.tensor
    def _(pe):
        def rows_step(q, i, m, src, chunks, g, first, last):
            pe.wait_ge(lo_done, q + 1 + 8 * m * i)
            s = q % SPLIT_SLOTS
            for c in range(2):
                for t in range(NT):
                    acc = psum[:, 2 * (g % 2) + t, :]
                    hi = src[:, chunks[c], 0, t * P:(t + 1) * P]
                    lo = src[:, chunks[c], 1, t * P:(t + 1) * P]
                    pe.matmul(acc, hi, wh[s][:, c, :], start=first and c == 0, stop=False)
                    pe.matmul(acc, hi, wl[s][:, c, :], start=False, stop=False)
                    ins = pe.matmul(acc, lo, wh[s][:, c, :], start=False, stop=last and c == 1)
            ins.then_inc(mm_done, 1)

        def row_blocks(step0, g0, n, per, src, ready=None, extra=None):
            def one(b, g, q0, i, m):
                pe.wait_ge(row_free, g + 1 + m * i)
                for j in range(per):
                    if ready:
                        ready(j)
                    rows_step(q0 + j, i, m, src, (2 * j, 2 * j + 1), g, j == 0, j == per - 1)
                    if extra:
                        extra(b, j)
            if per != 8 or extra:
                for b in range(n):
                    one(b, g0 + b, step0 + per * b, 0, 0)
                return
            if n % 2:
                one(0, g0, step0, 0, 0)
            with pe.Fori(0, n // 2) as i:
                for b in (n % 2, n % 2 + 1):
                    one(b, g0 + b, step0 + 8 * b, i, 2)

        def channel_step(q, i, m, v, j, src):
            pe.wait_ge(lo_done, q + 1 + 8 * m * i)
            s = q % SPLIT_SLOTS
            for c in range(2):
                k = 2 * j + c
                both = src[:, k, :, :].rearrange("p a b -> p (a b)")
                for d in range(4):
                    acc = psum[:, 4 * v + d, :]
                    hi, lo = (w[s][:, c, P * d:P * d + P] for w in (wh, wl))
                    if k < KC - 1:
                        pe.matmul(acc, hi, both, start=k == 0, stop=False)
                        ins = pe.matmul(acc[:, 0:SEQ], lo, src[:, k, 0, :], start=False, stop=False)
                    else:
                        pe.matmul(acc[:, 0:SEQ], lo, src[:, k, 0, :], start=False, stop=False)
                        ins = pe.matmul(acc, hi, both, start=False, stop=True)
            ins.then_inc(mm_done, 1)

        def transposes(F, src):
            if F >= 4:
                pe.wait_ge(sem["tr_lo"], F - 3)
            for c in range(2):
                for t in range(NT):
                    ins = pe.transpose(psum[:, 4 + F % 4, SEQ * c + P * t:SEQ * c + P * t + P], src(c, t), ident[:])
            ins.then_inc(sem["tr_full"], 1)

        def x_group(fill0, c):
            for f in (2 * c, 2 * c + 1):
                transposes(fill0 + f, lambda k, t: x_rows[:, t, (2 * f + k) * P:(2 * f + k + 1) * P])

        def next_input(fill0, g0):
            def hook(b, j):
                if b and j == 1:
                    pe.wait_ge(row_free, FREE + g0 + b)
                    x_group(fill0, b - 1)
            return hook

        def row_of_roots(count):
            pe.wait_ge(sem["diag_ok"], count)
            for t in range(NT):
                ins = pe.matmul(psum[:, 4, P * t:P * t + P], ones[:], rstd_diag[:, t, :], start=True, stop=True)
            ins.then_inc(sem["rstd_row_mm"], 1)

        def split_by(fill0):
            return lambda j: pe.wait_ge(sem["tr_lo"], fill0 + j + 1)

        def head_stage(j, k, last):
            if j == 0 and k < last and k < N1:
                n = k
                kind, h, x, (qb, qc), (kb, kc_), _ = heads[n]
                if kind == "band":
                    pe.wait_ge(sem["a_ready"], 6)
                if kind == "near":
                    pe.wait_ge(sem["bn_ok"], h + 1)
                if n:
                    pe.wait_ge(sem["at_qksb"], n)
                for i, (b, c) in enumerate(((qb, qc), (kb, kc_))):
                    for t in range(NT):
                        ins = pe.transpose(psum[:, QK_BANK, SEQ * i + P * t:SEQ * i + P * t + P],
                                           x[:, b, t, c:c + HD], ident[:])
                ins.then_inc(sem["at_qk"], 1)
            if j == 1 and k - 1 >= first[0]:
                n = k - 1
                pe.wait_ge(sem["at_pn"], n + 1)
                if n:
                    pe.wait_ge(sem["at_ptsb"], n)
                for kt in range(NT):
                    for t in range(NT):
                        ins = pe.transpose(psum[:, PT_BANK, SEQ * kt + P * t:SEQ * kt + P * t + P],
                                           prob[n % 2][:, t, P * kt:P * kt + P], ident[:])
                ins.then_inc(sem["at_pt"], 1)
            if j == 2 and k < last:
                n = k
                kind, h = heads[n][:2]
                if n < N1:
                    pe.wait_ge(sem["at_qksb"], n + 1)
                    q_t, k_t = qk_t[n % 2][:, 0, :], qk_t[n % 2][:, 1, :]
                else:
                    pe.wait_ge(sem["kall_ok"], 1 if kind == "slc" else 2)
                    q_t, k_t = q_all[h // 4][:, h % 4, :], k_all[:, 2 * (kind == "win") + h // 4, :]
                if n:
                    pe.wait_ge(sem["at_s"], n)
                for t in range(NT):
                    ins = pe.matmul(psum[:, SC_BANK, SEQ * t:SEQ * t + SEQ], q_t[:, P * t:P * t + P], k_t,
                                    start=True, stop=True)
                ins.then_inc(sem["at_sc"], 1)
            if j == 3 and k - 1 >= first[0]:
                n = k - 1
                kind, h, x, _, _, (vb, vc) = heads[n]
                pe.wait_ge(sem["at_ptsb"], n + 1)
                if outs_before(n):
                    pe.wait_ge(sem["at_osb"], outs_before(n))
                acc = psum[:, O_BANK, 0:SEQ]
                if kind == "slc":
                    pe.matmul(acc, cmp_v[:, h // 4, :], cmp_pt[:, h, :], start=True, stop=False)
                for kt in range(NT):
                    ins = pe.matmul(acc, x[:, vb, kt, vc:vc + HD], prob_t[n % 2][:, kt, :],
                                    start=kind in ("band", "near") and kt == 0, stop=kind != "slc" and kt == 1)
                ins.then_inc(sem["at_o"], 1)

        first = [0]

        pe.wait_ge(sem["ident_in"], 16)
        pe.wait_ge(x_in[0], 16)
        x_group(T_MIX1, 0)
        pe.wait_ge(row_free, R_IN1 + 1)
        for j in range(8):
            pe.wait_ge(sem["tr_lo"], T_MIX1 + j + 1)
            rows_step(S_IN1 + j, 0, 0, ha, (2 * j, 2 * j + 1), R_IN1, j == 0, j == 7)
            if j in (0, 2, 4):
                pe.wait_ge(x_in[j // 2 + 1], 16)
                x_group(T_MIX1, j // 2 + 1)
        row_blocks(S_IN1 + 8, R_IN1 + 1, IN1_BLOCKS - 1, 8, ha)
        for s in range(8 * GATE_BLOCKS):
            b, j = s // 8, s % 8
            g = R_GATE + b
            if j == 0:
                pe.wait_ge(row_free, g + 1)
            rows_step(S_GATE + s, 0, 0, ha, (2 * j, 2 * j + 1), g, j == 0, j == 7)
            head_stage(s % 4, s // 4, N1)
        for n in range(4):
            for br in range(2):
                g = R_BRANCH + 2 * n + br
                pe.wait_ge(row_free, g + 1)
                for j in range(4):
                    if n == 0:
                        pe.wait_ge(sem["ot_lo"], 4 * br + j + 1)
                    rows_step(S_BRANCH + 8 * n + 4 * br + j, 0, 0, ha, (8 * br + 2 * j, 8 * br + 2 * j + 1), g,
                              j == 0, j == 3)
                    if n == 0 and br == 0:
                        head_stage(j, N1, N1)
                if br == 0 and n:
                    pe.wait_ge(sem["at_osb"], N1)
                    pe.wait_ge(sem["merge_rows"], n)
                    for f in range(2):
                        transposes(T_MERGE + 2 * (n - 1) + f,
                                   lambda c, t: merged[(n - 1) % 2][:, t, (2 * f + c) * P:(2 * f + c + 1) * P])
        pe.wait_ge(sem["merge_rows"], 4)
        for f in range(2):
            transposes(T_MERGE + 6 + f, lambda c, t: merged[1][:, t, (2 * f + c) * P:(2 * f + c + 1) * P])
        row_blocks(S_OUT1, R_OUT1, 4, 8, hb, split_by(T_MERGE), extra=next_input(T_FFN1, R_OUT1))

        def channel_blocks(step0, c0, n, src, rows_before):
            pe.wait_ge(row_free, FREE + rows_before)
            with pe.Fori(0, n) as i:
                for v in range(2):
                    pe.wait_ge(chan_free, FREE + c0 + v - 1 + 2 * i)
                    for j in range(8):
                        channel_step(step0 + 8 * v + j, i, 2, v, j, src)

        def first_pair(step0, c0, src, fill0, count, rows_before, extra):
            pe.wait_ge(row_free, FREE + rows_before)
            pe.wait_ge(chan_free, FREE + c0 - 1)
            for j in range(8):
                pe.wait_ge(sem["tr_lo"], fill0 + j + 1)
                channel_step(step0 + j, 0, 0, 0, j, src)
                extra(j)
            row_of_roots(count)
            pe.wait_ge(sem["rstd_row_ok"], count)
            pe.wait_ge(chan_free, FREE + c0)
            for j in range(8):
                channel_step(step0 + 8 + j, 0, 0, 1, j, src)

        def hb_by(base, per_count):
            return lambda j: pe.wait_ge(sem["hb_lo"], base + (2 * j + 1) // 4 + 1)

        rows_before = R_DOWN1[0]

        def last_group(j):
            if j == 1:
                pe.wait_ge(row_free, FREE + R_OUT1 + 4)
                x_group(T_FFN1, 3)

        for p, (j0, n) in enumerate(UP1_PASSES):
            peeled = 1 if p == 0 else 0
            if p == 0:
                first_pair(S_UP1[0], C_UP1[0], ha, T_FFN1, 1, rows_before, last_group)
            channel_blocks(S_UP1[p] + 16 * peeled, C_UP1[p] + 2 * peeled, n - peeled, ha, rows_before)
            pe.wait_ge(chan_free, FREE + C_UP1[p] + 2 * n - 1)
            enter = next_input(T_MIX2, R_DOWN1[p])

            def down_hook(b, j):
                if p == 2 and b:
                    if b == 1 and j == 1:
                        pe.wait_ge(chan_free, FREE + 22)
                    enter(b, j)

            row_blocks(S_DOWN1[p], R_DOWN1[p], 4, 2 * n, hb, hb_by(j0, 4), extra=down_hook if p == 2 else None)
            rows_before = R_DOWN1[p] + 4

        def four_transposes(bank, src, rows=P):
            for c in range(2):
                for t in range(NT):
                    ins = pe.transpose(psum[0:rows, bank, SEQ * c + P * t:SEQ * c + P * t + P], src(c, t), ident[:])
            return ins

        def in2_step(s):
            b, j = s // 8, s % 8
            g = R_IN2 + b
            if j == 0:
                pe.wait_ge(row_free, g + 1)
            if b == 0:
                pe.wait_ge(sem["tr_lo"], T_MIX2 + j + 1)
            rows_step(S_IN2 + s, 0, 0, ha, (2 * j, 2 * j + 1), g, j == 0, j == 7)

        for s in range(8 * IN2_BLOCKS):
            in2_step(s)
            if s == 1:
                pe.wait_ge(row_free, FREE + R_DOWN1[-1] + 4)
                x_group(T_MIX2, 3)
            if s == 8:
                pe.wait_ge(sem["t5_in"], 80)
                pe.matmul(psum[0:8, 7, :], t5_tab[:], t5_up[:], start=True, stop=True).then_inc(sem["t5_mm"], 1)
                for c in range(4):
                    ins = pe.matmul(psum[:, 6, 8 * c:8 * c + 8], t5_up[:, P * c:P * c + P], t5_tab[:],
                                    start=True, stop=True)
                ins.then_inc(sem["t5_mm"], 1)
            if s == 10:
                pe.wait_ge(row_free, FREE + R_IN2 + 1)
                for f in range(2):
                    four_transposes(4 + f, lambda c, t: proj2[:, 2, t, (2 * f + c) * HD:(2 * f + c + 1) * HD]
                                    ).then_inc(sem["kvt_mm"], 1)
            if s == 12:
                pe.wait_ge(sem["wg_lo"], 1)
                pe.wait_ge(sem["t5_rows_ok"], 1)
                acc = psum[0:N_GATES, 7, :]
                for k in range(KC):
                    both = ha[:, k, :, :].rearrange("p a b -> p (a b)")
                    if k == 0:
                        pe.matmul(acc, w_gate_h[:, k, :], both, start=True, stop=False)
                    pe.matmul(acc[:, 0:SEQ], w_gate_l[:, k, :], ha[:, k, 0, :], start=False, stop=False)
                    if k:
                        ins = pe.matmul(acc, w_gate_h[:, k, :], both, start=False, stop=k == KC - 1)
                ins.then_inc(sem["gate_mm"], 1)
            if s in (15, 17):
                kv = (s - 15) // 2
                pe.wait_ge(w1_in[kv], 32)
                pe.wait_ge(sem["cin_ok"], kv + 1)
                pe.wait_ge(sem["kvt_ok"], kv + 1)
                for l in range(CMP_BLOCK):
                    ins = pe.matmul(psum[0:2 * NCMP, 4 + kv, 0:HD], cmp_in[:, kv, l, :, :].rearrange("p g n -> p (g n)"),
                                    w1[:, kv, l, :], start=l == 0, stop=l == CMP_BLOCK - 1)
                ins.then_inc(sem["hid_mm"], 1)
            if s == 16:
                pe.wait_ge(sem["gate_sum"], 1)
                pe.wait_ge(sem["t5_cols_ok"], 1)
                for t in range(NT):
                    ins = pe.transpose(psum[:, 6, N_GATES * t:N_GATES * (t + 1)], gate_t[:, P * t:P * t + P],
                                       ident[0:N_GATES, 0:N_GATES])
                ins.then_inc(sem["gate_tr"], 1)
            if s == 20:
                pe.wait_ge(sem["hid_copied"], 2)
                for kv in range(2):
                    ins = pe.transpose(psum[:, 7, 2 * NCMP * kv:2 * NCMP * (kv + 1)], hid_t[:, kv, :],
                                       ident[0:2 * NCMP, 0:2 * NCMP])
                ins.then_inc(sem["hid_tr"], 1)
            if s in (21, 26):
                i = (s == 26)
                pe.wait_ge(row_free, FREE + R_IN2 + 2 + i)
                if i:
                    pe.wait_ge(sem["qall_ok"], 2)
                for f in range(2):
                    four_transposes(4 + f, lambda c, t: proj2[:, i, t, (2 * f + c) * HD:(2 * f + c + 1) * HD]
                                    ).then_inc(sem["qall_mm"], 1)
            if s == 22:
                pe.wait_ge(sem["w2_in"], 32)
                pe.wait_ge(sem["hid_ok"], 2)
                pe.wait_ge(sem["gate_ok"], 1)
                pe.matmul(psum[:, 6, 0:2 * NCMP], w2[:, 0, :], cmp_hid[:, 0, :, :].rearrange("p g n -> p (g n)"),
                          start=True, stop=True).then_inc(sem["kv_mm"], 1)
                for g in range(2):
                    ins = pe.matmul(psum[0:NCMP, 6, SEQ + HD * g:SEQ + HD * g + HD], cmp_hid[:, 1, g, :], w2[:, 1, :],
                                    start=True, stop=True)
                ins.then_inc(sem["kv_mm"], 1)
            if s == 29:
                pe.wait_ge(sem["kv_ok"], 1)
                pe.wait_ge(sem["qall_ok"], 4)
                for h in range(8):
                    for t in range(NT):
                        c = (h * NT + t) * NCMP
                        ins = pe.matmul(psum[:, 7, c:c + NCMP], q_all[h // 4][:, h % 4, P * t:P * t + P],
                                        cmp_k[:, h // 4, :], start=True, stop=True)
                ins.then_inc(sem["cs_mm"], 1)
            if s == 34:
                pe.wait_ge(row_free, FREE + R_IN2 + 4)
                four_transposes(4, lambda c, t: proj2[:, 3, t, c * HD:(c + 1) * HD]).then_inc(sem["kall_mm"], 1)
            if s == 36:
                pe.wait_ge(sem["cs_p"], 1)
                pe.wait_ge(sem["kv_ok"], 2)
                for f in range(4):
                    if f == 3:
                        pe.wait_ge(sem["kall_ok"], 1)
                    four_transposes(4 + (f + 1) % 4, lambda c, t: cmp_p[:, 2 * f + c, t, :], NCMP).then_inc(sem["cpt_mm"], 1)
        def retention_stage(r, j):
            if j == 0:
                pe.wait_ge(sem["at_s"], NH)
                for i, (mm, ok) in enumerate((("rq_mm", "rq_ok"), ("rk_mm", "rk_ok"))):
                    pe.wait_ge(sem["rope_ok"], 4 * i + 2 * (r // 2) + 2)
                    if r:
                        pe.wait_ge(sem[ok], r)
                    for c in range(2):
                        for t in range(NT):
                            col = RET_D * (r % 2) + P * c
                            ins = pe.transpose(psum[:, 4 + i, SEQ * c + P * t:SEQ * c + P * t + P],
                                               ret[:, 2 * i + r // 2, t, col:col + P], ident[:])
                    ins.then_inc(sem[mm], 1)
            if j == 1:
                pe.wait_ge(sem["rq_ok"], r + 1)
                pe.wait_ge(sem["rk_ok"], r + 1)
                if r:
                    pe.wait_ge(sem["rp_ok"], r)
                else:
                    pe.wait_ge(sem["at_ptsb"], NH)
                for kt in range(NT):
                    for c in range(2):
                        ins = pe.matmul(psum[:, 6, SEQ * kt:SEQ * kt + SEQ], ret_k[r % 2][:, c, P * kt:P * kt + P],
                                        ret_q[r % 2][:, c, :], start=c == 0, stop=c == 1)
                ins.then_inc(sem["rs_mm"], 1)
            if j == 2:
                pe.wait_ge(sem["rp_ok"], r + 1)
                pe.wait_ge(row_free, FREE + R_RET + 5 + r // 2)
                if r:
                    pe.wait_ge(sem["ro_ok"], r)
                else:
                    pe.wait_ge(sem["at_osb"], outs_before(NH))
                for t in range(NT):
                    for kt in range(NT):
                        ins = pe.matmul(psum[:, 7, RET_D * t:RET_D * t + RET_D],
                                        ret_p[r % 2][:, kt, P * t:P * t + P],
                                        ret[:, 4 + r // 2, kt, RET_D * (r % 2):RET_D * (r % 2) + RET_D],
                                        start=kt == 0, stop=kt == 1)
                ins.then_inc(sem["ro_mm"], 1)

        first[0] = N1
        for s in range(8 * RET_BLOCKS):
            b, j = s // 8, s % 8
            g = R_RET + b
            if j == 0:
                pe.wait_ge(row_free, g + 1)
            rows_step(S_RET + s, 0, 0, ha, (2 * j, 2 * j + 1), g, j == 0, j == 7)
            if s == 1:
                pe.wait_ge(row_free, FREE + R_IN2 + IN2_BLOCKS)
                pe.wait_ge(sem["cpt_ok"], 4)
                four_transposes(4, lambda c, t: proj2[:, 4, t, c * HD:(c + 1) * HD]).then_inc(sem["kall_mm"], 1)
            if s < RET_START:
                head_stage(1 + s % SLOT, N1 + s // SLOT, NH)
            r, j = divmod(s - RET_START, 3)
            if 0 <= r < RET_HEADS:
                retention_stage(r, j)

        def ret_fills(f0):
            pe.wait_ge(sem["ro_ok"], RET_HEADS if f0 else 1)
            pe.wait_ge(sem["ro_gated"], f0 + 2)
            for f in (f0, f0 + 1):
                transposes(T_RETO + f, lambda c, t: ret_o[:, t, (2 * f + c) * P:(2 * f + c + 1) * P])

        def mix_ready(j):
            if j < 4:
                pe.wait_ge(sem["ot_lo"], 8 + j + 1)
            else:
                pe.wait_ge(sem["tr_lo"], T_RETO + j - 4 + 1)

        ret_fills(0)
        row_blocks(S_OUT2, R_OUT2, 4, 8, ha, mix_ready, 
                   extra=lambda b, j: ret_fills(2) if (b, j) == (0, 3) else None)
        for c in range(2):
            pe.wait_ge(sem["post_ok"], c + 1)
            x_group(T_MLP2, c)

        def later_groups(j):
            if j in (0, 2):
                pe.wait_ge(sem["post_ok"], 3 + j // 2)
                x_group(T_MLP2, 2 + j // 2)

        first_pair(S_UP2[0], C_UP2[0], hb, T_MLP2, 2, R_OUT2 + 4, later_groups)
        rows_before = R_OUT2 + 4
        for p in range(UP2_PASSES):
            peeled = 1 if p == 0 else 0
            channel_blocks(S_UP2[p] + 16 * peeled, C_UP2[p] + 2 * peeled, 2 - peeled, hb, rows_before)
            pe.wait_ge(chan_free, FREE + C_UP2[p] + 3)
            row_blocks(S_DOWN2[p], R_DOWN2[p], 4, 8, ha, hb_by(11 + 4 * p, 4))
            rows_before = R_DOWN2[p] + 4

    block.__exit__(None, None, None)


CONST_SHAPES = shape_constants()
DRAM_INPUTS = ["x", "w_in", "a_q_norm", "a_k_norm", "a_sink", "b_rpb", "w_branch_a", "w_branch_b", "w_out", "w_up",
               "w_down", "w_in_2", "cmp_w1_k_2", "cmp_w2_k_2", "cmp_w1_v_2", "cmp_w2_v_2", "t5_bias_2", "w_out_2",
               "norm_mix_post_2", "w_up_2", "w_down_2", "norm_mlp_post_2"]


def kernel(**inputs):
    import concourse.bacc as bacc
    from concourse.bass_utils import run_bass_kernel_spmd

    nc = bacc.Bacc("TRN2", target_bir_lowering=False, num_devices=1, dynamic_dma_scratch_size=1024)
    arrays = {n: np.ascontiguousarray(inputs[n]) for n in DRAM_INPUTS}
    arrays["b_rpb"] = np.ascontiguousarray(arrays["b_rpb"][:, :, ::-1, ::-1])
    arrays.update(CONST_SHAPES)
    arrays["params"] = pack_columns(inputs)
    aps = {n: nc.dram_tensor(f"in_{n}", v.shape, mybir.dt.from_np(v.dtype), kind="ExternalInput").ap()
           for n, v in arrays.items()}
    out = nc.dram_tensor("out", (1, SEQ, D), F32, kind="ExternalOutput").ap()
    scratch = nc.dram_tensor("distance_rows", (8, 512), F32, kind="Internal").ap()
    scratch_cols = nc.dram_tensor("distance_columns", (512, 8), F32, kind="Internal").ap()
    build(nc, aps, out, scratch, scratch_cols)
    r = run_bass_kernel_spmd(nc, [{f"in_{n}": v for n, v in arrays.items()}], core_ids=[0])
    return r.results[0]["out"]
```
